# Optimizing a Trainium2 kernel written in Bass

```python
import jax, jax.numpy as jnp
from jax import lax
import numpy as np

D_MODEL = 1024
BATCH = 1
SEQ = 512
DEPTH = 1

EPS = 1e-6
N_SUB = 3
D_FF = 2816
CHUNK = 64
HG_HEADS = 4
HG_DK = 128
HG_DV = 128
HG_QK = HG_HEADS * HG_DK
HG_WIDTH = HG_HEADS * HG_DV
GLA_HEADS = 4
GLA_DK = 64
GLA_DV = 128
GLA_K = GLA_HEADS * GLA_DK
GLA_V = GLA_HEADS * GLA_DV
GLA_RANK = 16
GLA_NORMALIZER = 16.0
IN_SPLITS = (HG_QK, HG_QK, HG_WIDTH, HG_WIDTH,
             GLA_K, GLA_K, GLA_V, GLA_V, GLA_RANK,
             D_MODEL, D_MODEL)
IN_WIDTH = sum(IN_SPLITS)
IN_OFFSETS = tuple(int(o) for o in np.cumsum(IN_SPLITS)[:-1])

kernel_name = 'hybrid_hgrn2_gla_macaron_adaln'

def rms_norm(x, gain):
    xf = x.astype(jnp.float32)
    y = xf * lax.rsqrt(jnp.mean(xf * xf, axis=-1, keepdims=True) + EPS)
    return (y * gain.astype(jnp.float32)).astype(x.dtype)

def modulate(h, shift, scale):
    return h * (1 + scale[:, None, :]) + shift[:, None, :]

def swiglu(h, w_in, w_down):
    gate, up = jnp.split(h @ w_in, 2, axis=-1)
    return (jax.nn.silu(gate) * up) @ w_down

def to_heads(t, n_heads):
    b, s, w = t.shape
    return t.reshape(b, s, n_heads, w // n_heads).transpose(0, 2, 1, 3)

def from_heads(t):
    b, h, s, d = t.shape
    return t.transpose(0, 2, 1, 3).reshape(b, s, h * d)

def chunked_gated_linear_attention(q, k, v, log_a):
    b_, h_, t_, dk = q.shape
    dv = v.shape[-1]
    n = t_ // CHUNK

    def to_chunks(t):
        return jnp.moveaxis(t.astype(jnp.float32).reshape(b_, h_, n, CHUNK, t.shape[-1]), 2, 0)

    qc, kc, vc, gc = to_chunks(q), to_chunks(k), to_chunks(v), to_chunks(log_a)
    causal = jnp.tril(jnp.ones((CHUNK, CHUNK), dtype=bool))[:, :, None]

    def step(state, inp):
        qi, ki, vi, gi = inp
        b = jnp.cumsum(gi, axis=-2)
        o_inter = jnp.einsum('bhtk,bhkv->bhtv', qi * jnp.exp(b), state)
        diff = b[:, :, :, None, :] - b[:, :, None, :, :]
        decay = jnp.exp(jnp.where(causal, diff, -jnp.inf))
        scores = jnp.einsum('bhtk,bhsk,bhtsk->bhts', qi, ki, decay)
        o = o_inter + jnp.einsum('bhts,bhsv->bhtv', scores, vi)
        b_last = b[:, :, -1:, :]
        k_dec = ki * jnp.exp(b_last - b)
        state = (jnp.exp(b_last[:, :, 0, :])[..., None] * state
                 + jnp.einsum('bhsk,bhsv->bhkv', k_dec, vi))
        return state, o

    s0 = jnp.zeros((b_, h_, dk, dv), jnp.float32)
    _, o = lax.scan(step, s0, (qc, kc, vc, gc))
    return jnp.moveaxis(o, 0, 2).reshape(b_, h_, t_, dv)

def hgrn2_branch(q, f, i, g, lower_bound, norm_gain):
    dtype = i.dtype
    qf = jax.nn.silu(q.astype(jnp.float32))
    forget = lower_bound + (1 - lower_bound) * jax.nn.sigmoid(f.astype(jnp.float32))
    o = chunked_gated_linear_attention(to_heads(qf, HG_HEADS), to_heads(1 - forget, HG_HEADS),
                                       to_heads(i, HG_HEADS), to_heads(jnp.log(forget), HG_HEADS))
    o = rms_norm(o, norm_gain) * jax.nn.silu(to_heads(g, HG_HEADS).astype(jnp.float32))
    return from_heads(o).astype(dtype)

def gla_branch(q, k, v, g, gk_low, w_gk_up, b_gk_up, norm_gain):
    dtype = v.dtype
    gk = gk_low @ w_gk_up + b_gk_up
    log_a = jax.nn.log_sigmoid(gk.astype(jnp.float32)) / GLA_NORMALIZER
    qs = q.astype(jnp.float32) * (GLA_DK ** -0.5)
    o = chunked_gated_linear_attention(to_heads(qs, GLA_HEADS), to_heads(k, GLA_HEADS),
                                       to_heads(v, GLA_HEADS), to_heads(log_a, GLA_HEADS))
    o = rms_norm(o, norm_gain) * jax.nn.silu(to_heads(g, GLA_HEADS).astype(jnp.float32))
    return from_heads(o).astype(dtype)

def setup_inputs(seed: int = 0) -> dict:
    key = jax.random.key(seed)
    ks = jax.random.split(key, 20)
    D = D_MODEL

    def w(k, shape, fan_in, s=1.0):
        return jax.random.normal(k, shape, jnp.float32) * (s * fan_in ** -0.5)

    return {
        'x': jax.random.normal(ks[0], (BATCH, SEQ, D), jnp.float32),
        'c': jax.random.normal(ks[1], (BATCH, D), jnp.float32),
        'w_ada': w(ks[2], (DEPTH, D, N_SUB * 3 * D), D, 0.5),
        'b_ada': 0.02 * jax.random.normal(ks[3], (DEPTH, N_SUB * 3 * D), jnp.float32),
        'norm_gains': 1.0 + 0.02 * jax.random.normal(ks[4], (DEPTH, N_SUB, D), jnp.float32),
        'ffn1_w_in': w(ks[5], (DEPTH, D, 2 * D_FF), D),
        'ffn1_w_down': w(ks[6], (DEPTH, D_FF, D), D_FF),
        'w_in_mix': w(ks[7], (DEPTH, D, IN_WIDTH), D),
        'w_gk_up': w(ks[8], (DEPTH, GLA_RANK, GLA_K), GLA_RANK),
        'b_gk_up': 0.1 * jax.random.normal(ks[9], (DEPTH, GLA_K), jnp.float32),
        'lb_logits': 0.5 * jax.random.normal(ks[10], (DEPTH + 1, HG_QK), jnp.float32),
        'hg_norm': 1.0 + 0.02 * jax.random.normal(ks[11], (DEPTH, HG_DV), jnp.float32),
        'gla_norm': 1.0 + 0.02 * jax.random.normal(ks[12], (DEPTH, GLA_DV), jnp.float32),
        'w_up_hg': w(ks[13], (DEPTH, HG_WIDTH, D), HG_WIDTH),
        'w_up_gla': w(ks[14], (DEPTH, GLA_V, D), GLA_V),
        'w_out': w(ks[15], (DEPTH, D, D), D),
        'ffn2_w_in': w(ks[16], (DEPTH, D, 2 * D_FF), D),
        'ffn2_w_down': w(ks[17], (DEPTH, D_FF, D), D_FF),
        'final_norm': 1.0 + 0.02 * jax.random.normal(ks[18], (D,), jnp.float32),
    }

def reference(x, c, w_ada, b_ada, norm_gains, ffn1_w_in, ffn1_w_down, w_in_mix,
              w_gk_up, b_gk_up, lb_logits, hg_norm, gla_norm, w_up_hg, w_up_gla,
              w_out, ffn2_w_in, ffn2_w_down, final_norm):
    b_, _, d = x.shape
    lower_bounds = jnp.cumsum(jax.nn.softmax(lb_logits.astype(jnp.float32), axis=0), axis=0)
    cond = jax.nn.silu(c)
    for l in range(DEPTH):
        mod = (cond @ w_ada[l] + b_ada[l]).reshape(b_, N_SUB, 3, d)

        h = modulate(rms_norm(x, norm_gains[l, 0]), mod[:, 0, 0], mod[:, 0, 1])
        x = x + 0.5 * mod[:, 0, 2][:, None, :] * swiglu(h, ffn1_w_in[l], ffn1_w_down[l])

        h = modulate(rms_norm(x, norm_gains[l, 1]), mod[:, 1, 0], mod[:, 1, 1])
        proj = h @ w_in_mix[l]
        (hq, hf, hi, hg, gq, gk, gv, gg, g_low, r_hg, r_gla) = jnp.split(proj, IN_OFFSETS, axis=-1)
        y_hg = hgrn2_branch(hq, hf, hi, hg, lower_bounds[l], hg_norm[l])
        y_gla = gla_branch(gq, gk, gv, gg, g_low, w_gk_up[l], b_gk_up[l], gla_norm[l])
        merged = (jax.nn.sigmoid(r_hg) * (y_hg @ w_up_hg[l])
                  + jax.nn.sigmoid(r_gla) * (y_gla @ w_up_gla[l]))
        x = x + mod[:, 1, 2][:, None, :] * (merged @ w_out[l])

        h = modulate(rms_norm(x, norm_gains[l, 2]), mod[:, 2, 0], mod[:, 2, 1])
        x = x + 0.5 * mod[:, 2, 2][:, None, :] * swiglu(h, ffn2_w_in[l], ffn2_w_down[l])
    return rms_norm(x, final_norm)


_drawn_inputs = setup_inputs


def setup_inputs(seed=0):
    import zlib

    import numpy as np

    out = dict(_drawn_inputs(seed))
    spreads = {}
    factors = {'b_ada': 3.137,
     'norm_gains': 8.0,
     'b_gk_up': 8.0,
     'lb_logits': 8.0,
     'hg_norm': 8.0,
     'gla_norm': 8.0,
     'final_norm': 2.906}
    for name, (base, spread) in spreads.items():
        noise = np.random.default_rng([zlib.crc32(name.encode()), seed]).standard_normal(out[name].shape)
        drawn = base * np.exp(spread * noise) if base else spread * noise
        out[name] = __import__('jax').numpy.asarray(drawn.astype(out[name].dtype))
    for name, factor in factors.items():
        out[name] = (out[name] * factor).astype(out[name].dtype)
    return out
```

```python
import concourse.bass as bass
from concourse import mybir


def trunk_program(nc, x, c, w_ada, b_ada, norm_gains, ffn1_w_in, ffn1_w_down, w_in_mix, w_gk_up, b_gk_up,
                  lb_logits, hg_norm, gla_norm, w_up_hg, w_up_gla, w_out, ffn2_w_in, ffn2_w_down,
                  final_norm, out):
    F32, F32R, BF16, I8 = mybir.dt.float32, mybir.dt.float32r, mybir.dt.bfloat16, mybir.dt.int8
    ACT, ALU = mybir.ActivationFunctionType, mybir.AluOpType
    ds = bass.ds

    P = 128
    T = x.shape[1]
    D = x.shape[2]
    DB = D // P
    TT = T // P
    FF = ffn1_w_down.shape[1]
    FB = FF // P
    CW = 256
    NP = FF // CW
    CHUNK = 64
    NC = T // CHUNK
    HEADS = 4
    EPS = 1e-6
    UNIT = DB * CW
    LN_FLOOR = 2.0 ** -63

    xv = x[0]
    ada = w_ada[0]
    widths = (512, 512, 512, 512, 256, 256, 512, 512, 16, D, D)
    at = [sum(widths[:i]) for i in range(len(widths))]
    HQ, HF, HI, HG, GQ, GK, GV, GG, GLOW, RHG, RGLA = at

    N_F1IN = 0
    N_F1DOWN = N_F1IN + 2 * NP
    N_MIX = N_F1DOWN + 12
    MIX = [("hf", HF, 0), ("hq", HQ, 0), ("vh", HI, 0), ("gh", HG, 0), ("hf", HF, 1), ("hq", HQ, 1),
           ("vh", HI, 1), ("gh", HG, 1), ("low", GLOW, 0), ("gk", GK, 0), ("gq", GQ, 0), ("vg", GV, 0),
           ("gg", GG, 0), ("vg", GV, 1), ("gg", GG, 1)]
    N_END = N_MIX + len(MIX)
    N_OUT = N_END + 12
    N_F2IN = N_OUT + 4
    N_F2DOWN = N_F2IN + 2 * NP
    N_UNITS = N_F2DOWN + 12
    mix_at = {}
    for j, (kind, _, half) in enumerate(MIX):
        mix_at[kind, half] = j
    RANK = 16

    from contextlib import ExitStack
    ctx = ExitStack()
    with ctx:
        def sb(name, shape, dt=F32):
            return ctx.enter_context(nc.sbuf_tensor(name, shape, dt))

        def sem(name):
            return ctx.enter_context(nc.semaphore(name))

        X = sb("X", [P, DB, T])
        RAW = [sb(f"RAW{s}", [P, UNIT]) for s in range(2)]
        WH = [sb(f"WH{s}", [P, UNIT], F32R) for s in range(2)]
        WL = [sb(f"WL{s}", [P, UNIT], F32R) for s in range(2)]
        S = sb("S", [P, T])
        PT = sb("PT", [P, 124])
        PST = sb("PST", [124, P])
        MOD = sb("MOD", [P, 9 * DB])
        AV = sb("AV", [P, 4, DB])
        GATE = sb("GATE", [P, 3, DB])
        COND = sb("COND", [P, DB])
        IDENT = sb("IDENT", [P, P])
        ONES = sb("ONES", [P, P])
        MASKF = sb("MASKF", [P, 64])
        MASK = sb("MASK", [P, 6, 64], I8)
        MASKD = sb("MASKD", [P, P], I8)
        RST = sb("RST", [P, T], BF16)
        V4 = sb("V4", [P, TT])
        R4 = sb("R4", [P, TT])
        HALF4 = sb("HALF4", [P, TT])
        EPST = sb("EPST", [P, 1])
        LB = sb("LB", [P, HEADS])
        OML = sb("OML", [P, HEADS])
        LBD = sb("LBD", [P, HEADS])
        GT = sb("GT", [P, 2, NC])
        FT = sb("FT", [P, 2, NC])
        GKW = sb("GKW", [RANK, 256])

        H_BYTES = DB * T * 4
        ARENA = 106496
        arena = sb("arena", [P, (ARENA + 2 * H_BYTES) // 4])
        base = arena_offset(nc, arena)

        def place(name, shape, offset, dt=F32):
            return nc.alloc_sbuf_tensor_at(name, shape, dt, offset=base + offset)

        HO = ARENA
        HH = place("HH", [P, DB, T], HO, F32R)
        HL = place("HL", [P, DB, T], HO + H_BYTES, F32R)
        OUTT = place("OUTT", [P, TT, D], HO)
        UH = place("UH", [P, FB, T], 0, F32R)
        UL = place("UL", [P, FB, T], FB * T * 4, F32R)
        NT = 2 * FB * T * 4 - 8192
        TN = place("TN", [P, 2, T], NT)
        HFULL = place("HFULL", [P, 2, T], NT + 4096)
        SG = place("SG", [P, 2, T], 2 * FB * T * 4)
        DG = place("DG", [P, T], 2 * FB * T * 4)
        ADAW = [place(f"ADAW{s}", [P, 512], 94208 + 2048 * s) for s in range(4)]
        ADAD = [place(f"ADAD{s}", [P, 768], 94208 + 3072 * s) for s in range(2)]
        YF = [place(f"YF{s}", [P, T], 94208 + 2048 * s) for s in range(2)]
        ACC = place("ACC", [P, 768], 102400)
        ADA0 = place("ADA0", [P, DB, 2 * D], 0)
        XST = place("XST", [P, TT, D], 65536)
        ACC0 = place("ACC0", [P, 2 * D], NT)
        QHG = place("QHG", [P, HEADS, T], 0)
        KHG = place("KHG", [P, HEADS, T], 8192)
        CHG = place("CHG", [P, HEADS, T], 16384)
        VHG = place("VHG", [P, TT, 512], 24576)
        QGL = place("QGL", [P, 2, T], 32768)
        KGL = place("KGL", [P, 2, T], 36864)
        CGL = place("CGL", [P, 2, T], 40960)
        VGL = place("VGL", [P, TT, 512], 45056)
        GO = place("GO", [P, 2 * HEADS, T], 53248)
        KP = place("KP", [P, 6, T], 69632)
        SC = place("SC", [P, TT * 640], 81920)
        QP = place("QP", [P, 6, T // 2], 92160)
        QU = place("QU", [P, T], 98304)
        KL = place("KL", [P, T], 100352)
        W256 = place("W256", [P, T], 102400)
        W512 = place("W512", [P, T], 104448)
        YH = [place("YHh", [P, HEADS, T], 8192, F32R), place("YHg", [P, HEADS, T], 0, F32R)]
        YL = [place("YLh", [P, HEADS, T], 16384, F32R), place("YLg", [P, HEADS, T], 24576, F32R)]
        MH = place("MH", [P, DB, T], 53248, F32R)
        ML = place("ML", [P, DB, T], 69632, F32R)
        RG = [place(f"RG{s}", [P, 2, T], 86016 + 4096 * s) for s in range(2)]

        PS = ctx.enter_context(nc.psum_tensor("PS", [P, 8, 512], F32))

        PC_C, PC_BADA, PC_GAIN, PC_FINAL, PC_HGN, PC_GLN, PC_BGK, PC_LB = 0, 8, 80, 104, 112, 113, 114, 116

        raw_in = [sem("raw_in0"), sem("raw_in1")]
        unit_hi = sem("unit_hi")
        unit_lo = sem("unit_lo")
        unit_done = sem("unit_done")
        small_in, x_in, ada0_in, gkw_in = sem("small_in"), sem("x_in"), [sem(f"ada0_in{k}") for k in range(DB)], sem("gkw_in")
        ada_in = [sem(f"ada_in{s}") for s in range(4)]
        consts, constd = sem("consts"), sem("constd")
        small_t, small_ready, cond_ready, lb_ready = sem("small_t"), sem("small_ready"), sem("cond_ready"), sem("lb_ready")
        ada_acc, ada_red, mod_ready = sem("ada_acc"), sem("ada_red"), sem("mod_ready")
        xt_done, xready = sem("xt_done"), sem("xready")
        sq_ready, sacc = sem("sq_ready"), sem("sacc")
        ssq_done, v_ready, r_ready, dg_ready, bc_done = sem("ssq_done"), sem("v_ready"), sem("r_ready"), sem("dg_ready"), sem("bc_done")
        av_ready, t_ready, h_hi, h_lo = sem("av_ready"), sem("t_ready"), sem("h_hi"), sem("h_lo")
        silu_done, umul_done, u_hi, u_lo = sem("silu_done"), sem("umul_done"), sem("u_hi"), sem("u_lo")
        mix_evac = sem("mix_evac")
        sc_clear = sem("sc_clear")
        logf, cum, diffs, gtab, exps, prep = sem("logf"), sem("cum"), sem("diffs"), sem("gtab"), sem("exps"), sem("prep")
        kl_diff, near_done = sem("kl_diff"), sem("near_done")
        score_done, evac_v, evac_a, pv_done = sem("score_done"), sem("evac_v"), sem("evac_a"), sem("pv_done")
        sq_o, og_done, n_done, rs_ln, rs_ready = sem("sq_o"), sem("og_done"), sem("n_done"), sem("rs_ln"), sem("rs_ready")
        yf_ready, y_hi, y_lo = sem("yf_ready"), sem("y_hi"), sem("y_lo")
        gk_mm, gk_abs, gk_ln, gk_sub = sem("gk_mm"), sem("gk_abs"), sem("gk_ln"), sem("gk_sub")
        sig_done, merge, m_hi, m_lo = sem("sig_done"), sem("merge"), sem("m_hi"), sem("m_lo")
        fin_y, fin_t, fin_ev, fin_v, fin_a, out_dma = sem("fin_y"), sem("fin_t"), sem("fin_ev"), sem("fin_v"), sem("fin_a"), sem("out_dma")
        dve_self, act_self = sem("dve_self"), sem("act_self")

        LEVELS = [64, 32, 16, 8, 4, 2]

        def slot(n):
            return n % 2

        def raw_count(n):
            return 16 * (n // 2 + 1)

        def blocks(ap, size):
            return ap.rearrange("p (n b) -> p n b", b=size)

        PREPS = [dict(q=QHG[:, h, :], k=KHG[:, h, :], c=CHG[:, h, :]) for h in range(HEADS)] + \
                [dict(q=QGL[:, g, :], k=KGL[:, g, :], c=CGL[:, g, :]) for g in range(2)]
        PREP_NEEDS = [2, 2, 6, 6, 11, 11]
        V_NEEDS = [3, 3, 7, 7, 12, 12, 14, 14]
        G_NEEDS = [4, 4, 8, 8, 13, 13, 15, 15]

        def prep_of(a):
            return a if a < HEADS else HEADS + (a - HEADS) // 2

        def rows_of(a):
            return slice(0, P) if a < HEADS else slice(64 * (a % 2), 64 * (a % 2) + 64)

        def before_prep(p):
            return {1: 0, 2: 1, 3: 2, 4: 3, 5: 5}[p]

        def norm_in(a):
            if a < HEADS:
                return CHG[:, a, :], KHG[:, a, :]
            return QHG[:, a - HEADS, :], VHG[:, a - HEADS, :]

        ORDER = ["E0", "E1", "P0", "E2", "E3", "V0", "A0", "Q0", "P1", "E4", "T0", "V1", "A1", "Q1", "E5", "P2",
                 "T1", "E6", "E7", "V2", "A2", "Q2", "P3", "T2", "E8", "E9", "V3", "A3", "Q3", "G0", "G1", "E10",
                 "P4", "T3", "E11", "E12", "V4", "A4", "Q4", "V5", "T4", "A5", "Q5", "P5", "E13", "T5", "E14",
                 "V6", "A6", "Q6", "V7", "T6", "A7", "Q7", "T7"]

        block = ctx.enter_context(nc.Block())

        @block.sync
        def _(sp):
            def load(n, nslot, dst_cols, src, wait=None):
                if wait is not None:
                    sp.wait_ge(unit_lo, wait)
                sp.dma_start(dst_cols, src).then_inc(raw_in[nslot], 16)

            def cols(w, col, kb0=0, nk=DB, width=CW):
                return w.rearrange("(k p) n -> p k n", p=P)[:, kb0:kb0 + nk, col] if not isinstance(col, int) \
                    else w.rearrange("(k p) n -> p k n", p=P)[:, kb0:kb0 + nk, col:col + width]

            def raw(n, nk=DB, width=CW):
                return RAW[slot(n)][:, 0:nk * width].rearrange("p (k c) -> p k c", c=width)

            for t in range(TT):
                sp.dma_start(XST[:, t, :], xv[t * P:(t + 1) * P, :]).then_inc(x_in, 16)
            for k in range(DB):
                sp.dma_start(ADA0[:, k, :], ada[k * P:(k + 1) * P, 0:2 * D]).then_inc(ada0_in[k], 16)
            w1 = ffn1_w_in[0]
            load(0, 0, raw(0), cols(w1, 0))
            load(1, 1, raw(1), cols(w1, FF))

            def load_down(base_n, i, w, last=False):
                for q in range(2):
                    for piece, (kb0, nk) in enumerate(((0, 8), (8, 8), (16, FB - 16))):
                        n = base_n + 3 * q + piece
                        load(n, slot(n), raw(n, nk), cols(w, ds(2 * CW * i + q * CW, CW), kb0, nk), 6 * i + n - 1)

            with sp.Fori(0, NP - 1) as i:
                load(2, 0, raw(2), cols(w1, ds(CW * i + CW, CW)), 2 * i + 1)
                load(3, 1, raw(3), cols(w1, ds(CW * i + CW + FF, CW)), 2 * i + 2)
                for k in range(DB):
                    sp.wait_ge(ada_acc, DB + DB * i + k - 3)
                    sp.dma_start(ADAW[k % 4][:, :], ada[k * P:(k + 1) * P, ds(2 * D + 512 * i, 512)]).then_inc(ada_in[k % 4], 16)

            for j in range(12):
                n = N_F1DOWN + j
                kb0, nk = ((0, 8), (8, 8), (16, FB - 16))[j % 3]
                load(n, slot(n), raw(n, nk), cols(ffn1_w_down[0], j // 3 * CW, kb0, nk), n - 1)
                if j == 1:
                    for k in range(DB):
                        sp.wait_ge(ada_acc, DB + DB * (NP - 1) + k - 3)
                        sp.dma_start(ADAW[k % 4][:, :], ada[k * P:(k + 1) * P, 2 * D + 512 * (NP - 1):2 * D + 512 * NP])\
                            .then_inc(ada_in[k % 4], 16)
                if j % 6 == 5:
                    i = j // 6
                    a0 = 2 * D + 512 * NP + 768 * i
                    for k in range(DB):
                        sp.wait_ge(ada_acc, DB * (NP + 1) + DB * i + k - 1)
                        sp.dma_start(ADAD[k % 2][:, :], ada[k * P:(k + 1) * P, a0:a0 + 768]).then_inc(ada_in[k % 2], 16)

            wm = w_in_mix[0]
            for j, (kind, col, half) in enumerate(MIX):
                n = N_MIX + j
                width = RANK if kind == "low" else CW
                load(n, slot(n), raw(n, DB, width), cols(wm, col + half * CW, width=width), n - 1)

            with sp.Fori(0, 2) as i:
                for q in range(2):
                    n = N_END + 3 * q
                    load(n, slot(n), raw(n), cols(wm, ds(RHG + 2 * CW * i + CW * q, CW)), 6 * i + n - 1)
                    load(n + 1, slot(n + 1), raw(n + 1), cols(wm, ds(RGLA + 2 * CW * i + CW * q, CW)), 6 * i + n)
                    up = raw(n + 2)
                    sp.wait_ge(unit_lo, 6 * i + n + 1)
                    sp.dma_start(up[:, 0:4, :], cols(w_up_hg[0], ds((i + i) * CW + CW * q, CW), 0, 4)).then_inc(raw_in[slot(n)], 16)
                    sp.dma_start(up[:, 4:8, :], cols(w_up_gla[0], ds(2 * CW * i + CW * q, CW), 0, 4)).then_inc(raw_in[slot(n)], 16)
            with sp.Fori(0, 2) as i:
                for q in range(2):
                    n = N_OUT + q
                    load(n, slot(n), raw(n), cols(w_out[0], ds(2 * CW * i + CW * q, CW)), 2 * i + n - 1)
            w2 = ffn2_w_in[0]
            with sp.Fori(0, NP) as i:
                load(N_F2IN, slot(N_F2IN), raw(N_F2IN), cols(w2, ds(CW * i, CW)), 2 * i + N_F2IN - 1)
                load(N_F2IN + 1, slot(N_F2IN + 1), raw(N_F2IN + 1), cols(w2, ds(CW * i + FF, CW)), 2 * i + N_F2IN)
            with sp.Fori(0, 2) as i:
                load_down(N_F2DOWN, i, ffn2_w_down[0])
            for t in range(TT):
                sp.wait_ge(fin_v if t < 2 else fin_a, t % 2 + 1)
                sp.dma_start(out[0, t * P:(t + 1) * P, :], OUTT[:, t, :]).then_inc(out_dma, 16)
            sp.wait_ge(out_dma, 16 * TT)

        def raw_value(n, i_term=0):
            extra = 0
            for q in range(4):
                u = N_END + 3 * q + 2
                if u <= n and slot(u) == slot(n):
                    extra += 1
            return 16 * (n // 2 + 1 + extra) + i_term

        @block.gpsimd
        def _(pool):
            for counted in (silu_done, umul_done, u_lo, sig_done, merge, m_lo):
                pool.sem_inc(counted, 1)
            cn = [0]

            def done(ins):
                cn[0] += 1
                ins.then_inc(consts, 1)

            done(nc.gpsimd.memset(ONES[:, :], 1.0))
            done(nc.gpsimd.memset(IDENT[:, :], 0.0))
            done(nc.gpsimd.memset(HALF4[:, :], -0.5))
            done(nc.gpsimd.memset(EPST[:, :], EPS))
            done(nc.gpsimd.memset(GT[:, :, :], 0.0))
            done(nc.gpsimd.memset(RST[:, :], 1.0))
            pool.wait_ge(consts, cn[0])
            done(nc.gpsimd.affine_select(out=IDENT[:, :], in_=IDENT[:, :], compare_op=ALU.not_equal, fill=1.0,
                                         base=0, pattern=[[-1, P]], channel_multiplier=1))
            pool.wait_ge(consts, cn[0])
            done(nc.gpsimd.tensor_copy(MASKD[:, :], IDENT[:, :]))
            done(nc.gpsimd.memset(blocks(RST[:, :], CHUNK)[:, :, 0], 0.0))
            for l, B in enumerate(LEVELS):
                h, nb = B // 2, P // B
                done(nc.gpsimd.memset(MASKF[:, :], 1.0))
                pool.wait_ge(consts, cn[0])
                m = MASKF[:, :].rearrange("p (n h) -> p n h", h=h)
                done(nc.gpsimd.affine_select(out=m, in_=m, compare_op=ALU.is_ge, fill=0.0, base=0,
                                             pattern=[[-B, nb], [0, h]], channel_multiplier=1))
                pool.wait_ge(consts, cn[0])
                done(nc.gpsimd.affine_select(out=m, in_=m, compare_op=ALU.is_ge, fill=0.0, base=h - 1,
                                             pattern=[[B, nb], [0, h]], channel_multiplier=-1))
                pool.wait_ge(consts, cn[0])
                done(nc.gpsimd.tensor_copy(MASK[:, l, :], MASKF[:, :]))
                pool.wait_ge(consts, cn[0])

            def rsqrt(g):
                pool.wait_ge(v_ready, g + 1)
                nc.gpsimd.tensor_tensor(R4[:, :], V4[:, :], HALF4[:, :], ALU.pow).then_inc(r_ready, 1)

            rsqrt(0)
            rsqrt(1)
            pool.wait_ge(h_lo, 2 * DB)
            nc.gpsimd.memset(SC[:, :], 0.0).then_inc(sc_clear, 1)
            nc.gpsimd.memset(KP[:, :, :], 0.0).then_inc(sc_clear, 1)
            pool.wait_ge(sc_clear, 2)
            for p in range(6):
                cc = PREPS[p]["c"]
                pool.wait_ge(cum, p + 1)
                if p:
                    pool.wait_ge(score_done, 6 * before_prep(p) + 3)
                for l, B in enumerate(LEVELS):
                    h = B // 2
                    cb = blocks(cc, B)
                    mid = cb[:, :, h - 1:h].to_broadcast([P, T // B, h])
                    nc.gpsimd.tensor_tensor(QP[:, l, :].rearrange("p (n h) -> p n h", h=h), cb[:, :, h:B], mid,
                                            ALU.subtract).then_inc(diffs, 1)
                for l, B in enumerate(LEVELS):
                    h = B // 2
                    cb = blocks(cc, B)
                    mid = cb[:, :, h - 1:h].to_broadcast([P, T // B, h])
                    nc.gpsimd.tensor_tensor(blocks(KP[:, l, :], B)[:, :, 0:h], mid, cb[:, :, 0:h],
                                            ALU.subtract).then_inc(diffs, 1)
            rsqrt(2)
            rsqrt(3)

        @block.tensor
        def _(pe):
            mm = nc.tensor.matmul

            def weights(n, width=CW):
                hi = WH[slot(n)][:, :].rearrange("p (k c) -> p k c", c=width)
                lo = WL[slot(n)][:, :].rearrange("p (k c) -> p k c", c=width)
                return hi, lo

            def three(ps, whi, wlo, ahi, alo, start, stop):
                mm(ps, whi, ahi, start=start, stop=False)
                mm(ps, whi, alo, start=False, stop=False)
                return mm(ps, wlo, ahi, start=False, stop=stop)

            def unit(n, value, banks, ahi, alo, kb0=0, nk=DB, first=True, last=True, wait_h=None, mid=None,
                     width=CW):
                pe.wait_ge(unit_lo, value)
                whi, wlo = weights(n, width)
                for k in range(nk):
                    if wait_h is not None:
                        pe.wait_ge(h_lo, wait_h + k + 1)
                    if mid is not None and k == 3:
                        mid()
                    for m in range(max(width // P, 1)):
                        w = slice(m * P, min((m + 1) * P, width))
                        rows = w.stop - w.start
                        ins = three(PS[0:rows, banks[m], :], whi[:, k, w], wlo[:, k, w], ahi[:, kb0 + k, :],
                                    alo[:, kb0 + k, :], first and k == 0, last and k == nk - 1)
                ins.then_inc(unit_done, 1)

            def unit_v(n, banks, mid=None):
                pe.wait_ge(unit_lo, n + 1)
                whi, wlo = weights(n)
                for t in range(TT):
                    if mid is not None and t == 2:
                        mid()
                    ps = PS[:, banks[t // 2], (t % 2) * CW:(t % 2 + 1) * CW]
                    tok = slice(t * P, (t + 1) * P)
                    for k in range(DB):
                        mm(ps, HH[:, k, tok], whi[:, k, :], start=k == 0, stop=False)
                        mm(ps, HL[:, k, tok], whi[:, k, :], start=False, stop=False)
                        ins = mm(ps, HH[:, k, tok], wlo[:, k, :], start=False, stop=k == DB - 1)
                ins.then_inc(unit_done, 1)

            def mean_square(g):
                pe.wait_ge(sacc, 9 * g + 9)
                for t in range(TT):
                    ins = mm(PS[:, 6, 16 + t:17 + t], S[:, t * P:(t + 1) * P], ONES[:, 0:1], start=True, stop=True)
                ins.then_inc(ssq_done, 1)

            def broadcast_rstd(g):
                pe.wait_ge(dg_ready, TT * (g + 1))
                mm(PS[:, 7, :], ONES[:, :], DG[:, :], start=True, stop=True).then_inc(bc_done, 1)

            pe.wait_ge(consts, 7)
            pe.wait_ge(small_in, 16 * 8)
            nc.tensor.transpose(PS[:, 5, 0:124], PST[:, :], IDENT[0:124, 0:124]).then_inc(small_t, 1)
            pe.wait_ge(x_in, 16 * TT)
            for b in range(DB):
                if b >= 4:
                    pe.wait_ge(xready, b - 3)
                for t in range(TT):
                    ins = nc.tensor.transpose(PS[:, b % 4, t * P:(t + 1) * P], XST[:, t, b * P:(b + 1) * P], IDENT[:, :])
                ins.then_inc(xt_done, 1)
            mean_square(0)
            broadcast_rstd(0)
            pe.wait_ge(ada_acc, DB)
            for m in range(2 * DB):
                ins = mm(PS[:, 6, m:m + 1], ACC0[:, m * P:(m + 1) * P], ONES[:, 0:1], start=True, stop=True)
            ins.then_inc(ada_red, 1)

            def swiglu_in(base_n, which, count, with_ada):
                with pe.Fori(0, count) as i:
                    for half in range(2):
                        n = base_n + half
                        if half == 0:
                            pe.wait_ge(silu_done, 1 + NP * which + i)
                        else:
                            pe.wait_ge(umul_done, 1 + NP * which + i)
                        unit(n, 2 * i + n + 1, (2 * half, 2 * half + 1), HH, HL, wait_h=2 * DB * which if half == 0 else None)
                    if with_ada:
                        pe.wait_ge(ada_acc, 2 * DB + DB * i)
                        pe.wait_ge(mod_ready, i + 1)
                        for m in range(4):
                            ins = mm(PS[:, 6, m:m + 1], ACC[:, m * P:(m + 1) * P], ONES[:, 0:1], start=True, stop=True)
                        ins.then_inc(ada_red, 1)

            def down_pair(n0, q, value0, x_value, prologue=None):
                banks = (2 * q, 2 * q + 1)
                pe.wait_ge(xready, x_value)
                for piece, (kb0, nk) in enumerate(((0, 8), (8, 8), (16, FB - 16))):
                    unit(n0 + piece, value0 + piece, banks, UH, UL, kb0, nk, first=piece == 0, last=piece == 2)
                    if piece == 0 and prologue is not None:
                        prologue()

            swiglu_in(N_F1IN, 0, NP, True)
            pe.wait_ge(u_lo, 1 + NP)
            pe.wait_ge(u_hi, NP)
            with pe.Fori(0, 2) as i:
                for q in range(2):
                    n = N_F1DOWN + 3 * q
                    down_pair(n, q, 6 * i + n + 1, 8 + 4 * i + 2 * q - 2)
                pe.wait_ge(ada_acc, DB * (NP + 2) + DB * i)
                pe.wait_ge(mod_ready, NP + 1 + i)
                for m in range(6):
                    ins = mm(PS[:, 6, m:m + 1], ACC[:, m * P:(m + 1) * P], ONES[:, 0:1], start=True, stop=True)
                ins.then_inc(ada_red, 1)
            pe.wait_ge(mod_ready, NP + 3)
            mean_square(1)
            broadcast_rstd(1)

            def mix_unit(j, mid=None):
                n = N_MIX + j
                kind, _, half = MIX[j]
                banks = (0, 1) if j % 2 == 0 else (2, 3)
                if j >= 2:
                    pe.wait_ge(mix_evac, j - 1)
                if kind in ("vh", "vg"):
                    unit_v(n, banks, mid)
                else:
                    unit(n, n + 1, banks, HH, HL, wait_h=DB if j == 0 else None, mid=mid,
                         width=RANK if kind == "low" else CW)

            def head(a, before_far=None):
                p, r = prep_of(a), rows_of(a)
                q, k = PREPS[p]["q"], PREPS[p]["k"]
                for g in range(3):
                    bank = 4 + g % 2
                    pe.wait_ge(prep, 18 * p + 4 * (g + 1))
                    if g == 0 and a:
                        pe.wait_ge(evac_a, 2 * a)
                    if g == 1 and a:
                        pe.wait_ge(evac_v, a)
                    if g == 2:
                        pe.wait_ge(near_done, 6 * a + 2)
                    for j in range(2):
                        l = 2 * g + j
                        for t in range(TT):
                            ins = mm(PS[:, bank, 256 * j + 64 * t:256 * j + 64 * t + 64],
                                     KP[r, l, t * P:(t + 1) * P], QP[r, l, 64 * t:64 * t + 64], start=True, stop=True)
                    ins.then_inc(score_done, 1)
                pe.wait_ge(near_done, 6 * a + 4)
                for t in range(TT):
                    tok = slice(t * P, (t + 1) * P)
                    ins = mm(PS[:, 5, tok], k[r, tok], q[r, tok], start=True, stop=True)
                ins.then_inc(score_done, 1)
                if before_far is not None:
                    before_far()
                pe.wait_ge(prep, 18 * p + 16)
                if a:
                    pe.wait_ge(rs_ln, a)
                for t in range(TT):
                    mm(PS[0:64, 6, 64 * t:64 * t + 64], KL[r, t * P:t * P + 64], QU[r, t * P + 64:(t + 1) * P],
                       start=True, stop=True)
                for j in range(2):
                    ins = mm(PS[:, 6, 256 + P * j:256 + P * (j + 1)], W256[r, 2 * j * P:(2 * j + 1) * P],
                             W256[r, (2 * j + 1) * P:(2 * j + 2) * P], start=True, stop=True)
                ins.then_inc(score_done, 1)
                pe.wait_ge(prep, 18 * p + 18)
                pe.wait_ge(near_done, 6 * a + 6)
                for j in range(2):
                    ins = mm(PS[:, 4, 256 * j:256 * (j + 1)], W512[r, j * P:(j + 1) * P], W512[r, 256:512],
                             start=True, stop=True)
                ins.then_inc(score_done, 1)
                pe.wait_ge(mix_evac, V_NEEDS[a])
                pe.wait_ge(evac_v, a + 1)
                pe.wait_ge(evac_a, 2 * a + 2)
                if a:
                    pe.wait_ge(og_done, a)
                vv, hv = (VHG, a) if a < HEADS else (VGL, a - HEADS)
                for s in range(TT):
                    ins = mm(PS[:, 7, s * P:T], vv[:, s, hv * P:(hv + 1) * P], SC[:, s * T + s * P:(s + 1) * T],
                             start=s == 0, stop=s == TT - 1)
                ins.then_inc(pv_done, 1)

            def head_norm(a):
                def go():
                    pe.wait_ge(sq_o, a + 1)
                    pe.wait_ge(evac_a, 2 * a + 1)
                    mm(PS[:, 6, :], ONES[:, :], norm_in(a)[0], start=True, stop=True).then_inc(n_done, 1)
                return go

            for j in range(4):
                mix_unit(j)
            pe.wait_ge(sc_clear, 2)
            head(0)
            mix_unit(4, head_norm(0))
            head(1)
            mix_unit(5, head_norm(1))
            mix_unit(6)
            mix_unit(7)
            head(2)
            mix_unit(8, head_norm(2))
            mix_unit(9)
            head(3)
            pe.wait_ge(gkw_in, 16)
            pe.wait_ge(evac_a, 8)
            pe.wait_ge(evac_v, 4)
            for g in range(2):
                ins = mm(PS[:, 4 + g, :], GKW[:, g * P:(g + 1) * P], S[0:RANK, :], start=True, stop=True)
            ins.then_inc(gk_mm, 1)
            mix_unit(10, head_norm(3))
            mix_unit(11)
            mix_unit(12)
            pe.wait_ge(gk_sub, 4)
            head(4)
            head(5, head_norm(4))
            mix_unit(13, head_norm(5))
            mix_unit(14)
            head(6)
            head(7, head_norm(6))

            head_norm(7)()

            pe.wait_ge(mix_evac, len(MIX))
            with pe.Fori(0, 2) as i:
                for q in range(2):
                    n = N_END + 3 * q
                    for b in range(2):
                        pe.wait_ge(sig_done, 1 + 4 * i + 2 * q)
                        unit(n + b, 6 * i + n + b + 1, (2 * b, 2 * b + 1), HH, HL)
                    pe.wait_ge(y_lo, 2 * HEADS)
                    pe.wait_ge(y_hi, 2 * HEADS)
                    pe.wait_ge(merge, 1 + 6 * i + 3 * q)
                    pe.wait_ge(unit_lo, 6 * i + n + 3)
                    whi, wlo = weights(n + 2)
                    for br in range(2):
                        for k in range(HEADS):
                            for m in range(2):
                                w = slice(m * P, (m + 1) * P)
                                ins = three(PS[:, 4 + 2 * br + m, :], whi[:, HEADS * br + k, w], wlo[:, HEADS * br + k, w],
                                            YH[br][:, k, :], YL[br][:, k, :], k == 0, k == HEADS - 1)
                    ins.then_inc(unit_done, 1)

            pe.wait_ge(m_lo, 5)
            pe.wait_ge(m_hi, 4)
            pe.wait_ge(sig_done, 9)
            with pe.Fori(0, 2) as i:
                for q in range(2):
                    n = N_OUT + q
                    pe.wait_ge(xready, 16 + 4 * i + 2 * q - 2)
                    unit(n, 2 * i + n + 1, (2 * q, 2 * q + 1), MH, ML)
            mean_square(2)
            broadcast_rstd(2)

            swiglu_in(N_F2IN, 1, NP, False)
            pe.wait_ge(u_lo, 1 + 2 * NP)
            pe.wait_ge(u_hi, 2 * NP)

            def untranspose(b0):
                def go():
                    for b in (b0, b0 + 1):
                        pe.wait_ge(fin_y, b + 1)
                        if b >= 2:
                            pe.wait_ge(fin_ev, b - 1)
                        for t in range(TT):
                            ins = nc.tensor.transpose(PS[:, 4 + b % 2, t * P:(t + 1) * P],
                                                      YF[b % 2][:, t * P:(t + 1) * P], IDENT[:, :])
                        ins.then_inc(fin_t, 1)
                return go

            for i in range(2):
                for q in range(2):
                    n = N_F2DOWN + 3 * q
                    pair = 2 * i + q
                    down_pair(n, q, 6 * i + n + 1, 24 + 2 * pair - 2, untranspose(2 * pair - 2) if pair else None)
            untranspose(6)()
            mean_square(3)

        @block.scalar
        def _(act):
            A = nc.scalar.activation
            chain = [0]

            def self_wait(ins):
                chain[0] += 1
                ins.then_inc(act_self, 1)
                act.wait_ge(act_self, chain[0])

            row = 0
            for src in (c, b_ada.rearrange("a (n p) -> (a n) p", p=P), norm_gains[0].rearrange("g (n p) -> (g n) p", p=P),
                        final_norm.rearrange("(n p) -> n p", p=P), hg_norm, gla_norm,
                        b_gk_up.rearrange("a (n p) -> (a n) p", p=P), lb_logits.rearrange("a (n p) -> (a n) p", p=P)):
                if src is c:
                    src = c.rearrange("a (n p) -> (a n) p", p=P)
                n = src.shape[0]
                act.dma_start(PST[row:row + n, :], src).then_inc(small_in, 16)
                row += n
            act.dma_start(GKW[:, :], w_gk_up[0]).then_inc(gkw_in, 16)

            def split_hi(n, raw_val, done_val=None, size=UNIT):
                act.wait_ge(raw_in[slot(n)], raw_val)
                if done_val is not None:
                    act.wait_ge(unit_done, done_val)
                A(WH[slot(n)][:, 0:size], RAW[slot(n)][:, 0:size], ACT.Copy).then_inc(unit_hi, 1)

            def down_size(piece):
                return (UNIT, UNIT, (FB - 16) * CW)[piece]

            def square(b, x_val, sq_free, ap=None):
                act.wait_ge(xready, x_val)
                act.wait_ge(sacc, sq_free)
                A(SG[:, b % 2, :], ap, ACT.Square).then_inc(sq_ready, 1)

            def norm_blocks(g):
                act.wait_ge(av_ready, g + 1)
                for b in range(DB):
                    act.wait_ge(t_ready, DB * g + b + 1)
                    if b >= 2:
                        act.wait_ge(h_lo, DB * g + b - 1)
                    a, sh = AV[:, g, b:b + 1], MOD[:, 3 * DB * g + b:3 * DB * g + b + 1]
                    A(HFULL[:, b % 2, :], TN[:, b % 2, :], ACT.Identity, bias=sh, scale=a)
                    A(HH[:, b, :], TN[:, b % 2, :], ACT.Identity, bias=sh, scale=a).then_inc(h_hi, 1)

            act.wait_ge(small_ready, 1)
            A(COND[:, :], PT[:, PC_C:PC_C + DB], ACT.Silu).then_inc(cond_ready, 1)
            act.wait_ge(lb_ready, 1)
            A(LB[:, :], LBD[:, :], ACT.Sigmoid).then_inc(cond_ready, 1)
            A(OML[:, :], LBD[:, :], ACT.Sigmoid, scale=-1.0).then_inc(cond_ready, 1)
            for b in range(DB):
                square(b, b + 1, max(b, 1), X[:, b, :])
            split_hi(0, 16)
            split_hi(1, 16)
            norm_blocks(0)

            def swiglu_in(base_n, which, count, stop_split=False):
                with act.Fori(0, count) as i:
                    n = base_n
                    act.wait_ge(unit_done, 2 * i + n + 1)
                    act.wait_ge(u_lo, 1 + NP * which + i)
                    A(SG[:, :, :], PS[:, 0:2, :], ACT.Silu).then_inc(silu_done, 1)
                    split_hi(n + 2, 16 * i + raw_value(n + 2), 2 * i + n + 1)
                    split_hi(n + 3, 16 * i + raw_value(n + 3), 2 * i + n + 2)
                    act.wait_ge(umul_done, 1 + NP * which + i + 1)
                    A(UH[:, ds(2 * i, 2), :], SG[:, :, :], ACT.Copy).then_inc(u_hi, 1)

            swiglu_in(N_F1IN, 0, NP)

            def down(base_n, i, x0, sacc0, last=False, final=False):
                for q in range(2):
                    for piece in range(3):
                        n = base_n + 3 * q + piece
                        if not (last and q == 1 and piece >= 1):
                            nxt = (piece + 2) % 3
                            split_hi(n + 2, 16 * 3 * i + raw_value(n + 2), 6 * i + n + 1, down_size(nxt) if not (q == 1 and piece > 0) else UNIT)
                    for m in range(2):
                        b = 2 * q + m
                        if isinstance(i, int):
                            blk = X[:, 4 * i + b, :]
                        else:
                            blk = X[:, ds(4 * i + b, 1), :].rearrange("p a t -> p (a t)")
                        square(b, x0 + 4 * i + b + 1, sacc0 + 4 * i + b, blk)
                        if final:
                            g = 4 * i + b
                            if g >= 2:
                                act.wait_ge(fin_t, g - 1)
                            A(YF[g % 2][:, :], blk, ACT.Copy, scale=PT[:, PC_FINAL + g:PC_FINAL + g + 1]).then_inc(fin_y, 1)
                            if g >= 2:
                                final_copy(g - 2)

            def final_copy(b):
                act.wait_ge(fin_t, b + 1)
                A(OUTT[:, :, b * P:(b + 1) * P], PS[:, 4 + b % 2, :].rearrange("p (t f) -> p t f", f=P), ACT.Copy)\
                    .then_inc(fin_ev, 1)

            with act.Fori(0, 2) as i:
                down(N_F1DOWN, i, 8, 9)
            norm_blocks(1)

            def evacuate(j):
                n = N_MIX + j
                kind, _, half = MIX[j]
                act.wait_ge(unit_done, n + 1)
                ps = PS[:, 0:2, :] if j % 2 == 0 else PS[:, 2:4, :]
                two = slice(2 * half, 2 * half + 2)
                toks = ps.rearrange("p b (t c) -> p (b t) c", c=CW)
                if kind == "hf":
                    A(CHG[:, two, :], ps, ACT.Sigmoid)
                    A(KHG[:, two, :], ps, ACT.Sigmoid, scale=-1.0).then_inc(mix_evac, 1)
                elif kind == "hq":
                    A(QHG[:, two, :], ps, ACT.Silu).then_inc(mix_evac, 1)
                elif kind == "vh":
                    A(VHG[:, :, half * CW:(half + 1) * CW], toks, ACT.Copy).then_inc(mix_evac, 1)
                elif kind == "vg":
                    A(VGL[:, :, half * CW:(half + 1) * CW], toks, ACT.Copy).then_inc(mix_evac, 1)
                elif kind == "gh":
                    A(GO[:, two, :], ps, ACT.Silu).then_inc(mix_evac, 1)
                elif kind == "gg":
                    A(GO[:, HEADS + 2 * half:HEADS + 2 * half + 2, :], ps, ACT.Silu).then_inc(mix_evac, 1)
                elif kind == "low":
                    A(S[0:RANK, :], PS[0:RANK, 0 if j % 2 == 0 else 2, :], ACT.Copy).then_inc(mix_evac, 1)
                elif kind == "gk":
                    A(KGL[:, :, :], ps, ACT.Copy).then_inc(mix_evac, 1)
                elif kind == "gq":
                    A(QGL[:, :, :], ps, ACT.Copy, scale=64.0 ** -0.5).then_inc(mix_evac, 1)

            def unit_size(n):
                return DB * RANK if n == N_MIX + mix_at["low", 0] else UNIT

            def prepare(p):
                cc = PREPS[p]["c"]
                if p < HEADS:
                    act.wait_ge(mix_evac, PREP_NEEDS[p])
                    A(cc, cc, ACT.Ln, bias=LB[:, p:p + 1], scale=OML[:, p:p + 1]).then_inc(logf, 1)
                act.wait_ge(diffs, 12 * p + 6)
                A(QP[:, :, :], QP[:, :, :], ACT.Exp).then_inc(exps, 1)
                for l, B in enumerate(LEVELS):
                    act.wait_ge(diffs, 12 * p + 7 + l)
                    kk = blocks(KP[:, l, :], B)[:, :, 0:B // 2]
                    A(kk, kk, ACT.Exp).then_inc(exps, 1)
                act.wait_ge(cum, p + 1)
                if p:
                    act.wait_ge(score_done, 6 * before_prep(p) + 6)
                A(QU[:, :], cc, ACT.Exp).then_inc(exps, 1)
                act.wait_ge(kl_diff, p + 1)
                A(KL[:, :], KL[:, :], ACT.Exp).then_inc(exps, 1)
                act.wait_ge(gtab, p + 1)
                A(FT[:, :, :], GT[:, :, :], ACT.Exp).then_inc(exps, 1)

            def copy_far(a):
                act.wait_ge(score_done, 6 * a + 5)
                act.wait_ge(evac_v, a + 1)
                diag = SC[:, :].rearrange("p (i x) -> p i x", x=5 * P)
                A(diag[0:64, :, 64:P], PS[0:64, 6, 0:256].rearrange("p (i x) -> p i x", x=64), ACT.Copy)
                A(SC[:, :].rearrange("p (i x) -> p i x", x=2 * T + 2 * P)[:, :, P:2 * P],
                  PS[:, 6, 256:512].rearrange("p (i x) -> p i x", x=P), ACT.Copy).then_inc(evac_a, 1)
                act.wait_ge(score_done, 6 * a + 6)
                A(SC[:, 0:2 * T].rearrange("p (i x) -> p i x", x=T)[:, :, T // 2:T],
                  PS[:, 4, :].rearrange("p (i x) -> p i x", x=T // 2), ACT.Copy).then_inc(evac_a, 1)

            def squares(a):
                act.wait_ge(pv_done, a + 1)
                A(norm_in(a)[0], PS[:, 7, :], ACT.Square).then_inc(sq_o, 1)

            def finish(a):
                act.wait_ge(n_done, a + 1)
                rs = norm_in(a)[1]
                A(rs, PS[:, 6, :], ACT.Ln, bias=EPST[:, 0:1], scale=1.0 / P).then_inc(rs_ln, 1)
                act.wait_ge(rs_ln, a + 1)
                A(rs, rs, ACT.Exp, scale=-0.5).then_inc(rs_ready, 1)
                act.wait_ge(yf_ready, a + 1)
                A(YH[a // HEADS][:, a % HEADS, :], GO[:, a, :], ACT.Copy).then_inc(y_hi, 1)

            def decay_gla(g):
                act.wait_ge(gk_mm, 1)
                if g:
                    act.wait_ge(gk_sub, 2)
                A(S[:, :], PS[:, 4 + g, :], ACT.Abs, bias=PT[:, PC_BGK + g:PC_BGK + g + 1]).then_inc(gk_abs, 1)
                act.wait_ge(gk_abs, g + 1)
                self_wait(A(S[:, :], S[:, :], ACT.Exp, scale=-1.0))
                A(S[:, :], S[:, :], ACT.Ln, bias=ONES[:, 0:1]).then_inc(gk_ln, 1)

            for step in ORDER:
                kind, j = step[0], int(step[1:])
                if kind == "E":
                    n = N_MIX + j
                    split_hi(n + 2, raw_value(n + 2), n + 1, unit_size(n + 2))
                    evacuate(j)
                elif kind == "P":
                    prepare(j)
                elif kind == "A":
                    copy_far(j)
                elif kind == "Q":
                    squares(j)
                elif kind == "T":
                    finish(j)
                elif kind == "G":
                    decay_gla(j)

            with act.Fori(0, 2) as i:
                for q in range(2):
                    for b in range(2):
                        n = N_END + 3 * q + b
                        act.wait_ge(unit_done, 6 * i + n + 1)
                        act.wait_ge(m_lo, 1 + 2 * i + q)
                        A(RG[b][:, :, :], PS[:, 2 * b:2 * b + 2, :], ACT.Sigmoid).then_inc(sig_done, 1)
                        split_hi(n + 2, 64 * i + raw_value(n + 2), 6 * i + n + 1)
                    n = N_END + 3 * q + 2
                    split_hi(n + 2, 64 * i + raw_value(n + 2), 6 * i + n + 1)
                    act.wait_ge(merge, 1 + 6 * i + 3 * q + 3)
                    A(MH[:, ds(4 * i + 2 * q, 2), :], RG[0][:, :, :], ACT.Copy).then_inc(m_hi, 1)

            with act.Fori(0, 2) as i:
                for q in range(2):
                    n = N_OUT + q
                    split_hi(n + 2, 16 * i + raw_value(n + 2), 2 * i + n + 1)
                    for m in range(2):
                        b = 2 * q + m
                        square(b, 16 + 4 * i + b + 1, 18 + 4 * i + b, X[:, ds(4 * i + b, 1), :].rearrange("p a t -> p (a t)"))
            norm_blocks(2)
            swiglu_in(N_F2IN, 1, NP)
            for i in range(2):
                down(N_F2DOWN, i, 24, 27, last=i == 1, final=True)
            final_copy(6)
            final_copy(7)
            act.wait_ge(r_ready, 4)
            act.wait_ge(fin_ev, DB)
            for t in (2, 3):
                A(OUTT[:, t, :], OUTT[:, t, :], ACT.Copy, scale=R4[:, t:t + 1]).then_inc(fin_a, 1)

        @block.vector
        def _(dve):
            V = nc.vector
            chain = [0]

            def self_wait(ins):
                chain[0] += 1
                ins.then_inc(dve_self, 1)
                dve.wait_ge(dve_self, chain[0])

            def split_lo(n, value, done_val=None, size=UNIT):
                if done_val is not None:
                    dve.wait_ge(unit_done, done_val)
                dve.wait_ge(unit_hi, value)
                s = slot(n)
                V.tensor_tensor(WL[s][:, 0:size], RAW[s][:, 0:size], WH[s][:, 0:size].bitcast(F32), ALU.subtract)\
                    .then_inc(unit_lo, 1)

            def add_square(b, sq_val, acc_val):
                dve.wait_ge(sq_ready, sq_val)
                dve.wait_ge(sacc, acc_val)
                V.tensor_tensor(S[:, :], S[:, :], SG[:, b % 2, :], ALU.add).then_inc(sacc, 1)

            def clear_s():
                V.memset(S[:, :], 0.0).then_inc(sacc, 1)

            def mean_square(g):
                dve.wait_ge(ssq_done, g + 1)
                V.tensor_scalar(V4[:, :], PS[:, 6, 16:16 + TT], 1.0 / D, EPS, ALU.mult, ALU.add).then_inc(v_ready, 1)

            def norm(g, vectors):
                mean_square(g)
                dve.wait_ge(r_ready, g + 1)
                for t in range(TT):
                    V.tensor_scalar(DG[:, t * P:(t + 1) * P], IDENT[:, :], R4[:, t:t + 1], None, ALU.mult).then_inc(dg_ready, 1)
                vectors()
                dve.wait_ge(bc_done, g + 1)

                def lo(b):
                    dve.wait_ge(h_hi, DB * g + b + 1)
                    V.tensor_tensor(HL[:, b, :], HFULL[:, b % 2, :], HH[:, b, :].bitcast(F32), ALU.subtract).then_inc(h_lo, 1)

                for b in range(DB):
                    if b >= 2:
                        dve.wait_ge(h_hi, DB * g + b - 1)
                    V.tensor_tensor(TN[:, b % 2, :], X[:, b, :], PS[:, 7, :], ALU.mult).then_inc(t_ready, 1)
                    if b:
                        lo(b - 1)
                lo(DB - 1)

            def scale_vector(g):
                V.scalar_tensor_tensor(AV[:, g, :], MOD[:, 3 * DB * g + DB:3 * DB * g + 2 * DB], 1.0,
                                       PT[:, PC_GAIN + DB * g:PC_GAIN + DB * (g + 1)], ALU.add, ALU.mult).then_inc(av_ready, 1)

            dve.wait_ge(small_t, 1)
            V.tensor_copy(PT[:, :], PS[:, 5, 0:124]).then_inc(small_ready, 1)
            dve.wait_ge(small_ready, 1)
            V.tensor_tensor(LBD[:, :], PT[:, PC_LB:PC_LB + HEADS], PT[:, PC_LB + HEADS:PC_LB + 2 * HEADS],
                            ALU.subtract).then_inc(lb_ready, 1)
            clear_s()
            for b in range(DB):
                dve.wait_ge(xt_done, b + 1)
                V.tensor_copy(X[:, b, :], PS[:, b % 4, :]).then_inc(xready, 1)
                if b >= 1:
                    add_square(b - 1, b, b)
            add_square(DB - 1, DB, DB)
            dve.wait_ge(cond_ready, 3)
            V.tensor_scalar(LB[:, :], LB[:, :], LN_FLOOR, None, ALU.max).then_inc(lb_ready, 1)
            for k in range(DB):
                dve.wait_ge(ada0_in[k], 16)
                if k == 0:
                    V.tensor_scalar(ACC0[:, :], ADA0[:, 0, :], COND[:, 0:1], None, ALU.mult).then_inc(ada_acc, 1)
                else:
                    dve.wait_ge(ada_acc, k)
                    V.scalar_tensor_tensor(ACC0[:, :], ADA0[:, k, :], COND[:, k:k + 1], ACC0[:, :], ALU.mult, ALU.add)\
                        .then_inc(ada_acc, 1)
            split_lo(0, 1)
            split_lo(1, 2)

            def vectors0():
                dve.wait_ge(ada_red, 1)
                V.tensor_tensor(MOD[:, 0:2 * DB], PS[:, 6, 0:2 * DB], PT[:, PC_BADA:PC_BADA + 2 * DB], ALU.add)\
                    .then_inc(mod_ready, 1)
                dve.wait_ge(mod_ready, 1)
                scale_vector(0)

            norm(0, vectors0)

            def ada_piece(tiles, width, nslots, in_vals, acc0, red_val):
                dve.wait_ge(ada_red, red_val)
                for k in range(DB):
                    dve.wait_ge(ada_in[k % nslots], in_vals[k])
                    w = tiles[k % nslots][:, :]
                    if k == 0:
                        V.tensor_scalar(ACC[:, 0:width], w, COND[:, 0:1], None, ALU.mult).then_inc(ada_acc, 1)
                    else:
                        dve.wait_ge(ada_acc, acc0 + k)
                        V.scalar_tensor_tensor(ACC[:, 0:width], w, COND[:, k:k + 1], ACC[:, 0:width], ALU.mult, ALU.add)\
                            .then_inc(ada_acc, 1)

            def swiglu_in(base_n, which, with_ada):
                with dve.Fori(0, NP) as i:
                    n = base_n
                    split_lo(n + 2, 2 * i + n + 3, 2 * i + n + 1)
                    if with_ada:
                        ada_piece(ADAW, 512, 4, [32 * i + 16 * (k // 4 + 1) for k in range(DB)], DB + DB * i, i + 1)
                    dve.wait_ge(silu_done, 1 + NP * which + i + 1)
                    dve.wait_ge(unit_done, 2 * i + n + 2)
                    V.tensor_tensor(SG[:, :, :], SG[:, :, :], PS[:, 2:4, :], ALU.mult).then_inc(umul_done, 1)
                    split_lo(n + 3, 2 * i + n + 4, 2 * i + n + 2)
                    dve.wait_ge(u_hi, NP * which + i + 1)
                    V.tensor_tensor(UL[:, ds(2 * i, 2), :], SG[:, :, :], UH[:, ds(2 * i, 2), :].bitcast(F32),
                                    ALU.subtract).then_inc(u_lo, 1)
                    if with_ada:
                        dve.wait_ge(ada_red, i + 2)
                        V.tensor_tensor(MOD[:, ds(2 * DB + 4 * i, 4)], PS[:, 6, 0:4],
                                        PT[:, ds(PC_BADA + 2 * DB + 4 * i, 4)], ALU.add).then_inc(mod_ready, 1)

            swiglu_in(N_F1IN, 0, True)

            def add_to_x(i, b, bank, gate, x_val=None):
                if isinstance(i, int):
                    xb, gg = X[:, 4 * i + b, :], GATE[:, gate, 4 * i + b:4 * i + b + 1]
                else:
                    xb = X[:, ds(4 * i + b, 1), :].rearrange("p a t -> p (a t)")
                    gg = GATE[:, gate, ds(4 * i + b, 1)]
                V.scalar_tensor_tensor(xb, PS[:, bank, :], gg, xb, ALU.mult, ALU.add).then_inc(xready, 1)

            def down(base_n, i, gate, sq0, sacc0, last=False, ada=False):
                for q in range(2):
                    for piece in range(3):
                        n = base_n + 3 * q + piece
                        if piece == 2:
                            dve.wait_ge(unit_done, 6 * i + n + 1)
                            for m in range(2):
                                add_to_x(i, 2 * q + m, 2 * q + m, gate)
                        if not (last and q == 1 and piece >= 1):
                            nxt = (piece + 2) % 3
                            size = (FB - 16) * CW if nxt == 2 and not (q == 1 and piece > 0) else UNIT
                            split_lo(n + 2, 6 * i + n + 3, 6 * i + n + 1, size)
                        if ada and q == 0 and piece == 1:
                            ada_piece(ADAD, 768, 2, [16 * 2 * NP + 64 * i + 16 * (k // 2 + 1) for k in range(DB)],
                                      DB * (NP + 1) + DB * i, NP + 1 + i)
                    for m in range(2):
                        b = 2 * q + m
                        add_square(b, sq0 + 4 * i + b + 1, sacc0 + 4 * i + b)
                if ada:
                    dve.wait_ge(ada_red, NP + 2 + i)
                    V.tensor_tensor(MOD[:, ds(2 * DB + 4 * NP + 6 * i, 6)], PS[:, 6, 0:6],
                                    PT[:, ds(PC_BADA + 2 * DB + 4 * NP + 6 * i, 6)], ALU.add).then_inc(mod_ready, 1)

            dve.wait_ge(mod_ready, NP + 1)
            self_wait(V.tensor_scalar(GATE[:, 0, :], MOD[:, 2 * DB:3 * DB], 0.5, None, ALU.mult))
            clear_s()
            with dve.Fori(0, 2) as i:
                down(N_F1DOWN, i, 0, 8, 10, ada=True)

            def vectors1():
                dve.wait_ge(mod_ready, NP + 3)
                scale_vector(1)
                V.tensor_copy(GATE[:, 1, :], MOD[:, 5 * DB:6 * DB])
                self_wait(V.tensor_scalar(GATE[:, 2, :], MOD[:, 8 * DB:9 * DB], 0.5, None, ALU.mult))

            norm(1, vectors1)

            def prepare(p):
                q, k, cc = PREPS[p]["q"], PREPS[p]["k"], PREPS[p]["c"]
                dve.wait_ge(mix_evac, PREP_NEEDS[p])
                if p < HEADS:
                    V.tensor_scalar(k, k, OML[:, p:p + 1], None, ALU.mult)
                    dve.wait_ge(logf, p + 1)
                self_wait_cum(cc, p)
                tot = blocks(cc, CHUNK)[:, :, CHUNK - 1:CHUNK]
                if p:
                    dve.wait_ge(score_done, 6 * before_prep(p) + 6)
                V.tensor_tensor(blocks(KL[:, :], CHUNK), tot.to_broadcast([P, NC, CHUNK]), blocks(cc, CHUNK),
                                ALU.subtract).then_inc(kl_diff, 1)
                t1 = cc.rearrange("p (n b) -> p n b", b=CHUNK)[:, :, CHUNK - 1]
                if p:
                    dve.wait_ge(exps, 10 * p)
                V.tensor_copy(GT[:, 0, 0:5:4], t1[:, 1:6:4])
                V.tensor_copy(GT[:, 0, 3:8:4], t1[:, 2:7:4])
                V.tensor_copy(GT[:, 1, 2:6:3], t1[:, 3:5])
                self_wait(V.tensor_tensor(GT[:, 1, 1:7:5], t1[:, 2:6:3], t1[:, 3:5], ALU.add))
                V.tensor_tensor(GT[:, 1, 0:8:7], GT[:, 1, 1:7:5], t1[:, 1:7:5], ALU.add).then_inc(gtab, 1)
                for l, B in enumerate(LEVELS):
                    h = B // 2
                    dve.wait_ge(exps, 10 * p + 1)
                    qp = QP[:, l, :].rearrange("p (n h) -> p n h", h=h)
                    V.tensor_tensor(qp, qp, blocks(q, B)[:, :, h:B], ALU.mult).then_inc(prep, 1)
                    dve.wait_ge(exps, 10 * p + 2 + l)
                    kp = blocks(KP[:, l, :], B)[:, :, 0:h]
                    V.tensor_tensor(kp, kp, blocks(k, B)[:, :, 0:h], ALU.mult).then_inc(prep, 1)
                dve.wait_ge(exps, 10 * p + 9)
                V.tensor_tensor(QU[:, :], QU[:, :], q, ALU.mult).then_inc(prep, 1)
                V.tensor_tensor(KL[:, :], KL[:, :], k, ALU.mult).then_inc(prep, 1)
                dve.wait_ge(exps, 10 * p + 10)
                dve.wait_ge(prep, 18 * p + 14)
                f = FT[:, 0, :].rearrange("p (j n) -> p j n", n=4)
                for src, c0 in ((KL, 0), (QU, 2)):
                    for j in range(2):
                        cs = slice(4 * j + c0, 4 * j + c0 + 2)
                        ins = V.tensor_tensor(blocks(W256[:, :], CHUNK)[:, cs, :], blocks(src[:, :], CHUNK)[:, cs, :],
                                              FT[:, 0, cs].unsqueeze(2).to_broadcast([P, 2, CHUNK]), ALU.mult)
                    ins.then_inc(prep, 1)
                for src, c0 in ((KL, 0), (QU, 4)):
                    cs = slice(c0, c0 + 4)
                    V.tensor_tensor(blocks(W512[:, :], CHUNK)[:, cs, :], blocks(src[:, :], CHUNK)[:, cs, :],
                                    FT[:, 1, cs].unsqueeze(2).to_broadcast([P, 4, CHUNK]), ALU.mult).then_inc(prep, 1)

            def self_wait_cum(cc, p):
                V.tensor_tensor_scan(cc, RST[:, :], cc, 0.0, ALU.mult, ALU.add).then_inc(cum, 1)
                dve.wait_ge(cum, p + 1)

            diag = SC[:, :].rearrange("p (i x) -> p i x", x=5 * P)[:, :, 0:P]

            def copy_near(a):
                for g in range(3):
                    dve.wait_ge(score_done, 6 * a + g + 1)
                    for j in range(2):
                        l = 2 * g + j
                        h = LEVELS[l] // 2
                        near = diag.rearrange("p i (n b) -> p i n b", b=2 * h)[:, :, :, h:2 * h]
                        ps = PS[:, 4 + g % 2, 256 * j:256 * (j + 1)].rearrange("p (i n h) -> p i n h", i=TT, h=h)
                        m = MASK[:, l, :].rearrange("p (n h) -> p n h", h=h).unsqueeze(1).to_broadcast([P, TT, 64 // h, h])
                        if l:
                            dve.wait_ge(near_done, 6 * a + l)
                        ins = V.copy_predicated(near, m, ps).then_inc(near_done, 1)
                dve.wait_ge(score_done, 6 * a + 4)
                dve.wait_ge(near_done, 6 * a + 6)
                V.copy_predicated(diag, MASKD[:, :].unsqueeze(1).to_broadcast([P, TT, P]),
                                  PS[:, 5, :].rearrange("p (i x) -> p i x", x=P)).then_inc(evac_v, 1)

            def gate_out(a):
                dve.wait_ge(sq_o, a + 1)
                dve.wait_ge(mix_evac, G_NEEDS[a])
                V.tensor_tensor(GO[:, a, :], GO[:, a, :], PS[:, 7, :], ALU.mult).then_inc(og_done, 1)

            def finish(a):
                gain = PT[:, PC_HGN:PC_HGN + 1] if a < HEADS else PT[:, PC_GLN:PC_GLN + 1]
                dve.wait_ge(og_done, a + 1)
                dve.wait_ge(rs_ready, a + 1)
                V.scalar_tensor_tensor(GO[:, a, :], GO[:, a, :], gain, norm_in(a)[1], ALU.mult, ALU.mult).then_inc(yf_ready, 1)
                dve.wait_ge(y_hi, a + 1)
                V.tensor_tensor(YL[a // HEADS][:, a % HEADS, :], GO[:, a, :], YH[a // HEADS][:, a % HEADS, :].bitcast(F32),
                                ALU.subtract).then_inc(y_lo, 1)

            def decay_gla(g):
                cc = CGL[:, g, :]
                dve.wait_ge(gk_abs, g + 1)
                V.tensor_scalar(cc, PS[:, 4 + g, :], PT[:, PC_BGK + g:PC_BGK + g + 1], 0.0, ALU.add, ALU.min).then_inc(gk_sub, 1)
                dve.wait_ge(gk_sub, 2 * g + 1)
                dve.wait_ge(gk_ln, g + 1)
                V.tensor_tensor(cc, cc, S[:, :], ALU.subtract).then_inc(gk_sub, 1)
                dve.wait_ge(gk_sub, 2 * g + 2)
                self_wait(V.tensor_scalar(cc, cc, 1.0 / 16.0, None, ALU.mult))

            for step in ORDER:
                kind, j = step[0], int(step[1:])
                if kind == "E":
                    n = N_MIX + j
                    size = DB * RANK if n + 2 == N_MIX + mix_at["low", 0] else UNIT
                    split_lo(n + 2, n + 3, n + 1, size)
                elif kind == "P":
                    prepare(j)
                elif kind == "V":
                    if j == 0:
                        dve.wait_ge(consts, 33)
                    copy_near(j)
                elif kind == "Q":
                    gate_out(j)
                elif kind == "T":
                    finish(j)
                elif kind == "G":
                    decay_gla(j)

            with dve.Fori(0, 2) as i:
                for q in range(2):
                    for b in range(3):
                        n = N_END + 3 * q + b
                        if b == 2:
                            dve.wait_ge(unit_done, 6 * i + n + 1)
                            dve.wait_ge(sig_done, 1 + 4 * i + 2 * q + 2)
                            for br in range(2):
                                V.tensor_tensor(RG[br][:, :, :], RG[br][:, :, :], PS[:, 4 + 2 * br:6 + 2 * br, :],
                                                ALU.mult).then_inc(merge, 1)
                            dve.wait_ge(merge, 1 + 6 * i + 3 * q + 2)
                            V.tensor_tensor(RG[0][:, :, :], RG[0][:, :, :], RG[1][:, :, :], ALU.add).then_inc(merge, 1)
                        split_lo(n + 2, 6 * i + n + 3, 6 * i + n + 1)
                    dve.wait_ge(m_hi, 2 * i + q + 1)
                    V.tensor_tensor(ML[:, ds(4 * i + 2 * q, 2), :], RG[0][:, :, :],
                                    MH[:, ds(4 * i + 2 * q, 2), :].bitcast(F32), ALU.subtract).then_inc(m_lo, 1)

            clear_s()
            with dve.Fori(0, 2) as i:
                for q in range(2):
                    n = N_OUT + q
                    dve.wait_ge(unit_done, 2 * i + n + 1)
                    for m in range(2):
                        add_to_x(i, 2 * q + m, 2 * q + m, 1)
                    split_lo(n + 2, 2 * i + n + 3, 2 * i + n + 1)
                    for m in range(2):
                        b = 2 * q + m
                        add_square(b, 16 + 4 * i + b + 1, 19 + 4 * i + b)
            norm(2, lambda: scale_vector(2))
            swiglu_in(N_F2IN, 1, False)
            clear_s()
            for i in range(2):
                down(N_F2DOWN, i, 2, 24, 28, last=i == 1)
            mean_square(3)
            dve.wait_ge(r_ready, 4)
            dve.wait_ge(fin_ev, DB)
            for t in (0, 1):
                V.tensor_scalar(OUTT[:, t, :], OUTT[:, t, :], R4[:, t:t + 1], None, ALU.mult).then_inc(fin_v, 1)


def arena_offset(nc, arena):
    size = arena.shape[1] * 4
    return (nc.sbuf_base - size) // 32 * 32


_INS = ["x", "c", "w_ada", "b_ada", "norm_gains", "ffn1_w_in", "ffn1_w_down", "w_in_mix", "w_gk_up", "b_gk_up",
        "lb_logits", "hg_norm", "gla_norm", "w_up_hg", "w_up_gla", "w_out", "ffn2_w_in", "ffn2_w_down", "final_norm"]


def kernel(**inputs):
    import numpy as _np
    import concourse.bacc as _bacc
    from concourse import mybir as _mybir
    from concourse.bass_utils import run_bass_kernel_spmd as _run

    nc = _bacc.Bacc("TRN2", target_bir_lowering=False, num_devices=1)
    arrays, args = {}, []
    for name in _INS:
        a = _np.ascontiguousarray(inputs[name])
        arrays[f"in_{name}_dram"] = a
        args.append(nc.dram_tensor(f"in_{name}_dram", a.shape, _mybir.dt.from_np(a.dtype), kind="ExternalInput").ap())
    args.append(nc.dram_tensor("out_0_dram", inputs["x"].shape, _mybir.dt.float32, kind="ExternalOutput").ap())
    trunk_program(nc, *args)
    r = _run(nc, [arrays], core_ids=[0])
    return r.results[0]["out_0_dram"]
```

```python
import concourse.bass as bass
from concourse import mybir


def trunk_program(nc, x, c, w_ada, b_ada, norm_gains, ffn1_w_in, ffn1_w_down, w_in_mix, w_gk_up, b_gk_up,
                  lb_logits, hg_norm, gla_norm, w_up_hg, w_up_gla, w_out, ffn2_w_in, ffn2_w_down,
                  final_norm, out):
    F32, F32R, BF16, I8 = mybir.dt.float32, mybir.dt.float32r, mybir.dt.bfloat16, mybir.dt.int8
    ACT, ALU = mybir.ActivationFunctionType, mybir.AluOpType
    ds = bass.ds

    P = 128
    T = x.shape[1]
    D = x.shape[2]
    DB = D // P
    TT = T // P
    FF = ffn1_w_down.shape[1]
    FB = FF // P
    CW = 256
    NP = FF // CW
    CHUNK = 64
    NC = T // CHUNK
    HEADS = 4
    EPS = 1e-6
    UNIT = DB * CW
    AW = 512
    LN_FLOOR = 2.0 ** -63

    xv = x[0]
    ada = w_ada[0]
    widths = (512, 512, 512, 512, 256, 256, 512, 512, 16, D, D)
    at = [sum(widths[:i]) for i in range(len(widths))]
    HQ, HF, HI, HG, GQ, GK, GV, GG, GLOW, RHG, RGLA = at

    N_F1IN = 0
    N_F1DOWN = N_F1IN + 2 * NP
    N_MIX = N_F1DOWN + 12
    MIX = [("hf", HF, 0), ("hq", HQ, 0), ("vh", HI, 0), ("gh", HG, 0), ("hf", HF, 1), ("hq", HQ, 1),
           ("vh", HI, 1), ("gh", HG, 1), ("low", GLOW, 0), ("gk", GK, 0), ("gq", GQ, 0), ("vg", GV, 0),
           ("gg", GG, 0), ("vg", GV, 1), ("gg", GG, 1)]
    N_END = N_MIX + len(MIX)
    N_OUT = N_END + 12
    N_F2IN = N_OUT + 4
    N_F2DOWN = N_F2IN + 2 * NP
    N_UNITS = N_F2DOWN + 12
    mix_at = {}
    for j, (kind, _, half) in enumerate(MIX):
        mix_at[kind, half] = j
    RANK = 16

    from contextlib import ExitStack
    ctx = ExitStack()
    with ctx:
        def sb(name, shape, dt=F32):
            return ctx.enter_context(nc.sbuf_tensor(name, shape, dt))

        def sem(name):
            return ctx.enter_context(nc.semaphore(name))

        X = sb("X", [P, DB, T])
        RAW = [sb(f"RAW{s}", [P, UNIT]) for s in range(2)]
        WH = [sb(f"WH{s}", [P, UNIT], F32R) for s in range(2)]
        WL = [sb(f"WL{s}", [P, UNIT], F32R) for s in range(2)]
        S = sb("S", [P, T])
        PT = sb("PT", [P, 124])
        PST = sb("PST", [124, P])
        MOD = sb("MOD", [P, 9 * DB])
        AV = sb("AV", [P, 4, DB])
        GATE = sb("GATE", [P, 3, DB])
        COND = sb("COND", [P, DB])
        IDENT = sb("IDENT", [P, P])
        ONES = sb("ONES", [P, P])
        MASKF = sb("MASKF", [P, 64])
        MASK = sb("MASK", [P, 6, 64], I8)
        MASKD = sb("MASKD", [P, P], I8)
        RST = sb("RST", [P, T], BF16)
        V4 = sb("V4", [P, TT])
        R4 = sb("R4", [P, TT])
        HALF4 = sb("HALF4", [P, TT])
        EPST = sb("EPST", [P, 1])
        LB = sb("LB", [P, HEADS])
        OML = sb("OML", [P, HEADS])
        LBD = sb("LBD", [P, HEADS])
        GT = sb("GT", [P, 2, NC])
        FT = sb("FT", [P, 2, NC])
        GKW = sb("GKW", [RANK, 256])

        H_BYTES = DB * T * 4
        ARENA = 106496
        arena = sb("arena", [P, (ARENA + 2 * H_BYTES) // 4])
        base = arena_offset(nc, arena)

        def place(name, shape, offset, dt=F32):
            return nc.alloc_sbuf_tensor_at(name, shape, dt, offset=base + offset)

        HO = ARENA
        HH = place("HH", [P, DB, T], HO, F32R)
        HL = place("HL", [P, DB, T], HO + H_BYTES, F32R)
        OUTT = place("OUTT", [P, TT, D], HO)
        UH = place("UH", [P, FB, T], 0, F32R)
        UL = place("UL", [P, FB, T], FB * T * 4, F32R)
        NT = 2 * FB * T * 4 - 8192
        TN = place("TN", [P, 2, T], NT)
        HFULL = place("HFULL", [P, 2, T], NT + 4096)
        SG = place("SG", [P, 2, T], 2 * FB * T * 4)
        DG = place("DG", [P, T], 2 * FB * T * 4)
        ADAW = [place(f"ADAW{s}", [P, 2, AW], 94208 + 4096 * s) for s in range(2)]
        YF = [place(f"YF{s}", [P, T], 94208 + 2048 * s) for s in range(2)]
        ACC = place("ACC", [P, AW], 102400)
        ADA0 = place("ADA0", [P, 4, DB, AW], 0)
        XST = place("XST", [P, TT, D], 65536)
        ACC0 = place("ACC0", [P, 4, AW], NT)
        QHG = place("QHG", [P, HEADS, T], 0)
        KHG = place("KHG", [P, HEADS, T], 8192)
        CHG = place("CHG", [P, HEADS, T], 16384)
        VHG = place("VHG", [P, TT, 512], 24576)
        QGL = place("QGL", [P, 2, T], 32768)
        KGL = place("KGL", [P, 2, T], 36864)
        CGL = place("CGL", [P, 2, T], 40960)
        VGL = place("VGL", [P, TT, 512], 45056)
        GO = place("GO", [P, 2 * HEADS, T], 53248)
        KP = place("KP", [P, 6, T], 69632)
        SC = place("SC", [P, TT * 640], 81920)
        QP = place("QP", [P, 6, T // 2], 92160)
        QU = place("QU", [P, T], 98304)
        KL = place("KL", [P, T], 100352)
        W256 = place("W256", [P, T], 102400)
        W512 = place("W512", [P, T], 104448)
        YH = [place("YHh", [P, HEADS, T], 8192, F32R), place("YHg", [P, HEADS, T], 0, F32R)]
        YL = [place("YLh", [P, HEADS, T], 16384, F32R), place("YLg", [P, HEADS, T], 24576, F32R)]
        MH = place("MH", [P, DB, T], 53248, F32R)
        ML = place("ML", [P, DB, T], 69632, F32R)
        RG = [place(f"RG{s}", [P, 2, T], 86016 + 4096 * s) for s in range(2)]

        PS = ctx.enter_context(nc.psum_tensor("PS", [P, 8, 512], F32))

        PC_C, PC_BADA, PC_GAIN, PC_FINAL, PC_HGN, PC_GLN, PC_BGK, PC_LB = 0, 8, 80, 104, 112, 113, 114, 116

        raw_in = [sem("raw_in0"), sem("raw_in1")]
        unit_hi = sem("unit_hi")
        unit_lo = sem("unit_lo")
        unit_done = sem("unit_done")
        small_in, x_in, ada0_in, gkw_in = sem("small_in"), sem("x_in"), [sem(f"ada0_in{j}") for j in range(8)], sem("gkw_in")
        ada_in = [sem(f"ada_in{s}") for s in range(2)]
        consts, constd = sem("consts"), sem("constd")
        small_t, small_ready, cond_ready, lb_ready = sem("small_t"), sem("small_ready"), sem("cond_ready"), sem("lb_ready")
        ada_acc, ada_red, mod_ready = sem("ada_acc"), sem("ada_red"), sem("mod_ready")
        xt_done, xready = sem("xt_done"), sem("xready")
        sq_ready, sacc = sem("sq_ready"), sem("sacc")
        ssq_done, v_ready, r_ready, dg_ready, bc_done = sem("ssq_done"), sem("v_ready"), sem("r_ready"), sem("dg_ready"), sem("bc_done")
        av_ready, t_ready, h_hi, h_lo = sem("av_ready"), sem("t_ready"), sem("h_hi"), sem("h_lo")
        silu_done, umul_done, u_hi, u_lo = sem("silu_done"), sem("umul_done"), sem("u_hi"), sem("u_lo")
        mix_evac = sem("mix_evac")
        sc_clear = sem("sc_clear")
        logf, cum, diffs, gtab, exps, prep = sem("logf"), sem("cum"), sem("diffs"), sem("gtab"), sem("exps"), sem("prep")
        kl_diff, near_done = sem("kl_diff"), sem("near_done")
        score_done, evac_v, evac_a, pv_done = sem("score_done"), sem("evac_v"), sem("evac_a"), sem("pv_done")
        sq_o, og_done, n_done, rs_ln, rs_ready = sem("sq_o"), sem("og_done"), sem("n_done"), sem("rs_ln"), sem("rs_ready")
        yf_ready, y_hi, y_lo = sem("yf_ready"), sem("y_hi"), sem("y_lo")
        gk_mm, gk_abs, gk_ln, gk_sub = sem("gk_mm"), sem("gk_abs"), sem("gk_ln"), sem("gk_sub")
        sig_done, merge, m_hi, m_lo = sem("sig_done"), sem("merge"), sem("m_hi"), sem("m_lo")
        fin_y, fin_t, fin_ev, fin_v, fin_a, out_dma = sem("fin_y"), sem("fin_t"), sem("fin_ev"), sem("fin_v"), sem("fin_a"), sem("out_dma")
        dve_self, act_self = sem("dve_self"), sem("act_self")

        LEVELS = [64, 32, 16, 8, 4, 2]

        def slot(n):
            return n % 2

        def raw_count(n):
            return 16 * (n // 2 + 1)

        def blocks(ap, size):
            return ap.rearrange("p (n b) -> p n b", b=size)

        PREPS = [dict(q=QHG[:, h, :], k=KHG[:, h, :], c=CHG[:, h, :]) for h in range(HEADS)] + \
                [dict(q=QGL[:, g, :], k=KGL[:, g, :], c=CGL[:, g, :]) for g in range(2)]
        PREP_NEEDS = [2, 2, 6, 6, 11, 11]
        V_NEEDS = [3, 3, 7, 7, 12, 12, 14, 14]
        G_NEEDS = [4, 4, 8, 8, 13, 13, 15, 15]

        def prep_of(a):
            return a if a < HEADS else HEADS + (a - HEADS) // 2

        def rows_of(a):
            return slice(0, P) if a < HEADS else slice(64 * (a % 2), 64 * (a % 2) + 64)

        def before_prep(p):
            return {1: 0, 2: 1, 3: 2, 4: 3, 5: 5}[p]

        def norm_in(a):
            if a < HEADS:
                return CHG[:, a, :], KHG[:, a, :]
            return QHG[:, a - HEADS, :], VHG[:, a - HEADS, :]

        STAGES_AT = [(29, 30, 31, 33, 36), (41, 42, 43, 45, 48), (59, 60, 61, 64, 67), (74, 75, 76, 78, 81),
                     (91, 92, 93, 98, 107), (99, 100, 101, 110, 112), (113, 114, 115, 117, 123),
                     (118, 119, 120, 125, 128)]
        GK_AT = 80
        ORDER = ("E0 E1 a0 b0 E2 V0 A0 E3 a1 Q0 b1 T0 E4 U0 V1 A1 Q1 E5 T1 a2 U1 b2 E6 V2 A2 E7 Q2 a3 T2 b3 U2 E8 "
                 "V3 A3 E9 Q3 G0 G1 T3 a4 U3 E10 b4 V4 A4 E11 V5 A5 E12 Q4 a5 T4 b5 U4 Q5 E13 T5 V6 A6 U5 V7 A7 "
                 "E14 Q6 T6 U6 Q7 T7 U7").split()

        def mix_banks(j):
            return (2, 3) if j % 2 == 0 else (0, 1)

        small, row = [], 0
        for src in (c.rearrange("a (n p) -> (a n) p", p=P), b_ada.rearrange("a (n p) -> (a n) p", p=P),
                    norm_gains[0].rearrange("g (n p) -> (g n) p", p=P), final_norm.rearrange("(n p) -> n p", p=P),
                    hg_norm, gla_norm, b_gk_up.rearrange("a (n p) -> (a n) p", p=P),
                    lb_logits.rearrange("a (n p) -> (a n) p", p=P)):
            small.append((PST[row:row + src.shape[0], :], src))
            row += src.shape[0]

        block = ctx.enter_context(nc.Block())

        @block.sync
        def _(sp):
            def load(n, nslot, dst_cols, src, wait=None):
                if wait is not None:
                    sp.wait_ge(unit_lo, wait)
                sp.dma_start(dst_cols, src).then_inc(raw_in[nslot], 16)

            def cols(w, col, kb0=0, nk=DB, width=CW):
                return w.rearrange("(k p) n -> p k n", p=P)[:, kb0:kb0 + nk, col] if not isinstance(col, int) \
                    else w.rearrange("(k p) n -> p k n", p=P)[:, kb0:kb0 + nk, col:col + width]

            def raw(n, nk=DB, width=CW):
                return RAW[slot(n)][:, 0:nk * width].rearrange("p (k c) -> p k c", c=width)

            for t in range(TT):
                sp.dma_start(XST[:, t, :], xv[t * P:(t + 1) * P, :]).then_inc(x_in, 16)
            for dst, src in small[len(small) // 2:]:
                sp.dma_start(dst, src).then_inc(small_in, 16)
            ada_rows = ada.rearrange("(k p) n -> p k n", p=P)
            for piece in range(4):
                for half in range(2):
                    ks = slice(4 * half, 4 * half + 4)
                    sp.dma_start(ADA0[:, piece, ks, :], ada_rows[:, ks, piece * AW:(piece + 1) * AW])\
                        .then_inc(ada0_in[2 * piece + half], 16)

            def load_ada(acc, col):
                for j in range(4):
                    sp.wait_ge(ada_acc, acc + 2 * j - 2)
                    sp.dma_start(ADAW[j % 2][:, :, :], ada_rows[:, 2 * j:2 * j + 2, col]).then_inc(ada_in[j % 2], 16)

            w1 = ffn1_w_in[0]
            load(0, 0, raw(0), cols(w1, 0))
            load(1, 1, raw(1), cols(w1, FF))
            load_ada(4 * DB, slice(4 * AW, 5 * AW))

            def load_down(base_n, i, w, last=False):
                for q in range(2):
                    for piece, (kb0, nk) in enumerate(((0, 8), (8, 8), (16, FB - 16))):
                        n = base_n + 3 * q + piece
                        load(n, slot(n), raw(n, nk), cols(w, ds(2 * CW * i + q * CW, CW), kb0, nk), 6 * i + n - 1)

            with sp.Fori(0, NP - 1) as i:
                load(2, 0, raw(2), cols(w1, ds(CW * i + CW, CW)), 2 * i + 1)
                load(3, 1, raw(3), cols(w1, ds(CW * i + CW + FF, CW)), 2 * i + 2)
                load_ada(5 * DB + DB * i, ds(AW * i + 5 * AW, AW))

            for j in range(12):
                n = N_F1DOWN + j
                kb0, nk = ((0, 8), (8, 8), (16, FB - 16))[j % 3]
                load(n, slot(n), raw(n, nk), cols(ffn1_w_down[0], j // 3 * CW, kb0, nk), n - 1)
                if j in (1, 4, 10):
                    piece = NP + 4 + (1, 4, 10).index(j)
                    load_ada(DB * piece, slice(piece * AW, (piece + 1) * AW))

            wm = w_in_mix[0]
            for j, (kind, col, half) in enumerate(MIX):
                n = N_MIX + j
                width = RANK if kind == "low" else CW
                load(n, slot(n), raw(n, DB, width), cols(wm, col + half * CW, width=width), n - 1)

            with sp.Fori(0, 2) as i:
                for q in range(2):
                    n = N_END + 3 * q
                    load(n, slot(n), raw(n), cols(wm, ds(RHG + 2 * CW * i + CW * q, CW)), 6 * i + n - 1)
                    load(n + 1, slot(n + 1), raw(n + 1), cols(wm, ds(RGLA + 2 * CW * i + CW * q, CW)), 6 * i + n)
                    up = raw(n + 2)
                    sp.wait_ge(unit_lo, 6 * i + n + 1)
                    sp.dma_start(up[:, 0:4, :], cols(w_up_hg[0], ds((i + i) * CW + CW * q, CW), 0, 4)).then_inc(raw_in[slot(n)], 16)
                    sp.dma_start(up[:, 4:8, :], cols(w_up_gla[0], ds(2 * CW * i + CW * q, CW), 0, 4)).then_inc(raw_in[slot(n)], 16)
            with sp.Fori(0, 2) as i:
                for q in range(2):
                    n = N_OUT + q
                    load(n, slot(n), raw(n), cols(w_out[0], ds(2 * CW * i + CW * q, CW)), 2 * i + n - 1)
            w2 = ffn2_w_in[0]
            with sp.Fori(0, NP) as i:
                load(N_F2IN, slot(N_F2IN), raw(N_F2IN), cols(w2, ds(CW * i, CW)), 2 * i + N_F2IN - 1)
                load(N_F2IN + 1, slot(N_F2IN + 1), raw(N_F2IN + 1), cols(w2, ds(CW * i + FF, CW)), 2 * i + N_F2IN)
            with sp.Fori(0, 2) as i:
                load_down(N_F2DOWN, i, ffn2_w_down[0])
            for t in range(TT):
                sp.wait_ge(fin_v if t < 2 else fin_a, t % 2 + 1)
                sp.dma_start(out[0, t * P:(t + 1) * P, :], OUTT[:, t, :]).then_inc(out_dma, 16)
            sp.wait_ge(out_dma, 16 * TT)

        def raw_value(n, i_term=0):
            extra = 0
            for q in range(4):
                u = N_END + 3 * q + 2
                if u <= n and slot(u) == slot(n):
                    extra += 1
            return 16 * (n // 2 + 1 + extra) + i_term

        @block.gpsimd
        def _(pool):
            for counted in (silu_done, umul_done, u_lo, sig_done, merge, m_lo):
                pool.sem_inc(counted, 1)
            cn = [0]

            def done(ins):
                cn[0] += 1
                ins.then_inc(consts, 1)

            done(nc.gpsimd.memset(ONES[:, :], 1.0))
            done(nc.gpsimd.memset(IDENT[:, :], 0.0))
            done(nc.gpsimd.memset(HALF4[:, :], -0.5))
            done(nc.gpsimd.memset(EPST[:, :], EPS))
            done(nc.gpsimd.memset(GT[:, :, :], 0.0))
            done(nc.gpsimd.memset(RST[:, :], 1.0))
            pool.wait_ge(consts, cn[0])
            done(nc.gpsimd.affine_select(out=IDENT[:, :], in_=IDENT[:, :], compare_op=ALU.not_equal, fill=1.0,
                                         base=0, pattern=[[-1, P]], channel_multiplier=1))
            pool.wait_ge(consts, cn[0])
            done(nc.gpsimd.tensor_copy(MASKD[:, :], IDENT[:, :]))
            done(nc.gpsimd.memset(blocks(RST[:, :], CHUNK)[:, :, 0], 0.0))
            nc.gpsimd.memset(S[:, :], 0.0).then_inc(sacc, 1)
            for b in range(DB):
                pool.wait_ge(sq_ready, b + 1)
                pool.wait_ge(sacc, b + 1)
                nc.gpsimd.tensor_tensor(S[:, :], S[:, :], SG[:, b % 2, :], ALU.add).then_inc(sacc, 1)
            pool.wait_ge(v_ready, 1)
            nc.gpsimd.tensor_tensor(R4[:, :], V4[:, :], HALF4[:, :], ALU.pow).then_inc(r_ready, 1)
            for l, B in enumerate(LEVELS):
                h, nb = B // 2, P // B
                done(nc.gpsimd.memset(MASKF[:, :], 1.0))
                pool.wait_ge(consts, cn[0])
                m = MASKF[:, :].rearrange("p (n h) -> p n h", h=h)
                done(nc.gpsimd.affine_select(out=m, in_=m, compare_op=ALU.is_ge, fill=0.0, base=0,
                                             pattern=[[-B, nb], [0, h]], channel_multiplier=1))
                pool.wait_ge(consts, cn[0])
                done(nc.gpsimd.affine_select(out=m, in_=m, compare_op=ALU.is_ge, fill=0.0, base=h - 1,
                                             pattern=[[B, nb], [0, h]], channel_multiplier=-1))
                pool.wait_ge(consts, cn[0])
                done(nc.gpsimd.tensor_copy(MASK[:, l, :], MASKF[:, :]))
                pool.wait_ge(consts, cn[0])

            def rsqrt(g):
                pool.wait_ge(v_ready, g + 1)
                nc.gpsimd.tensor_tensor(R4[:, :], V4[:, :], HALF4[:, :], ALU.pow).then_inc(r_ready, 1)

            rsqrt(1)
            pool.wait_ge(h_lo, 2 * DB)
            nc.gpsimd.memset(SC[:, :], 0.0).then_inc(sc_clear, 1)
            nc.gpsimd.memset(KP[:, :, :], 0.0).then_inc(sc_clear, 1)
            pool.wait_ge(sc_clear, 2)
            for p in range(6):
                cc = PREPS[p]["c"]
                pool.wait_ge(cum, p + 1)
                if p:
                    pool.wait_ge(score_done, 6 * before_prep(p) + 3)
                for l, B in enumerate(LEVELS):
                    h = B // 2
                    cb = blocks(cc, B)
                    mid = cb[:, :, h - 1:h].to_broadcast([P, T // B, h])
                    nc.gpsimd.tensor_tensor(QP[:, l, :].rearrange("p (n h) -> p n h", h=h), cb[:, :, h:B], mid,
                                            ALU.subtract).then_inc(diffs, 1)
                for l, B in enumerate(LEVELS):
                    h = B // 2
                    cb = blocks(cc, B)
                    mid = cb[:, :, h - 1:h].to_broadcast([P, T // B, h])
                    nc.gpsimd.tensor_tensor(blocks(KP[:, l, :], B)[:, :, 0:h], mid, cb[:, :, 0:h],
                                            ALU.subtract).then_inc(diffs, 1)
            rsqrt(2)
            rsqrt(3)

        @block.tensor
        def _(pe):
            mm = nc.tensor.matmul

            def weights(n, width=CW):
                hi = WH[slot(n)][:, :].rearrange("p (k c) -> p k c", c=width)
                lo = WL[slot(n)][:, :].rearrange("p (k c) -> p k c", c=width)
                return hi, lo

            def three(ps, whi, wlo, ahi, alo, start, stop):
                mm(ps, whi, ahi, start=start, stop=False)
                mm(ps, whi, alo, start=False, stop=False)
                return mm(ps, wlo, ahi, start=False, stop=stop)

            def unit(n, value, banks, ahi, alo, kb0=0, nk=DB, first=True, last=True, wait_h=None,
                     width=CW, before=None):
                pe.wait_ge(unit_lo, value)
                whi, wlo = weights(n, width)
                for k in range(nk):
                    if before is not None:
                        before(k)
                    if wait_h is not None:
                        pe.wait_ge(h_lo, wait_h + k + 1)
                    for m in range(max(width // P, 1)):
                        w = slice(m * P, min((m + 1) * P, width))
                        rows = w.stop - w.start
                        ins = three(PS[0:rows, banks[m], :], whi[:, k, w], wlo[:, k, w], ahi[:, kb0 + k, :],
                                    alo[:, kb0 + k, :], first and k == 0, last and k == nk - 1)
                ins.then_inc(unit_done, 1)

            def unit_v(n, banks, before):
                pe.wait_ge(unit_lo, n + 1)
                whi, wlo = weights(n)
                for t in range(TT):
                    ps = PS[:, banks[t // 2], (t % 2) * CW:(t % 2 + 1) * CW]
                    tok = slice(t * P, (t + 1) * P)
                    for k in range(DB):
                        if k % 4 == 0:
                            before(2 * t + k // 4)
                        mm(ps, HH[:, k, tok], whi[:, k, :], start=k == 0, stop=False)
                        mm(ps, HL[:, k, tok], whi[:, k, :], start=False, stop=False)
                        ins = mm(ps, HH[:, k, tok], wlo[:, k, :], start=False, stop=k == DB - 1)
                ins.then_inc(unit_done, 1)

            def mean_square(g):
                pe.wait_ge(sacc, 9 * g + 9)
                for t in range(TT):
                    ins = mm(PS[:, 7, t:t + 1], S[:, t * P:(t + 1) * P], ONES[:, 0:1], start=True, stop=True)
                ins.then_inc(ssq_done, 1)

            def broadcast_rstd(g):
                pe.wait_ge(dg_ready, TT * (g + 1))
                mm(PS[:, 7, :], ONES[:, :], DG[:, :], start=True, stop=True).then_inc(bc_done, 1)

            pe.wait_ge(consts, 7)
            pe.wait_ge(small_in, 16 * 8)
            nc.tensor.transpose(PS[:, 5, 0:124], PST[:, :], IDENT[0:124, 0:124]).then_inc(small_t, 1)
            pe.wait_ge(x_in, 16 * TT)
            for b in range(DB):
                if b >= 4:
                    pe.wait_ge(xready, b - 3)
                for t in range(TT):
                    ins = nc.tensor.transpose(PS[:, b % 4, t * P:(t + 1) * P], XST[:, t, b * P:(b + 1) * P], IDENT[:, :])
                ins.then_inc(xt_done, 1)
            mean_square(0)
            broadcast_rstd(0)
            for piece in range(4):
                pe.wait_ge(ada_acc, DB * (piece + 1))
                for m in range(4):
                    ins = mm(PS[:, 6, 4 * piece + m:4 * piece + m + 1], ACC0[:, piece, m * P:(m + 1) * P],
                             ONES[:, 0:1], start=True, stop=True)
                ins.then_inc(ada_red, 1)

            def ada_reduce(acc, mod):
                pe.wait_ge(ada_acc, acc)
                pe.wait_ge(mod_ready, mod)
                for m in range(4):
                    ins = mm(PS[:, 6, m:m + 1], ACC[:, m * P:(m + 1) * P], ONES[:, 0:1], start=True, stop=True)
                ins.then_inc(ada_red, 1)

            def ada_reduce_at(at, acc, mod):
                def go(k):
                    if k == at:
                        ada_reduce(acc, mod)
                return go

            def swiglu_in(base_n, which, count, with_ada):
                with pe.Fori(0, count) as i:
                    for half in range(2):
                        n = base_n + half
                        if half == 0:
                            pe.wait_ge(silu_done, 1 + NP * which + i)
                        else:
                            pe.wait_ge(umul_done, 1 + NP * which + i)
                        unit(n, 2 * i + n + 1, (2 * half, 2 * half + 1), HH, HL, wait_h=2 * DB * which if half == 0 else None,
                             before=ada_reduce_at(5, 5 * DB + DB * i, 4 + i) if with_ada and half == 1 else None)

            def down_pair(n0, q, value0, x_value, which, prologue=None):
                banks = (2 * q, 2 * q + 1)
                pe.wait_ge(xready, x_value)
                for piece, (kb0, nk) in enumerate(((0, 8), (8, 8), (16, FB - 16))):
                    if piece == 2:
                        pe.wait_ge(u_lo, 1 + NP * (which + 1))
                        pe.wait_ge(u_hi, NP * (which + 1))
                    unit(n0 + piece, value0 + piece, banks, UH, UL, kb0, nk, first=piece == 0, last=piece == 2)
                    if piece == 0 and prologue is not None:
                        prologue()

            swiglu_in(N_F1IN, 0, NP, True)
            pe.wait_ge(u_lo, NP)
            pe.wait_ge(u_hi, NP - 1)
            pe.wait_ge(silu_done, 1 + NP)
            with pe.Fori(0, 2) as i:
                for q in range(2):
                    n = N_F1DOWN + 3 * q
                    down_pair(n, q, 6 * i + n + 1, 8 + 4 * i + 2 * q - 2, 0,
                              (lambda: ada_reduce(DB * (NP + 5) + DB * i, NP + 4 + i)) if q == 0 else None)
            mean_square(1)
            ada_reduce(DB * (NP + 7), NP + 6)
            broadcast_rstd(1)

            def score_levels(a, g):
                p, r = prep_of(a), rows_of(a)
                bank = 4 + g % 2
                pe.wait_ge(prep, 18 * p + 6 + 4 * (g + 1))
                if g == 0 and a:
                    pe.wait_ge(evac_a, 2 * a)
                if g == 1 and a:
                    pe.wait_ge(evac_v, a)
                if g == 2:
                    pe.wait_ge(near_done, 6 * a + 2)
                for j in range(2):
                    l = 2 * g + j
                    for t in range(TT):
                        ins = mm(PS[:, bank, 256 * j + 64 * t:256 * j + 64 * t + 64],
                                 KP[r, l, t * P:(t + 1) * P], QP[r, l, 64 * t:64 * t + 64], start=True, stop=True)
                ins.then_inc(score_done, 1)

            def score_diagonal(a):
                p, r = prep_of(a), rows_of(a)
                q, k = PREPS[p]["q"], PREPS[p]["k"]
                pe.wait_ge(near_done, 6 * a + 4)
                for t in range(TT):
                    tok = slice(t * P, (t + 1) * P)
                    ins = mm(PS[:, 5, tok], k[r, tok], q[r, tok], start=True, stop=True)
                ins.then_inc(score_done, 1)

            def score_far(a):
                p, r = prep_of(a), rows_of(a)
                pe.wait_ge(prep, 18 * p + 6)
                if a:
                    pe.wait_ge(evac_a, 2 * a - 1)
                for t in range(TT):
                    mm(PS[0:64, 6, 64 * t:64 * t + 64], KL[r, t * P:t * P + 64], QU[r, t * P + 64:(t + 1) * P],
                       start=True, stop=True)
                for j in range(2):
                    ins = mm(PS[:, 6, 256 + P * j:256 + P * (j + 1)], W256[r, 2 * j * P:(2 * j + 1) * P],
                             W256[r, (2 * j + 1) * P:(2 * j + 2) * P], start=True, stop=True)
                ins.then_inc(score_done, 1)
                pe.wait_ge(near_done, 6 * a + 6)
                for j in range(2):
                    ins = mm(PS[:, 4, 256 * j:256 * (j + 1)], W512[r, j * P:(j + 1) * P], W512[r, 256:512],
                             start=True, stop=True)
                ins.then_inc(score_done, 1)

            def head_out(a):
                pe.wait_ge(mix_evac, V_NEEDS[a])
                pe.wait_ge(evac_v, a + 1)
                pe.wait_ge(evac_a, 2 * a + 2)
                if a:
                    pe.wait_ge(rs_ln, a)
                vv, hv = (VHG, a) if a < HEADS else (VGL, a - HEADS)
                for s in range(TT):
                    ins = mm(PS[:, 7, s * P:T], vv[:, s, hv * P:(hv + 1) * P], SC[:, s * T + s * P:(s + 1) * T],
                             start=s == 0, stop=s == TT - 1)
                ins.then_inc(pv_done, 1)

            def head_norm(a):
                pe.wait_ge(sq_o, a + 1)
                pe.wait_ge(og_done, a + 1)
                mm(PS[:, 7, :], ONES[:, :], norm_in(a)[0], start=True, stop=True).then_inc(n_done, 1)

            def gk_up():
                pe.wait_ge(gkw_in, 16)
                pe.wait_ge(mix_evac, mix_at["low", 0] + 1)
                pe.wait_ge(evac_a, 2 * HEADS)
                pe.wait_ge(evac_v, HEADS)
                for g in range(2):
                    ins = mm(PS[:, 4 + g, :], GKW[:, g * P:(g + 1) * P], S[0:RANK, :], start=True, stop=True)
                ins.then_inc(gk_mm, 1)

            def stages_at(step):
                if step == STAGES_AT[0][0]:
                    pe.wait_ge(sc_clear, 2)
                if step == STAGES_AT[HEADS][0]:
                    pe.wait_ge(gk_sub, 4)
                if step == GK_AT:
                    gk_up()
                for a, (near0, near1, far, o, norm) in enumerate(STAGES_AT):
                    if step == near0:
                        score_levels(a, 0)
                        score_levels(a, 1)
                    if step == near1:
                        score_levels(a, 2)
                        score_diagonal(a)
                    if step == far:
                        score_far(a)
                    if step == o:
                        head_out(a)
                    if step == norm:
                        head_norm(a)

            for j in range(len(MIX)):
                n = N_MIX + j
                kind = MIX[j][0]
                if j >= 2:
                    pe.wait_ge(mix_evac, j - 1)
                if kind in ("vh", "vg"):
                    unit_v(n, mix_banks(j), lambda k: stages_at(8 * j + k))
                else:
                    unit(n, n + 1, mix_banks(j), HH, HL, wait_h=DB if j == 0 else None,
                         width=RANK if kind == "low" else CW, before=lambda k: stages_at(8 * j + k))

            for pair in range(DB // 2):
                n = N_END + 3 * pair
                for b in range(2):
                    if pair == 0:
                        pe.wait_ge(mix_evac, len(MIX) - 1 + b)
                        unit(n + b, n + b + 1, (2 * b, 2 * b + 1), HH, HL,
                             before=lambda k: stages_at(8 * (len(MIX) + b) + k))
                    else:
                        pe.wait_ge(sig_done, 1 + 2 * pair)
                        unit(n + b, n + b + 1, (2 * b, 2 * b + 1), HH, HL)
                pe.wait_ge(y_lo, 2 * HEADS)
                pe.wait_ge(y_hi, 2 * HEADS)
                pe.wait_ge(merge, 1 + 3 * pair)
                pe.wait_ge(unit_lo, n + 3)
                whi, wlo = weights(n + 2)
                for br in range(2):
                    for k in range(HEADS):
                        for m in range(2):
                            w = slice(m * P, (m + 1) * P)
                            ins = three(PS[:, 4 + 2 * br + m, :], whi[:, HEADS * br + k, w], wlo[:, HEADS * br + k, w],
                                        YH[br][:, k, :], YL[br][:, k, :], k == 0, k == HEADS - 1)
                ins.then_inc(unit_done, 1)

            def merged(k):
                if k % 2 == 0:
                    pe.wait_ge(m_lo, 2 + k // 2)
                    pe.wait_ge(m_hi, 1 + k // 2)

            pe.wait_ge(sig_done, 9)
            with pe.Fori(0, 2) as i:
                for q in range(2):
                    n = N_OUT + q
                    pe.wait_ge(xready, 16 + 4 * i + 2 * q - 2)
                    unit(n, 2 * i + n + 1, (2 * q, 2 * q + 1), MH, ML, before=merged)
            mean_square(2)
            broadcast_rstd(2)

            swiglu_in(N_F2IN, 1, NP, False)
            pe.wait_ge(u_lo, 2 * NP)
            pe.wait_ge(u_hi, 2 * NP - 1)
            pe.wait_ge(silu_done, 1 + 2 * NP)

            def untranspose(b0):
                def go():
                    for b in (b0, b0 + 1):
                        pe.wait_ge(fin_y, b + 1)
                        if b >= 2:
                            pe.wait_ge(fin_ev, b - 1)
                        for t in range(TT):
                            ins = nc.tensor.transpose(PS[:, 4 + b % 2, t * P:(t + 1) * P],
                                                      YF[b % 2][:, t * P:(t + 1) * P], IDENT[:, :])
                        ins.then_inc(fin_t, 1)
                return go

            for i in range(2):
                for q in range(2):
                    n = N_F2DOWN + 3 * q
                    pair = 2 * i + q
                    down_pair(n, q, 6 * i + n + 1, 24 + 2 * pair - 2, 1, untranspose(2 * pair - 2) if pair else None)
            untranspose(6)()
            mean_square(3)

        @block.scalar
        def _(act):
            A = nc.scalar.activation
            chain = [0]

            def self_wait(ins):
                chain[0] += 1
                ins.then_inc(act_self, 1)
                act.wait_ge(act_self, chain[0])

            for dst, src in small[:len(small) // 2]:
                act.dma_start(dst, src).then_inc(small_in, 16)
            act.dma_start(GKW[:, :], w_gk_up[0]).then_inc(gkw_in, 16)

            def split_hi(n, raw_val, done_val=None, size=UNIT):
                act.wait_ge(raw_in[slot(n)], raw_val)
                if done_val is not None:
                    act.wait_ge(unit_done, done_val)
                A(WH[slot(n)][:, 0:size], RAW[slot(n)][:, 0:size], ACT.Copy).then_inc(unit_hi, 1)

            def down_size(piece):
                return (UNIT, UNIT, (FB - 16) * CW)[piece]

            def square(b, x_val, sq_free, ap=None):
                act.wait_ge(xready, x_val)
                act.wait_ge(sacc, sq_free)
                A(SG[:, b % 2, :], ap, ACT.Square).then_inc(sq_ready, 1)

            def norm_blocks(g):
                act.wait_ge(av_ready, g + 1)
                for b in range(DB):
                    act.wait_ge(t_ready, DB * g + b + 1)
                    if b >= 2:
                        act.wait_ge(h_lo, DB * g + b - 1)
                    a, sh = AV[:, g, b:b + 1], MOD[:, 3 * DB * g + b:3 * DB * g + b + 1]
                    A(HFULL[:, b % 2, :], TN[:, b % 2, :], ACT.Identity, bias=sh, scale=a)
                    A(HH[:, b, :], TN[:, b % 2, :], ACT.Identity, bias=sh, scale=a).then_inc(h_hi, 1)

            act.wait_ge(small_ready, 1)
            A(COND[:, :], PT[:, PC_C:PC_C + DB], ACT.Silu).then_inc(cond_ready, 1)
            act.wait_ge(lb_ready, 1)
            A(LB[:, :], LBD[:, :], ACT.Sigmoid).then_inc(cond_ready, 1)
            A(OML[:, :], LBD[:, :], ACT.Sigmoid, scale=-1.0).then_inc(cond_ready, 1)
            for b in range(DB):
                act.wait_ge(xt_done, b + 1)
                A(X[:, b, :], PS[:, b % 4, :], ACT.Copy).then_inc(xready, 1)
                square(b, b + 1, max(b, 1), X[:, b, :])
            split_hi(0, 16)
            split_hi(1, 16)
            norm_blocks(0)

            def swiglu_in(base_n, which, count, stop_split=False):
                with act.Fori(0, count) as i:
                    n = base_n
                    act.wait_ge(unit_done, 2 * i + n + 1)
                    act.wait_ge(u_lo, 1 + NP * which + i)
                    A(SG[:, :, :], PS[:, 0:2, :], ACT.Silu).then_inc(silu_done, 1)
                    split_hi(n + 2, 16 * i + raw_value(n + 2), 2 * i + n + 1)
                    split_hi(n + 3, 16 * i + raw_value(n + 3), 2 * i + n + 2)
                    act.wait_ge(umul_done, 1 + NP * which + i + 1)
                    A(UH[:, ds(2 * i, 2), :], SG[:, :, :], ACT.Copy).then_inc(u_hi, 1)

            swiglu_in(N_F1IN, 0, NP)

            def down(base_n, i, x0, sacc0, last=False, final=False):
                for q in range(2):
                    for piece in range(3):
                        n = base_n + 3 * q + piece
                        if not (last and q == 1 and piece >= 1):
                            nxt = (piece + 2) % 3
                            split_hi(n + 2, 16 * 3 * i + raw_value(n + 2), 6 * i + n + 1, down_size(nxt) if not (q == 1 and piece > 0) else UNIT)
                    for m in range(2):
                        b = 2 * q + m
                        if isinstance(i, int):
                            blk = X[:, 4 * i + b, :]
                        else:
                            blk = X[:, ds(4 * i + b, 1), :].rearrange("p a t -> p (a t)")
                        square(b, x0 + 4 * i + b + 1, sacc0 + 4 * i + b, blk)
                        if final:
                            g = 4 * i + b
                            if g >= 2:
                                act.wait_ge(fin_t, g - 1)
                            A(YF[g % 2][:, :], blk, ACT.Copy, scale=PT[:, PC_FINAL + g:PC_FINAL + g + 1]).then_inc(fin_y, 1)
                            if g >= 2:
                                final_copy(g - 2)

            def final_copy(b):
                act.wait_ge(fin_t, b + 1)
                A(OUTT[:, :, b * P:(b + 1) * P], PS[:, 4 + b % 2, :].rearrange("p (t f) -> p t f", f=P), ACT.Copy)\
                    .then_inc(fin_ev, 1)

            with act.Fori(0, 2) as i:
                down(N_F1DOWN, i, 8, 9)
            norm_blocks(1)

            tables = [""]

            def exp_ln_tables():
                if tables[0] != "exp_ln":
                    nc.scalar.preload_act_table_set("natural_log_exp_and_others")
                tables[0] = "exp_ln"

            def evacuate(j):
                if MIX[j][0] in ("hf", "hq", "gh", "gg"):
                    tables[0] = "sigmoid or silu"
                n = N_MIX + j
                kind, _, half = MIX[j]
                act.wait_ge(unit_done, n + 1)
                ps = PS[:, mix_banks(j)[0]:mix_banks(j)[0] + 2, :]
                two = slice(2 * half, 2 * half + 2)
                toks = ps.rearrange("p b (t c) -> p (b t) c", c=CW)
                if kind == "hf":
                    A(CHG[:, two, :], ps, ACT.Sigmoid)
                    A(KHG[:, two, :], ps, ACT.Sigmoid, scale=-1.0).then_inc(mix_evac, 1)
                elif kind == "hq":
                    A(QHG[:, two, :], ps, ACT.Silu).then_inc(mix_evac, 1)
                elif kind == "vh":
                    A(VHG[:, :, half * CW:(half + 1) * CW], toks, ACT.Copy).then_inc(mix_evac, 1)
                elif kind == "vg":
                    A(VGL[:, :, half * CW:(half + 1) * CW], toks, ACT.Copy).then_inc(mix_evac, 1)
                elif kind == "gh":
                    A(GO[:, two, :], ps, ACT.Silu).then_inc(mix_evac, 1)
                elif kind == "gg":
                    A(GO[:, HEADS + 2 * half:HEADS + 2 * half + 2, :], ps, ACT.Silu).then_inc(mix_evac, 1)
                elif kind == "low":
                    A(S[0:RANK, :], PS[0:RANK, mix_banks(j)[0], :], ACT.Copy).then_inc(mix_evac, 1)
                elif kind == "gk":
                    A(KGL[:, :, :], ps, ACT.Copy).then_inc(mix_evac, 1)
                elif kind == "gq":
                    A(QGL[:, :, :], ps, ACT.Copy, scale=64.0 ** -0.5).then_inc(mix_evac, 1)

            def unit_size(n):
                return DB * RANK if n == N_MIX + mix_at["low", 0] else UNIT

            def decays(p):
                exp_ln_tables()
                cc = PREPS[p]["c"]
                if p < HEADS:
                    act.wait_ge(mix_evac, PREP_NEEDS[p])
                    A(cc, cc, ACT.Ln, bias=LB[:, p:p + 1], scale=OML[:, p:p + 1]).then_inc(logf, 1)
                act.wait_ge(cum, p + 1)
                if p:
                    act.wait_ge(score_done, 6 * before_prep(p) + 6)
                A(QU[:, :], cc, ACT.Exp).then_inc(exps, 1)
                act.wait_ge(kl_diff, p + 1)
                A(KL[:, :], KL[:, :], ACT.Exp).then_inc(exps, 1)
                act.wait_ge(gtab, p + 1)
                A(FT[:, :, :], GT[:, :, :], ACT.Exp).then_inc(exps, 1)

            def near_factors(p):
                exp_ln_tables()
                act.wait_ge(diffs, 12 * p + 6)
                A(QP[:, :, :], QP[:, :, :], ACT.Exp).then_inc(exps, 1)
                for l, B in enumerate(LEVELS):
                    act.wait_ge(diffs, 12 * p + 7 + l)
                    kk = blocks(KP[:, l, :], B)[:, :, 0:B // 2]
                    A(kk, kk, ACT.Exp).then_inc(exps, 1)

            def copy_far(a):
                act.wait_ge(score_done, 6 * a + 5)
                act.wait_ge(evac_v, a + 1)
                diag = SC[:, :].rearrange("p (i x) -> p i x", x=5 * P)
                A(diag[0:64, :, 64:P], PS[0:64, 6, 0:256].rearrange("p (i x) -> p i x", x=64), ACT.Copy)
                A(SC[:, :].rearrange("p (i x) -> p i x", x=2 * T + 2 * P)[:, :, P:2 * P],
                  PS[:, 6, 256:512].rearrange("p (i x) -> p i x", x=P), ACT.Copy).then_inc(evac_a, 1)
                act.wait_ge(score_done, 6 * a + 6)
                A(SC[:, 0:2 * T].rearrange("p (i x) -> p i x", x=T)[:, :, T // 2:T],
                  PS[:, 4, :].rearrange("p (i x) -> p i x", x=T // 2), ACT.Copy).then_inc(evac_a, 1)

            def squares(a):
                act.wait_ge(pv_done, a + 1)
                A(norm_in(a)[0], PS[:, 7, :], ACT.Square).then_inc(sq_o, 1)

            def inverse_rms(a):
                exp_ln_tables()
                act.wait_ge(n_done, a + 1)
                rs = norm_in(a)[1]
                A(rs, PS[:, 7, :], ACT.Ln, bias=EPST[:, 0:1], scale=1.0 / P).then_inc(rs_ln, 1)
                act.wait_ge(rs_ln, a + 1)
                A(rs, rs, ACT.Exp, scale=-0.5).then_inc(rs_ready, 1)

            def output_hi(a):
                act.wait_ge(yf_ready, a + 1)
                A(YH[a // HEADS][:, a % HEADS, :], GO[:, a, :], ACT.Copy).then_inc(y_hi, 1)

            def decay_gla(g):
                exp_ln_tables()
                act.wait_ge(gk_mm, 1)
                if g:
                    act.wait_ge(gk_sub, 2)
                A(S[:, :], PS[:, 4 + g, :], ACT.Abs, bias=PT[:, PC_BGK + g:PC_BGK + g + 1]).then_inc(gk_abs, 1)
                act.wait_ge(gk_abs, g + 1)
                self_wait(A(S[:, :], S[:, :], ACT.Exp, scale=-1.0))
                A(S[:, :], S[:, :], ACT.Ln, bias=ONES[:, 0:1]).then_inc(gk_ln, 1)

            for step in ORDER:
                kind, j = step[0], int(step[1:])
                if kind == "E":
                    n = N_MIX + j
                    split_hi(n + 2, raw_value(n + 2), n + 1, unit_size(n + 2))
                    evacuate(j)
                elif kind == "a":
                    decays(j)
                elif kind == "b":
                    near_factors(j)
                elif kind == "A":
                    copy_far(j)
                elif kind == "Q":
                    squares(j)
                elif kind == "T":
                    inverse_rms(j)
                elif kind == "U":
                    output_hi(j)
                elif kind == "G":
                    decay_gla(j)

            with act.Fori(0, 2) as i:
                for q in range(2):
                    for b in range(2):
                        n = N_END + 3 * q + b
                        act.wait_ge(unit_done, 6 * i + n + 1)
                        act.wait_ge(m_lo, 1 + 2 * i + q)
                        A(RG[b][:, :, :], PS[:, 2 * b:2 * b + 2, :], ACT.Sigmoid).then_inc(sig_done, 1)
                        split_hi(n + 2, 64 * i + raw_value(n + 2), 6 * i + n + 1)
                    n = N_END + 3 * q + 2
                    split_hi(n + 2, 64 * i + raw_value(n + 2), 6 * i + n + 1)
                    act.wait_ge(merge, 1 + 6 * i + 3 * q + 3)
                    A(MH[:, ds(4 * i + 2 * q, 2), :], RG[0][:, :, :], ACT.Copy).then_inc(m_hi, 1)

            with act.Fori(0, 2) as i:
                for q in range(2):
                    n = N_OUT + q
                    split_hi(n + 2, 16 * i + raw_value(n + 2), 2 * i + n + 1)
                    for m in range(2):
                        b = 2 * q + m
                        square(b, 16 + 4 * i + b + 1, 18 + 4 * i + b, X[:, ds(4 * i + b, 1), :].rearrange("p a t -> p (a t)"))
            norm_blocks(2)
            swiglu_in(N_F2IN, 1, NP)
            for i in range(2):
                down(N_F2DOWN, i, 24, 27, last=i == 1, final=True)
            final_copy(6)
            final_copy(7)
            act.wait_ge(r_ready, 4)
            act.wait_ge(fin_ev, DB)
            for t in (2, 3):
                A(OUTT[:, t, :], OUTT[:, t, :], ACT.Copy, scale=R4[:, t:t + 1]).then_inc(fin_a, 1)

        @block.vector
        def _(dve):
            V = nc.vector
            chain = [0]

            def self_wait(ins):
                chain[0] += 1
                ins.then_inc(dve_self, 1)
                dve.wait_ge(dve_self, chain[0])

            def split_lo(n, value, done_val=None, size=UNIT):
                if done_val is not None:
                    dve.wait_ge(unit_done, done_val)
                dve.wait_ge(unit_hi, value)
                s = slot(n)
                V.tensor_tensor(WL[s][:, 0:size], RAW[s][:, 0:size], WH[s][:, 0:size].bitcast(F32), ALU.subtract)\
                    .then_inc(unit_lo, 1)

            def add_square(b, sq_val, acc_val):
                dve.wait_ge(sq_ready, sq_val)
                dve.wait_ge(sacc, acc_val)
                V.tensor_tensor(S[:, :], S[:, :], SG[:, b % 2, :], ALU.add).then_inc(sacc, 1)

            def clear_s():
                V.memset(S[:, :], 0.0).then_inc(sacc, 1)

            def mean_square(g):
                dve.wait_ge(ssq_done, g + 1)
                V.tensor_scalar(V4[:, :], PS[:, 7, 0:TT], 1.0 / D, EPS, ALU.mult, ALU.add).then_inc(v_ready, 1)

            def rms(g):
                mean_square(g)
                dve.wait_ge(r_ready, g + 1)
                for t in range(TT):
                    V.tensor_scalar(DG[:, t * P:(t + 1) * P], IDENT[:, :], R4[:, t:t + 1], None, ALU.mult).then_inc(dg_ready, 1)

            def normalise(g, between=None):
                dve.wait_ge(bc_done, g + 1)

                def lo(b):
                    dve.wait_ge(h_hi, DB * g + b + 1)
                    V.tensor_tensor(HL[:, b, :], HFULL[:, b % 2, :], HH[:, b, :].bitcast(F32), ALU.subtract).then_inc(h_lo, 1)

                for b in range(DB):
                    if b >= 2:
                        dve.wait_ge(h_hi, DB * g + b - 1)
                    V.tensor_tensor(TN[:, b % 2, :], X[:, b, :], PS[:, 7, :], ALU.mult).then_inc(t_ready, 1)
                    if b:
                        lo(b - 1)
                    if b == 4 and between is not None:
                        between()
                lo(DB - 1)

            def scale_vector(g):
                V.scalar_tensor_tensor(AV[:, g, :], MOD[:, 3 * DB * g + DB:3 * DB * g + 2 * DB], 1.0,
                                       PT[:, PC_GAIN + DB * g:PC_GAIN + DB * (g + 1)], ALU.add, ALU.mult).then_inc(av_ready, 1)

            dve.wait_ge(small_t, 1)
            V.tensor_copy(PT[:, :], PS[:, 5, 0:124]).then_inc(small_ready, 1)
            dve.wait_ge(small_ready, 1)
            V.tensor_tensor(LBD[:, :], PT[:, PC_LB:PC_LB + HEADS], PT[:, PC_LB + HEADS:PC_LB + 2 * HEADS],
                            ALU.subtract).then_inc(lb_ready, 1)
            dve.wait_ge(cond_ready, 3)
            V.tensor_scalar(LB[:, :], LB[:, :], LN_FLOOR, None, ALU.max).then_inc(lb_ready, 1)

            def ada_term(k, acc_tile, w, acc_val):
                if k == 0:
                    V.tensor_scalar(acc_tile, w, COND[:, 0:1], None, ALU.mult).then_inc(ada_acc, 1)
                else:
                    dve.wait_ge(ada_acc, acc_val)
                    V.scalar_tensor_tensor(acc_tile, w, COND[:, k:k + 1], acc_tile, ALU.mult, ALU.add).then_inc(ada_acc, 1)

            for piece in range(4):
                for k in range(DB):
                    if k % 4 == 0:
                        dve.wait_ge(ada0_in[2 * piece + k // 4], 16)
                    ada_term(k, ACC0[:, piece, :], ADA0[:, piece, k, :], DB * piece + k)
                if piece == 2:
                    rms(0)
            dve.wait_ge(ada_red, 4)
            V.tensor_tensor(MOD[:, 0:2 * DB], PS[:, 6, 0:2 * DB], PT[:, PC_BADA:PC_BADA + 2 * DB], ALU.add)\
                .then_inc(mod_ready, 4)
            dve.wait_ge(mod_ready, 4)
            scale_vector(0)
            split_lo(0, 1)
            normalise(0, between=lambda: split_lo(1, 2))

            def ada_piece(red_val, in_val, acc0):
                dve.wait_ge(ada_red, red_val)
                for k in range(DB):
                    j = k // 2
                    if k % 2 == 0:
                        dve.wait_ge(ada_in[j % 2], in_val + 16 * (j // 2 + 1))
                    ada_term(k, ACC[:, :], ADAW[j % 2][:, k % 2, :], acc0 + k)

            def add_ada_bias(i, piece):
                dve.wait_ge(ada_red, i + piece + 1)
                V.tensor_tensor(MOD[:, ds(4 * i + 4 * piece, 4)], PS[:, 6, 0:4], PT[:, ds(4 * i + PC_BADA + 4 * piece, 4)],
                                ALU.add).then_inc(mod_ready, 1)

            ada_piece(4, 0, 4 * DB)

            def swiglu_in(base_n, which, with_ada):
                with dve.Fori(0, NP) as i:
                    n = base_n
                    split_lo(n + 2, 2 * i + n + 3, 2 * i + n + 1)
                    if with_ada:
                        add_ada_bias(i, 4)
                        ada_piece(i + 5, 32 * i + 32, DB * i + 5 * DB)
                    dve.wait_ge(silu_done, 1 + NP * which + i + 1)
                    dve.wait_ge(unit_done, 2 * i + n + 2)
                    V.tensor_tensor(SG[:, :, :], SG[:, :, :], PS[:, 2:4, :], ALU.mult).then_inc(umul_done, 1)
                    split_lo(n + 3, 2 * i + n + 4, 2 * i + n + 2)
                    dve.wait_ge(u_hi, NP * which + i + 1)
                    V.tensor_tensor(UL[:, ds(2 * i, 2), :], SG[:, :, :], UH[:, ds(2 * i, 2), :].bitcast(F32),
                                    ALU.subtract).then_inc(u_lo, 1)

            swiglu_in(N_F1IN, 0, True)

            def add_to_x(i, b, bank, gate, x_val=None):
                if isinstance(i, int):
                    xb, gg = X[:, 4 * i + b, :], GATE[:, gate, 4 * i + b:4 * i + b + 1]
                else:
                    xb = X[:, ds(4 * i + b, 1), :].rearrange("p a t -> p (a t)")
                    gg = GATE[:, gate, ds(4 * i + b, 1)]
                V.scalar_tensor_tensor(xb, PS[:, bank, :], gg, xb, ALU.mult, ALU.add).then_inc(xready, 1)

            def down(base_n, i, gate, sq0, sacc0, last=False, ada=False):
                for q in range(2):
                    for piece in range(3):
                        n = base_n + 3 * q + piece
                        if piece == 2:
                            dve.wait_ge(unit_done, 6 * i + n + 1)
                            for m in range(2):
                                add_to_x(i, 2 * q + m, 2 * q + m, gate)
                        if not (last and q == 1 and piece >= 1):
                            nxt = (piece + 2) % 3
                            size = (FB - 16) * CW if nxt == 2 and not (q == 1 and piece > 0) else UNIT
                            split_lo(n + 2, 6 * i + n + 3, 6 * i + n + 1, size)
                        if ada and q == 0 and piece == 1:
                            add_ada_bias(i, NP + 4)
                            ada_piece(i + NP + 5, 32 * i + 32 * (NP + 1), DB * i + DB * (NP + 5))
                    for m in range(2):
                        b = 2 * q + m
                        add_square(b, sq0 + 4 * i + b + 1, sacc0 + 4 * i + b)
            dve.wait_ge(mod_ready, 6)
            self_wait(V.tensor_scalar(GATE[:, 0, :], MOD[:, 2 * DB:3 * DB], 0.5, None, ALU.mult))
            clear_s()
            with dve.Fori(0, 2) as i:
                down(N_F1DOWN, i, 0, 8, 10, ada=True)

            rms(1)
            scale_vector(1)
            normalise(1)
            dve.wait_ge(ada_red, NP + 7)
            V.tensor_tensor(MOD[:, 8 * DB + 4:9 * DB], PS[:, 6, 0:4], PT[:, PC_BADA + 8 * DB + 4:PC_BADA + 9 * DB],
                            ALU.add).then_inc(mod_ready, 1)
            dve.wait_ge(mod_ready, NP + 7)
            V.tensor_copy(GATE[:, 1, :], MOD[:, 5 * DB:6 * DB])
            self_wait(V.tensor_scalar(GATE[:, 2, :], MOD[:, 8 * DB:9 * DB], 0.5, None, ALU.mult))

            def decays(p):
                k, cc = PREPS[p]["k"], PREPS[p]["c"]
                if p < HEADS:
                    dve.wait_ge(mix_evac, PREP_NEEDS[p])
                    V.tensor_scalar(k, k, OML[:, p:p + 1], None, ALU.mult)
                    dve.wait_ge(logf, p + 1)
                V.tensor_tensor_scan(cc, RST[:, :], cc, 0.0, ALU.mult, ALU.add).then_inc(cum, 1)
                dve.wait_ge(cum, p + 1)
                tot = blocks(cc, CHUNK)[:, :, CHUNK - 1:CHUNK]
                if p:
                    dve.wait_ge(score_done, 6 * before_prep(p) + 6)
                V.tensor_tensor(blocks(KL[:, :], CHUNK), tot.to_broadcast([P, NC, CHUNK]), blocks(cc, CHUNK),
                                ALU.subtract).then_inc(kl_diff, 1)
                t1 = cc.rearrange("p (n b) -> p n b", b=CHUNK)[:, :, CHUNK - 1]
                if p:
                    dve.wait_ge(exps, 10 * p - 7)
                V.tensor_copy(GT[:, 0, 0:5:4], t1[:, 1:6:4])
                V.tensor_copy(GT[:, 0, 3:8:4], t1[:, 2:7:4])
                V.tensor_copy(GT[:, 1, 2:6:3], t1[:, 3:5])
                self_wait(V.tensor_tensor(GT[:, 1, 1:7:5], t1[:, 2:6:3], t1[:, 3:5], ALU.add))
                V.tensor_tensor(GT[:, 1, 0:8:7], GT[:, 1, 1:7:5], t1[:, 1:7:5], ALU.add).then_inc(gtab, 1)

            def decayed(p):
                q, k = PREPS[p]["q"], PREPS[p]["k"]
                dve.wait_ge(mix_evac, PREP_NEEDS[p])
                dve.wait_ge(exps, 10 * p + 2)
                V.tensor_tensor(QU[:, :], QU[:, :], q, ALU.mult).then_inc(prep, 1)
                V.tensor_tensor(KL[:, :], KL[:, :], k, ALU.mult).then_inc(prep, 1)
                dve.wait_ge(exps, 10 * p + 3)
                dve.wait_ge(prep, 18 * p + 2)
                for src, c0 in ((KL, 0), (QU, 2)):
                    for j in range(2):
                        cs = slice(4 * j + c0, 4 * j + c0 + 2)
                        ins = V.tensor_tensor(blocks(W256[:, :], CHUNK)[:, cs, :], blocks(src[:, :], CHUNK)[:, cs, :],
                                              FT[:, 0, cs].unsqueeze(2).to_broadcast([P, 2, CHUNK]), ALU.mult)
                    ins.then_inc(prep, 1)
                for src, c0 in ((KL, 0), (QU, 4)):
                    cs = slice(c0, c0 + 4)
                    V.tensor_tensor(blocks(W512[:, :], CHUNK)[:, cs, :], blocks(src[:, :], CHUNK)[:, cs, :],
                                    FT[:, 1, cs].unsqueeze(2).to_broadcast([P, 4, CHUNK]), ALU.mult).then_inc(prep, 1)
                for l, B in enumerate(LEVELS):
                    h = B // 2
                    dve.wait_ge(exps, 10 * p + 4)
                    qp = QP[:, l, :].rearrange("p (n h) -> p n h", h=h)
                    V.tensor_tensor(qp, qp, blocks(q, B)[:, :, h:B], ALU.mult).then_inc(prep, 1)
                    dve.wait_ge(exps, 10 * p + 5 + l)
                    kp = blocks(KP[:, l, :], B)[:, :, 0:h]
                    V.tensor_tensor(kp, kp, blocks(k, B)[:, :, 0:h], ALU.mult).then_inc(prep, 1)

            diag = SC[:, :].rearrange("p (i x) -> p i x", x=5 * P)[:, :, 0:P]

            def copy_near(a):
                for g in range(3):
                    dve.wait_ge(score_done, 6 * a + g + 1)
                    for j in range(2):
                        l = 2 * g + j
                        h = LEVELS[l] // 2
                        near = diag.rearrange("p i (n b) -> p i n b", b=2 * h)[:, :, :, h:2 * h]
                        ps = PS[:, 4 + g % 2, 256 * j:256 * (j + 1)].rearrange("p (i n h) -> p i n h", i=TT, h=h)
                        m = MASK[:, l, :].rearrange("p (n h) -> p n h", h=h).unsqueeze(1).to_broadcast([P, TT, 64 // h, h])
                        if l:
                            dve.wait_ge(near_done, 6 * a + l)
                        ins = V.copy_predicated(near, m, ps).then_inc(near_done, 1)
                dve.wait_ge(score_done, 6 * a + 4)
                dve.wait_ge(near_done, 6 * a + 6)
                V.copy_predicated(diag, MASKD[:, :].unsqueeze(1).to_broadcast([P, TT, P]),
                                  PS[:, 5, :].rearrange("p (i x) -> p i x", x=P)).then_inc(evac_v, 1)

            def gate_out(a):
                dve.wait_ge(sq_o, a + 1)
                dve.wait_ge(mix_evac, G_NEEDS[a])
                V.tensor_tensor(GO[:, a, :], GO[:, a, :], PS[:, 7, :], ALU.mult).then_inc(og_done, 1)

            def finish(a):
                gain = PT[:, PC_HGN:PC_HGN + 1] if a < HEADS else PT[:, PC_GLN:PC_GLN + 1]
                dve.wait_ge(og_done, a + 1)
                dve.wait_ge(rs_ready, a + 1)
                V.scalar_tensor_tensor(GO[:, a, :], GO[:, a, :], gain, norm_in(a)[1], ALU.mult, ALU.mult).then_inc(yf_ready, 1)

            def output_lo(a):
                dve.wait_ge(y_hi, a + 1)
                V.tensor_tensor(YL[a // HEADS][:, a % HEADS, :], GO[:, a, :], YH[a // HEADS][:, a % HEADS, :].bitcast(F32),
                                ALU.subtract).then_inc(y_lo, 1)

            def decay_gla(g):
                cc = CGL[:, g, :]
                dve.wait_ge(gk_abs, g + 1)
                V.tensor_scalar(cc, PS[:, 4 + g, :], PT[:, PC_BGK + g:PC_BGK + g + 1], 0.0, ALU.add, ALU.min).then_inc(gk_sub, 1)
                dve.wait_ge(gk_sub, 2 * g + 1)
                dve.wait_ge(gk_ln, g + 1)
                V.tensor_tensor(cc, cc, S[:, :], ALU.subtract).then_inc(gk_sub, 1)
                dve.wait_ge(gk_sub, 2 * g + 2)
                self_wait(V.tensor_scalar(cc, cc, 1.0 / 16.0, None, ALU.mult))

            for step in ORDER:
                kind, j = step[0], int(step[1:])
                if kind == "E":
                    n = N_MIX + j
                    size = DB * RANK if n + 2 == N_MIX + mix_at["low", 0] else UNIT
                    split_lo(n + 2, n + 3, n + 1, size)
                elif kind == "a":
                    decays(j)
                elif kind == "b":
                    decayed(j)
                elif kind == "V":
                    if j == 0:
                        dve.wait_ge(consts, 33)
                    copy_near(j)
                elif kind == "Q":
                    gate_out(j)
                elif kind == "T":
                    finish(j)
                elif kind == "U":
                    output_lo(j)
                elif kind == "G":
                    decay_gla(j)

            with dve.Fori(0, 2) as i:
                for q in range(2):
                    for b in range(3):
                        n = N_END + 3 * q + b
                        if b == 2:
                            dve.wait_ge(unit_done, 6 * i + n + 1)
                            dve.wait_ge(sig_done, 1 + 4 * i + 2 * q + 2)
                            for br in range(2):
                                V.tensor_tensor(RG[br][:, :, :], RG[br][:, :, :], PS[:, 4 + 2 * br:6 + 2 * br, :],
                                                ALU.mult).then_inc(merge, 1)
                            dve.wait_ge(merge, 1 + 6 * i + 3 * q + 2)
                            V.tensor_tensor(RG[0][:, :, :], RG[0][:, :, :], RG[1][:, :, :], ALU.add).then_inc(merge, 1)
                        split_lo(n + 2, 6 * i + n + 3, 6 * i + n + 1)
                    dve.wait_ge(m_hi, 2 * i + q + 1)
                    V.tensor_tensor(ML[:, ds(4 * i + 2 * q, 2), :], RG[0][:, :, :],
                                    MH[:, ds(4 * i + 2 * q, 2), :].bitcast(F32), ALU.subtract).then_inc(m_lo, 1)

            clear_s()
            with dve.Fori(0, 2) as i:
                for q in range(2):
                    n = N_OUT + q
                    dve.wait_ge(unit_done, 2 * i + n + 1)
                    for m in range(2):
                        add_to_x(i, 2 * q + m, 2 * q + m, 1)
                    split_lo(n + 2, 2 * i + n + 3, 2 * i + n + 1)
                    for m in range(2):
                        b = 2 * q + m
                        add_square(b, 16 + 4 * i + b + 1, 19 + 4 * i + b)
            rms(2)
            scale_vector(2)
            normalise(2)
            swiglu_in(N_F2IN, 1, False)
            clear_s()
            for i in range(2):
                down(N_F2DOWN, i, 2, 24, 28, last=i == 1)
            mean_square(3)
            dve.wait_ge(r_ready, 4)
            dve.wait_ge(fin_ev, DB)
            for t in (0, 1):
                V.tensor_scalar(OUTT[:, t, :], OUTT[:, t, :], R4[:, t:t + 1], None, ALU.mult).then_inc(fin_v, 1)


def arena_offset(nc, arena):
    size = arena.shape[1] * 4
    return (nc.sbuf_base - size) // 32 * 32


_INS = ["x", "c", "w_ada", "b_ada", "norm_gains", "ffn1_w_in", "ffn1_w_down", "w_in_mix", "w_gk_up", "b_gk_up",
        "lb_logits", "hg_norm", "gla_norm", "w_up_hg", "w_up_gla", "w_out", "ffn2_w_in", "ffn2_w_down", "final_norm"]


def kernel(**inputs):
    import numpy as _np
    import concourse.bacc as _bacc
    from concourse import mybir as _mybir
    from concourse.bass_utils import run_bass_kernel_spmd as _run

    nc = _bacc.Bacc("TRN2", target_bir_lowering=False, num_devices=1)
    arrays, args = {}, []
    for name in _INS:
        a = _np.ascontiguousarray(inputs[name])
        arrays[f"in_{name}_dram"] = a
        args.append(nc.dram_tensor(f"in_{name}_dram", a.shape, _mybir.dt.from_np(a.dtype), kind="ExternalInput").ap())
    args.append(nc.dram_tensor("out_0_dram", inputs["x"].shape, _mybir.dt.float32, kind="ExternalOutput").ap())
    trunk_program(nc, *args)
    r = _run(nc, [arrays], core_ids=[0])
    return r.results[0]["out_0_dram"]
```

```python
from contextlib import ExitStack

import concourse.bass as bass
from concourse import mybir


def trunk_program(nc, x, c, w_ada, b_ada, norm_gains, ffn1_w_in, ffn1_w_down, w_in_mix, w_gk_up, b_gk_up,
                  lb_logits, hg_norm, gla_norm, w_up_hg, w_up_gla, w_out, ffn2_w_in, ffn2_w_down,
                  final_norm, out):
    F32, F32R, BF16, I8 = mybir.dt.float32, mybir.dt.float32r, mybir.dt.bfloat16, mybir.dt.int8
    ACT, ALU = mybir.ActivationFunctionType, mybir.AluOpType
    ds = bass.ds

    P = 128
    T = x.shape[1]
    D = x.shape[2]
    DB = D // P
    TT = T // P
    FF = ffn1_w_down.shape[1]
    FB = FF // P
    CW = 256
    NP = FF // CW
    CHUNK = 64
    NC = T // CHUNK
    HEADS = 4
    EPS = 1e-6
    UNIT = DB * CW
    AW = 512
    LN_FLOOR = 2.0 ** -63

    xv = x[0]
    ada = w_ada[0]
    widths = (512, 512, 512, 512, 256, 256, 512, 512, 16, D, D)
    at = [sum(widths[:i]) for i in range(len(widths))]
    HQ, HF, HI, HG, GQ, GK, GV, GG, GLOW, RHG, RGLA = at

    N_F1IN = 0
    N_F1DOWN = N_F1IN + 2 * NP
    N_MIX = N_F1DOWN + 12
    MIX = [("hf", HF, 0), ("hq", HQ, 0), ("vh", HI, 0), ("gh", HG, 0), ("hf", HF, 1), ("hq", HQ, 1),
           ("vh", HI, 1), ("gh", HG, 1), ("low", GLOW, 0), ("gk", GK, 0), ("gq", GQ, 0), ("vg", GV, 0),
           ("gg", GG, 0), ("vg", GV, 1), ("gg", GG, 1)]
    N_END = N_MIX + len(MIX)
    N_OUT = N_END + 12
    N_F2IN = N_OUT + 4
    N_F2DOWN = N_F2IN + 2 * NP
    mix_at = {}
    for j, (kind, _, half) in enumerate(MIX):
        mix_at[kind, half] = j
    RANK = 16

    ctx = ExitStack()
    with ctx:
        def sb(name, shape, dt=F32):
            return ctx.enter_context(nc.sbuf_tensor(name, shape, dt))

        def sem(name):
            return ctx.enter_context(nc.semaphore(name))

        X = sb("X", [P, DB, T])
        RAW = [sb(f"RAW{s}", [P, UNIT]) for s in range(2)]
        WH = [sb(f"WH{s}", [P, UNIT], F32R) for s in range(2)]
        WL = [sb(f"WL{s}", [P, UNIT], F32R) for s in range(2)]
        S = sb("S", [P, T])
        PT = sb("PT", [P, 124])
        PST = sb("PST", [124, P])
        MOD = sb("MOD", [P, 9 * DB])
        AV = sb("AV", [P, 4, DB])
        GATE = sb("GATE", [P, 3, DB])
        COND = sb("COND", [P, DB])
        IDENT = sb("IDENT", [P, P])
        ONES = sb("ONES", [P, P])
        MASKF = sb("MASKF", [P, 64])
        MASK = sb("MASK", [P, 6, 64], I8)
        MASKD = sb("MASKD", [P, P], I8)
        RST = sb("RST", [P, T], BF16)
        V4 = sb("V4", [P, TT])
        R4 = sb("R4", [P, TT])
        HALF4 = sb("HALF4", [P, TT])
        EPST = sb("EPST", [P, 1])
        LB = sb("LB", [P, HEADS])
        OML = sb("OML", [P, HEADS])
        LBD = sb("LBD", [P, HEADS])
        GT = sb("GT", [P, 2, NC])
        FT = sb("FT", [P, 2, NC])
        GKW = sb("GKW", [RANK, 256])

        H_BYTES = DB * T * 4
        ARENA = 106496
        arena = sb("arena", [P, (ARENA + 2 * H_BYTES) // 4])
        base = arena_offset(nc, arena)

        def place(name, shape, offset, dt=F32):
            return nc.alloc_sbuf_tensor_at(name, shape, dt, offset=base + offset)

        HO = ARENA
        HH = place("HH", [P, DB, T], HO, F32R)
        HL = place("HL", [P, DB, T], HO + H_BYTES, F32R)
        OUTT = place("OUTT", [P, TT, D], HO)
        UH = place("UH", [P, FB, T], 0, F32R)
        UL = place("UL", [P, FB, T], FB * T * 4, F32R)
        NT = 2 * FB * T * 4 - 8192
        TN = place("TN", [P, 2, T], NT)
        HFULL = place("HFULL", [P, 2, T], NT + 4096)
        SG = place("SG", [P, 2, T], 2 * FB * T * 4)
        RMS = place("RMS", [P, T], 2 * FB * T * 4)
        ADAW = [place(f"ADAW{s}", [P, 2, AW], 94208 + 4096 * s) for s in range(2)]
        YF = [place(f"YF{s}", [P, T], 94208 + 2048 * s) for s in range(2)]
        ACC = place("ACC", [P, AW], 102400)
        ADA0 = place("ADA0", [P, 2, DB, 2 * AW], 0)
        XST = place("XST", [P, TT, D], 65536)
        ACC0 = place("ACC0", [P, 4, AW], HO + 2 * H_BYTES - 4 * AW * 4)
        QHG = place("QHG", [P, HEADS, T], 0)
        KHG = place("KHG", [P, HEADS, T], 8192)
        CHG = place("CHG", [P, HEADS, T], 16384)
        VHG = place("VHG", [P, TT, 512], 24576)
        QGL = place("QGL", [P, 2, T], 32768)
        KGL = place("KGL", [P, 2, T], 36864)
        CGL = place("CGL", [P, 2, T], 40960)
        VGL = place("VGL", [P, TT, 512], 45056)
        GO = place("GO", [P, 2 * HEADS, T], 53248)
        KP = place("KP", [P, 6, T], 69632)
        SC = place("SC", [P, TT * 640], 81920)
        QP = place("QP", [P, 6, T // 2], 92160)
        QU = place("QU", [P, T], 98304)
        KL = place("KL", [P, T], 100352)
        W256 = place("W256", [P, T], 102400)
        W512 = place("W512", [P, T], 104448)
        YH = [place("YHh", [P, HEADS, T], 8192, F32R), place("YHg", [P, HEADS, T], 0, F32R)]
        YL = [place("YLh", [P, HEADS, T], 16384, F32R), place("YLg", [P, HEADS, T], 24576, F32R)]
        MH = place("MH", [P, DB, T], 53248, F32R)
        ML = place("ML", [P, DB, T], 69632, F32R)
        RG = [place(f"RG{s}", [P, 2, T], 86016 + 4096 * s) for s in range(2)]

        PS = ctx.enter_context(nc.psum_tensor("PS", [P, 8, 512], F32))

        PC_C, PC_BADA, PC_GAIN, PC_FINAL, PC_HGN, PC_GLN, PC_BGK, PC_LB = 0, 8, 80, 104, 112, 113, 114, 116

        raw_in = [sem("raw_in0"), sem("raw_in1")]
        unit_hi = sem("unit_hi")
        unit_lo = sem("unit_lo")
        unit_done = sem("unit_done")
        unit_half = sem("unit_half")
        small_in, x_in, gkw_in = sem("small_in"), sem("x_in"), sem("gkw_in")
        ada0_in = [sem(f"ada0_in{j}") for j in range(8)]
        consts = sem("consts")
        small_t, small_ready = sem("small_t"), sem("small_ready")
        cond_ready, lb_ready = sem("cond_ready"), sem("lb_ready")
        xt_done = sem("xt_done")
        ada_in = [sem(f"ada_in{s}") for s in range(2)]
        ada_acc = sem("ada_acc")
        ada_red = sem("ada_red")
        mod_ready = sem("mod_ready")
        xready = sem("xready")
        sq_ready, sacc = sem("sq_ready"), sem("sacc")
        ssq_done = sem("ssq_done")
        x_ln, x_rms = sem("x_ln"), sem("x_rms")
        v_ready, r_ready = sem("v_ready"), sem("r_ready")
        av_ready, t_ready = sem("av_ready"), sem("t_ready")
        h_hi, h_lo = sem("h_hi"), sem("h_lo")
        silu_done, umul_done = sem("silu_done"), sem("umul_done")
        u_hi, u_lo = sem("u_hi"), sem("u_lo")
        mix_evac = sem("mix_evac")
        sc_clear = sem("sc_clear")
        gk_mm, gk_abs, gk_ln = sem("gk_mm"), sem("gk_abs"), sem("gk_ln")
        gk_sub = sem("gk_sub")
        logf, cum = sem("logf"), sem("cum")
        diffs, kl_diff = sem("diffs"), sem("kl_diff")
        gtab = sem("gtab")
        exps, prep = sem("exps"), sem("prep")
        score_done = sem("score_done")
        near_done, evac_v = sem("near_done"), sem("evac_v")
        evac_a = sem("evac_a")
        pv_done = sem("pv_done")
        sq_o, og_done = sem("sq_o"), sem("og_done")
        n_done, rs_ln, rs_ready = sem("n_done"), sem("rs_ln"), sem("rs_ready")
        yf_ready, y_hi, y_lo = sem("yf_ready"), sem("y_hi"), sem("y_lo")
        sig_done, merge = sem("sig_done"), sem("merge")
        m_hi, m_lo = sem("m_hi"), sem("m_lo")
        fin_y, fin_t, fin_ev = sem("fin_y"), sem("fin_t"), sem("fin_ev")
        fin_v, fin_a = sem("fin_v"), sem("fin_a")
        out_dma = sem("out_dma")
        dve_self, act_self = sem("dve_self"), sem("act_self")

        LEVELS = [64, 32, 16, 8, 4, 2]

        def slot(n):
            return n % 2

        def raw_value(n):
            ups = sum(1 for q in range(4) if N_END + 3 * q + 2 <= n and slot(N_END + 3 * q + 2) == slot(n))
            return 16 * (n // 2 + 1 + ups)

        def blocks(ap, size):
            return ap.rearrange("p (n b) -> p n b", b=size)

        PREPS = [dict(q=QHG[:, h, :], k=KHG[:, h, :], c=CHG[:, h, :]) for h in range(HEADS)] + \
                [dict(q=QGL[:, g, :], k=KGL[:, g, :], c=CGL[:, g, :]) for g in range(2)]
        PREP_NEEDS = [2, 2, 6, 6, 11, 11]
        V_NEEDS = [3, 3, 7, 7, 12, 12, 14, 14]
        G_NEEDS = [4, 4, 8, 8, 13, 13, 15, 15]

        def prep_of(a):
            return a if a < HEADS else HEADS + (a - HEADS) // 2

        def rows_of(a):
            return slice(0, P) if a < HEADS else slice(64 * (a % 2), 64 * (a % 2) + 64)

        def before_prep(p):
            return {1: 0, 2: 1, 3: 2, 4: 3, 5: 5}[p]

        def norm_in(a):
            if a < HEADS:
                return CHG[:, a, :], KHG[:, a, :]
            return QHG[:, a - HEADS, :], VHG[:, a - HEADS, :]

        STAGES_AT = [(29, 30, 31, 32, 34, 39), (41, 43, 45, 46, 48, 51), (60, 61, 62, 63, 65, 70),
                     (78, 79, 81, 84, 86, 89), (97, 98, 99, 100, 103, 110), (104, 105, 106, 107, 113, 118),
                     (115, 116, 118, 119, 121, 125), (122, 123, 124, 126, 128, 131)]
        GK_AT = 80
        ORDER = ("E0 E1 a0 b0 E2 V0 A0 E3 a1 Q0 b1 T0 E4 U0 V1 A1 Q1 E5 T1 a2 U1 b2 E6 V2 A2 E7 Q2 a3 T2 b3 U2 E8 "
                 "V3 G0 G1 A3 E9 Q3 a4 T3 E10 b4 U3 V4 A4 E11 E12 Q4 V5 A5 a5 T4 b5 U4 Q5 E13 V6 T5 A6 U5 E14 Q6 "
                 "V7 T6 A7 U6 S0 Q7 T7 U7").split()

        def mix_banks(j):
            return (2, 3) if j % 2 == 0 else (0, 1)

        small, row = [], 0
        for src in (c.rearrange("a (n p) -> (a n) p", p=P), b_ada.rearrange("a (n p) -> (a n) p", p=P),
                    norm_gains[0].rearrange("g (n p) -> (g n) p", p=P), final_norm.rearrange("(n p) -> n p", p=P),
                    hg_norm, gla_norm, b_gk_up.rearrange("a (n p) -> (a n) p", p=P),
                    lb_logits.rearrange("a (n p) -> (a n) p", p=P)):
            small.append((PST[row:row + src.shape[0], :], src))
            row += src.shape[0]

        block = ctx.enter_context(nc.Block())

        @block.sync
        def _(sp):
            def load(n, nslot, dst_cols, src, wait=None):
                if wait is not None:
                    sp.wait_ge(unit_lo, wait)
                sp.dma_start(dst_cols, src).then_inc(raw_in[nslot], 16)

            def cols(w, col, kb0=0, nk=DB, width=CW):
                return w.rearrange("(k p) n -> p k n", p=P)[:, kb0:kb0 + nk, col] if not isinstance(col, int) \
                    else w.rearrange("(k p) n -> p k n", p=P)[:, kb0:kb0 + nk, col:col + width]

            def raw(n, nk=DB, width=CW):
                return RAW[slot(n)][:, 0:nk * width].rearrange("p (k c) -> p k c", c=width)

            for t in range(TT):
                sp.dma_start(XST[:, t, :], xv[t * P:(t + 1) * P, :]).then_inc(x_in, 16)
            for dst, src in small[len(small) // 2:]:
                sp.dma_start(dst, src).then_inc(small_in, 16)
            ada_rows = ada.rearrange("(k p) n -> p k n", p=P)
            for pair in range(2):
                for j in range(DB // 2):
                    sp.dma_start(ADA0[:, pair, 2 * j:2 * j + 2, :],
                                 ada_rows[:, 2 * j:2 * j + 2, 2 * AW * pair:2 * AW * (pair + 1)])\
                        .then_inc(ada0_in[4 * pair + j], 16)

            def load_ada(acc, col):
                for j in range(4):
                    sp.wait_ge(ada_acc, acc + 2 * j - 2)
                    sp.dma_start(ADAW[j % 2][:, :, :], ada_rows[:, 2 * j:2 * j + 2, col]).then_inc(ada_in[j % 2], 16)

            w1 = ffn1_w_in[0]
            load(0, 0, raw(0), cols(w1, 0))
            load(1, 1, raw(1), cols(w1, FF))
            load_ada(4 * DB, slice(4 * AW, 5 * AW))

            def load_down(base_n, i, w):
                for q in range(2):
                    for piece, (kb0, nk) in enumerate(((0, 8), (8, 8), (16, FB - 16))):
                        n = base_n + 3 * q + piece
                        load(n, slot(n), raw(n, nk), cols(w, ds(2 * CW * i + q * CW, CW), kb0, nk), 6 * i + n - 1)

            with sp.Fori(0, NP - 1) as i:
                load(2, 0, raw(2), cols(w1, ds(CW * i + CW, CW)), 2 * i + 1)
                load(3, 1, raw(3), cols(w1, ds(CW * i + CW + FF, CW)), 2 * i + 2)
                load_ada(5 * DB + DB * i, ds(AW * i + 5 * AW, AW))

            for j in range(12):
                n = N_F1DOWN + j
                kb0, nk = ((0, 8), (8, 8), (16, FB - 16))[j % 3]
                load(n, slot(n), raw(n, nk), cols(ffn1_w_down[0], j // 3 * CW, kb0, nk), n - 1)
                if j in (1, 5, 11):
                    piece = NP + 4 + (1, 5, 11).index(j)
                    load_ada(DB * piece, slice(piece * AW, (piece + 1) * AW))

            wm = w_in_mix[0]
            for j, (kind, col, half) in enumerate(MIX):
                n = N_MIX + j
                width = RANK if kind == "low" else CW
                load(n, slot(n), raw(n, DB, width), cols(wm, col + half * CW, width=width), n - 1)

            with sp.Fori(0, 2) as i:
                for q in range(2):
                    n = N_END + 3 * q
                    load(n, slot(n), raw(n), cols(wm, ds(RHG + 2 * CW * i + CW * q, CW)), 6 * i + n - 1)
                    load(n + 1, slot(n + 1), raw(n + 1), cols(wm, ds(RGLA + 2 * CW * i + CW * q, CW)), 6 * i + n)
                    up = raw(n + 2)
                    sp.wait_ge(unit_lo, 6 * i + n + 1)
                    sp.dma_start(up[:, 0:4, :], cols(w_up_hg[0], ds((i + i) * CW + CW * q, CW), 0, 4)).then_inc(raw_in[slot(n)], 16)
                    sp.dma_start(up[:, 4:8, :], cols(w_up_gla[0], ds(2 * CW * i + CW * q, CW), 0, 4)).then_inc(raw_in[slot(n)], 16)
            with sp.Fori(0, 2) as i:
                for q in range(2):
                    n = N_OUT + q
                    load(n, slot(n), raw(n), cols(w_out[0], ds(2 * CW * i + CW * q, CW)), 2 * i + n - 1)
            w2 = ffn2_w_in[0]
            with sp.Fori(0, NP) as i:
                load(N_F2IN, slot(N_F2IN), raw(N_F2IN), cols(w2, ds(CW * i, CW)), 2 * i + N_F2IN - 1)
                load(N_F2IN + 1, slot(N_F2IN + 1), raw(N_F2IN + 1), cols(w2, ds(CW * i + FF, CW)), 2 * i + N_F2IN)
            with sp.Fori(0, 2) as i:
                load_down(N_F2DOWN, i, ffn2_w_down[0])
            for t in range(TT):
                sp.wait_ge(fin_v if t < 2 else fin_a, t % 2 + 1)
                sp.dma_start(out[0, t * P:(t + 1) * P, :], OUTT[:, t, :]).then_inc(out_dma, 16)
            sp.wait_ge(out_dma, 16 * TT)

        @block.gpsimd
        def _(pool):
            for counted in (silu_done, umul_done, u_lo, sig_done, merge, m_lo):
                pool.sem_inc(counted, 1)
            cn = [0]

            def done(ins):
                cn[0] += 1
                ins.then_inc(consts, 1)

            done(nc.gpsimd.memset(ONES[:, :], 1.0))
            done(nc.gpsimd.memset(IDENT[:, :], 0.0))
            done(nc.gpsimd.memset(HALF4[:, :], -0.5))
            done(nc.gpsimd.memset(EPST[:, :], EPS))
            done(nc.gpsimd.memset(GT[:, :, :], 0.0))
            done(nc.gpsimd.memset(RST[:, :], 1.0))
            pool.wait_ge(consts, cn[0])
            done(nc.gpsimd.affine_select(out=IDENT[:, :], in_=IDENT[:, :], compare_op=ALU.not_equal, fill=1.0,
                                         base=0, pattern=[[-1, P]], channel_multiplier=1))
            pool.wait_ge(consts, cn[0])
            done(nc.gpsimd.tensor_copy(MASKD[:, :], IDENT[:, :]))
            done(nc.gpsimd.memset(blocks(RST[:, :], CHUNK)[:, :, 0], 0.0))
            nc.gpsimd.memset(S[:, :], 0.0).then_inc(sacc, 1)
            for b in range(DB):
                pool.wait_ge(sq_ready, b + 1)
                pool.wait_ge(sacc, b + 1)
                nc.gpsimd.tensor_tensor(S[:, :], S[:, :], SG[:, b % 2, :], ALU.add).then_inc(sacc, 1)
            for l, B in enumerate(LEVELS):
                h, nb = B // 2, P // B
                done(nc.gpsimd.memset(MASKF[:, :], 1.0))
                pool.wait_ge(consts, cn[0])
                m = MASKF[:, :].rearrange("p (n h) -> p n h", h=h)
                done(nc.gpsimd.affine_select(out=m, in_=m, compare_op=ALU.is_ge, fill=0.0, base=0,
                                             pattern=[[-B, nb], [0, h]], channel_multiplier=1))
                pool.wait_ge(consts, cn[0])
                done(nc.gpsimd.affine_select(out=m, in_=m, compare_op=ALU.is_ge, fill=0.0, base=h - 1,
                                             pattern=[[B, nb], [0, h]], channel_multiplier=-1))
                pool.wait_ge(consts, cn[0])
                done(nc.gpsimd.tensor_copy(MASK[:, l, :], MASKF[:, :]))
                pool.wait_ge(consts, cn[0])

            pool.wait_ge(h_lo, 2 * DB)
            nc.gpsimd.memset(SC[:, :], 0.0).then_inc(sc_clear, 1)
            nc.gpsimd.memset(KP[:, :, :], 0.0).then_inc(sc_clear, 1)
            pool.wait_ge(sc_clear, 2)
            for p in range(6):
                cc = PREPS[p]["c"]
                pool.wait_ge(cum, p + 1)
                if p:
                    pool.wait_ge(score_done, 6 * before_prep(p) + 3)
                for l, B in enumerate(LEVELS):
                    h = B // 2
                    cb = blocks(cc, B)
                    mid = cb[:, :, h - 1:h].to_broadcast([P, T // B, h])
                    nc.gpsimd.tensor_tensor(QP[:, l, :].rearrange("p (n h) -> p n h", h=h), cb[:, :, h:B], mid,
                                            ALU.subtract).then_inc(diffs, 1)
                for l, B in enumerate(LEVELS):
                    h = B // 2
                    cb = blocks(cc, B)
                    mid = cb[:, :, h - 1:h].to_broadcast([P, T // B, h])
                    nc.gpsimd.tensor_tensor(blocks(KP[:, l, :], B)[:, :, 0:h], mid, cb[:, :, 0:h],
                                            ALU.subtract).then_inc(diffs, 1)
            pool.wait_ge(v_ready, 1)
            nc.gpsimd.tensor_tensor(R4[:, :], V4[:, :], HALF4[:, :], ALU.pow).then_inc(r_ready, 1)

        @block.tensor
        def _(pe):
            mm = nc.tensor.matmul

            def weights(n, width=CW):
                hi = WH[slot(n)][:, :].rearrange("p (k c) -> p k c", c=width)
                lo = WL[slot(n)][:, :].rearrange("p (k c) -> p k c", c=width)
                return hi, lo

            def three(ps, whi, wlo, ahi, alo, start, stop):
                mm(ps, whi, ahi, start=start, stop=False)
                mm(ps, whi, alo, start=False, stop=False)
                return mm(ps, wlo, ahi, start=False, stop=stop)

            def unit(n, value, banks, ahi, alo, kb0=0, nk=DB, first=True, last=True, wait_h=None,
                     width=CW, before=None):
                pe.wait_ge(unit_lo, value)
                whi, wlo = weights(n, width)
                for k in range(nk):
                    if before is not None:
                        before(k)
                    if wait_h is not None:
                        pe.wait_ge(h_lo, wait_h + k + 1)
                    for m in range(max(width // P, 1)):
                        w = slice(m * P, min((m + 1) * P, width))
                        rows = w.stop - w.start
                        ins = three(PS[0:rows, banks[m], :], whi[:, k, w], wlo[:, k, w], ahi[:, kb0 + k, :],
                                    alo[:, kb0 + k, :], first and k == 0, last and k == nk - 1)
                ins.then_inc(unit_done, 1)

            def unit_x(n, value, banks, ahi, alo, kb0=0, nk=DB, first=True):
                pe.wait_ge(unit_lo, value)
                whi, wlo = weights(n)
                for m in range(2):
                    for k in range(nk):
                        w = slice(m * P, (m + 1) * P)
                        ins = three(PS[:, banks[m], :], whi[:, k, w], wlo[:, k, w], ahi[:, kb0 + k, :],
                                    alo[:, kb0 + k, :], first and k == 0, k == nk - 1)
                    ins.then_inc(unit_half if m == 0 else unit_done, 1)

            def unit_v(n, banks, before):
                pe.wait_ge(unit_lo, n + 1)
                whi, wlo = weights(n)
                for t in range(TT):
                    ps = PS[:, banks[t // 2], (t % 2) * CW:(t % 2 + 1) * CW]
                    tok = slice(t * P, (t + 1) * P)
                    for k in range(DB):
                        if k % 4 == 0:
                            before(2 * t + k // 4)
                        mm(ps, HH[:, k, tok], whi[:, k, :], start=k == 0, stop=False)
                        mm(ps, HL[:, k, tok], whi[:, k, :], start=False, stop=False)
                        ins = mm(ps, HH[:, k, tok], wlo[:, k, :], start=False, stop=k == DB - 1)
                ins.then_inc(unit_done, 1)

            def sum_squares(g):
                pe.wait_ge(sacc, 9 * g + 9)
                mm(PS[:, 7, :], ONES[:, :], S[:, :], start=True, stop=True).then_inc(ssq_done, 1)

            pe.wait_ge(consts, 7)
            pe.wait_ge(small_in, 16 * 8)
            nc.tensor.transpose(PS[:, 5, 0:124], PST[:, :], IDENT[0:124, 0:124]).then_inc(small_t, 1)
            pe.wait_ge(x_in, 16 * TT)
            for b in range(DB):
                if b >= 4:
                    pe.wait_ge(xready, b - 3)
                for t in range(TT):
                    ins = nc.tensor.transpose(PS[:, b % 4, t * P:(t + 1) * P], XST[:, t, b * P:(b + 1) * P], IDENT[:, :])
                ins.then_inc(xt_done, 1)
            sum_squares(0)
            for piece in range(4):
                pe.wait_ge(ada_acc, 2 * DB * (piece // 2 + 1) - 1 + piece % 2)
                for m in range(4):
                    ins = mm(PS[:, 6, 4 * piece + m:4 * piece + m + 1], ACC0[:, piece, m * P:(m + 1) * P],
                             ONES[:, 0:1], start=True, stop=True)
                ins.then_inc(ada_red, 1)

            def ada_reduce(acc, mod):
                pe.wait_ge(ada_acc, acc)
                pe.wait_ge(mod_ready, mod)
                for m in range(4):
                    ins = mm(PS[:, 6, m:m + 1], ACC[:, m * P:(m + 1) * P], ONES[:, 0:1], start=True, stop=True)
                ins.then_inc(ada_red, 1)

            def ada_reduce_at(at, acc, mod):
                def go(k):
                    if k == at:
                        ada_reduce(acc, mod)
                return go

            def swiglu_in(base_n, which, with_ada):
                with pe.Fori(0, NP) as i:
                    for half in range(2):
                        n = base_n + half
                        if half == 0:
                            pe.wait_ge(silu_done, 1 + NP * which + i)
                        else:
                            pe.wait_ge(umul_done, 1 + NP * which + i)
                        unit(n, 2 * i + n + 1, (2 * half, 2 * half + 1), HH, HL, wait_h=2 * DB * which if half == 0 else None,
                             before=ada_reduce_at(5, 5 * DB + DB * i, 4 + i) if with_ada and half == 1 else None)

            def down_pair(n0, q, value0, x_value, which, after_first=None):
                banks = (2 * q, 2 * q + 1)
                pe.wait_ge(xready, x_value)
                for piece, (kb0, nk) in enumerate(((0, 8), (8, 8), (16, FB - 16))):
                    if piece == 2:
                        pe.wait_ge(u_lo, 1 + NP * (which + 1))
                        pe.wait_ge(u_hi, NP * (which + 1))
                    if piece == 2 and q == 1:
                        unit_x(n0 + piece, value0 + piece, banks, UH, UL, kb0, nk, first=False)
                    else:
                        unit(n0 + piece, value0 + piece, banks, UH, UL, kb0, nk, first=piece == 0, last=piece == 2)
                    if piece == 0 and after_first is not None:
                        after_first()

            swiglu_in(N_F1IN, 0, True)
            pe.wait_ge(u_lo, NP)
            pe.wait_ge(u_hi, NP - 1)
            pe.wait_ge(silu_done, 1 + NP)
            with pe.Fori(0, 2) as i:
                for q in range(2):
                    n = N_F1DOWN + 3 * q
                    down_pair(n, q, 6 * i + n + 1, 8 + 4 * i + 2 * q - 2, 0,
                              (lambda: ada_reduce(DB * (NP + 5) + DB * i, NP + 4 + i)) if q == 0 else None)
            sum_squares(1)
            ada_reduce(DB * (NP + 7), NP + 6)

            def score_levels(a, g):
                p, r = prep_of(a), rows_of(a)
                bank = 4 + g % 2
                pe.wait_ge(prep, 18 * p + 6 + 4 * (g + 1))
                if g == 0 and a:
                    pe.wait_ge(evac_a, 2 * a)
                if g == 1 and a:
                    pe.wait_ge(evac_v, a)
                if g == 2:
                    pe.wait_ge(near_done, 6 * a + 2)
                for j in range(2):
                    l = 2 * g + j
                    for t in range(TT):
                        ins = mm(PS[:, bank, 256 * j + 64 * t:256 * j + 64 * t + 64],
                                 KP[r, l, t * P:(t + 1) * P], QP[r, l, 64 * t:64 * t + 64], start=True, stop=True)
                ins.then_inc(score_done, 1)

            def score_diagonal(a):
                p, r = prep_of(a), rows_of(a)
                q, k = PREPS[p]["q"], PREPS[p]["k"]
                pe.wait_ge(near_done, 6 * a + 4)
                for t in range(TT):
                    tok = slice(t * P, (t + 1) * P)
                    ins = mm(PS[:, 5, tok], k[r, tok], q[r, tok], start=True, stop=True)
                ins.then_inc(score_done, 1)

            def score_far(a):
                p, r = prep_of(a), rows_of(a)
                pe.wait_ge(prep, 18 * p + 6)
                if a:
                    pe.wait_ge(evac_a, 2 * a - 1)
                for t in range(TT):
                    mm(PS[0:64, 6, 64 * t:64 * t + 64], KL[r, t * P:t * P + 64], QU[r, t * P + 64:(t + 1) * P],
                       start=True, stop=True)
                for j in range(2):
                    ins = mm(PS[:, 6, 256 + P * j:256 + P * (j + 1)], W256[r, 2 * j * P:(2 * j + 1) * P],
                             W256[r, (2 * j + 1) * P:(2 * j + 2) * P], start=True, stop=True)
                ins.then_inc(score_done, 1)
                pe.wait_ge(near_done, 6 * a + 6)
                for j in range(2):
                    ins = mm(PS[:, 4, 256 * j:256 * (j + 1)], W512[r, j * P:(j + 1) * P], W512[r, 256:512],
                             start=True, stop=True)
                ins.then_inc(score_done, 1)

            def head_out(a):
                pe.wait_ge(mix_evac, V_NEEDS[a])
                pe.wait_ge(evac_v, a + 1)
                pe.wait_ge(evac_a, 2 * a + 2)
                if a:
                    pe.wait_ge(rs_ln, a)
                vv, hv = (VHG, a) if a < HEADS else (VGL, a - HEADS)
                for s in range(TT):
                    ins = mm(PS[:, 7, s * P:T], vv[:, s, hv * P:(hv + 1) * P], SC[:, s * T + s * P:(s + 1) * T],
                             start=s == 0, stop=s == TT - 1)
                ins.then_inc(pv_done, 1)

            def head_norm(a):
                pe.wait_ge(sq_o, a + 1)
                pe.wait_ge(og_done, a + 1)
                mm(PS[:, 7, :], ONES[:, :], norm_in(a)[0], start=True, stop=True).then_inc(n_done, 1)

            def gk_up():
                pe.wait_ge(gkw_in, 16)
                pe.wait_ge(mix_evac, mix_at["low", 0] + 1)
                pe.wait_ge(evac_a, 2 * HEADS - 3)
                pe.wait_ge(rs_ln, HEADS - 1)
                for g in range(2):
                    ins = mm(PS[:, 6 + g, :], GKW[:, g * P:(g + 1) * P], S[0:RANK, :], start=True, stop=True)
                ins.then_inc(gk_mm, 1)

            def stages_at(step):
                if step == STAGES_AT[0][0]:
                    pe.wait_ge(sc_clear, 2)
                if step == STAGES_AT[HEADS - 1][3]:
                    pe.wait_ge(gk_sub, 3)
                    pe.wait_ge(gk_abs, 2)
                if step == GK_AT:
                    gk_up()
                for a, (near0, near1, near2, far, o, norm) in enumerate(STAGES_AT):
                    if step == near0:
                        score_levels(a, 0)
                    if step == near1:
                        score_levels(a, 1)
                    if step == near2:
                        score_levels(a, 2)
                        score_diagonal(a)
                    if step == far:
                        score_far(a)
                    if step == o:
                        head_out(a)
                    if step == norm:
                        head_norm(a)

            for j in range(len(MIX)):
                n = N_MIX + j
                kind = MIX[j][0]
                if j >= 2:
                    pe.wait_ge(mix_evac, j - 1)
                if kind in ("vh", "vg"):
                    unit_v(n, mix_banks(j), lambda k: stages_at(8 * j + k))
                else:
                    unit(n, n + 1, mix_banks(j), HH, HL, wait_h=DB if j == 0 else None,
                         width=RANK if kind == "low" else CW, before=lambda k: stages_at(8 * j + k))

            for pair in range(DB // 2):
                n = N_END + 3 * pair
                for b in range(2):
                    if pair == 0:
                        pe.wait_ge(mix_evac, len(MIX) - 1 + b)
                        unit(n + b, n + b + 1, (2 * b, 2 * b + 1), HH, HL,
                             before=lambda k: stages_at(8 * (len(MIX) + b) + k))
                    else:
                        pe.wait_ge(sig_done, 1 + 2 * pair)
                        unit(n + b, n + b + 1, (2 * b, 2 * b + 1), HH, HL)
                pe.wait_ge(y_lo, 2 * HEADS)
                pe.wait_ge(y_hi, 2 * HEADS)
                pe.wait_ge(merge, 1 + 3 * pair)
                pe.wait_ge(unit_lo, n + 3)
                whi, wlo = weights(n + 2)
                for br in range(2):
                    for k in range(HEADS):
                        for m in range(2):
                            w = slice(m * P, (m + 1) * P)
                            ins = three(PS[:, 4 + 2 * br + m, :], whi[:, HEADS * br + k, w], wlo[:, HEADS * br + k, w],
                                        YH[br][:, k, :], YL[br][:, k, :], k == 0, k == HEADS - 1)
                ins.then_inc(unit_done, 1)

            def merged(k):
                if k % 2 == 0:
                    pe.wait_ge(m_lo, 2 + k // 2)
                    pe.wait_ge(m_hi, 1 + k // 2)

            pe.wait_ge(sig_done, 9)
            with pe.Fori(0, 2) as i:
                for q in range(2):
                    n = N_OUT + q
                    pe.wait_ge(xready, 16 + 4 * i + 2 * q - 2)
                    if q == 0:
                        unit(n, 2 * i + n + 1, (0, 1), MH, ML, before=merged)
                    else:
                        unit_x(n, 2 * i + n + 1, (2, 3), MH, ML)
            sum_squares(2)

            swiglu_in(N_F2IN, 1, False)
            pe.wait_ge(u_lo, 2 * NP)
            pe.wait_ge(u_hi, 2 * NP - 1)
            pe.wait_ge(silu_done, 1 + 2 * NP)

            def untranspose(b0):
                def go():
                    for b in (b0, b0 + 1):
                        pe.wait_ge(fin_y, b + 1)
                        if b >= 2:
                            pe.wait_ge(fin_ev, b - 1)
                        for t in range(TT):
                            ins = nc.tensor.transpose(PS[:, 4 + b % 2, t * P:(t + 1) * P],
                                                      YF[b % 2][:, t * P:(t + 1) * P], IDENT[:, :])
                        ins.then_inc(fin_t, 1)
                return go

            for i in range(2):
                for q in range(2):
                    n = N_F2DOWN + 3 * q
                    pair = 2 * i + q
                    down_pair(n, q, 6 * i + n + 1, 24 + 2 * pair - 2, 1, untranspose(2 * pair - 2) if pair else None)
            untranspose(6)()
            pe.wait_ge(sacc, 36)
            for t in range(TT):
                ins = mm(PS[:, 7, t:t + 1], S[:, t * P:(t + 1) * P], ONES[:, 0:1], start=True, stop=True)
            ins.then_inc(ssq_done, 1)

        @block.scalar
        def _(act):
            A = nc.scalar.activation
            chain = [0]

            def self_wait(ins):
                chain[0] += 1
                ins.then_inc(act_self, 1)
                act.wait_ge(act_self, chain[0])

            for dst, src in small[:len(small) // 2]:
                act.dma_start(dst, src).then_inc(small_in, 16)
            act.dma_start(GKW[:, :], w_gk_up[0]).then_inc(gkw_in, 16)

            def split_hi(n, raw_val, done_val=None, size=UNIT):
                act.wait_ge(raw_in[slot(n)], raw_val)
                if done_val is not None:
                    act.wait_ge(unit_done, done_val)
                A(WH[slot(n)][:, 0:size], RAW[slot(n)][:, 0:size], ACT.Copy).then_inc(unit_hi, 1)

            def down_size(piece):
                return (UNIT, UNIT, (FB - 16) * CW)[piece]

            def square(b, x_val, sq_free, ap=None):
                act.wait_ge(xready, x_val)
                act.wait_ge(sacc, sq_free)
                A(SG[:, b % 2, :], ap, ACT.Square).then_inc(sq_ready, 1)

            def rms(g):
                act.wait_ge(ssq_done, g + 1)
                A(RMS[:, :], PS[:, 7, :], ACT.Ln, bias=EPST[:, 0:1], scale=1.0 / D).then_inc(x_ln, 1)
                act.wait_ge(x_ln, g + 1)
                A(RMS[:, :], RMS[:, :], ACT.Exp, scale=-0.5).then_inc(x_rms, 1)

            def norm_blocks(g):
                act.wait_ge(av_ready, g + 1)
                for b in range(DB):
                    act.wait_ge(t_ready, DB * g + b + 1)
                    if b >= 2:
                        act.wait_ge(h_lo, DB * g + b - 1)
                    a, sh = AV[:, g, b:b + 1], MOD[:, 3 * DB * g + b:3 * DB * g + b + 1]
                    if b:
                        A(HFULL[:, b % 2, :], TN[:, b % 2, :], ACT.Identity, bias=sh, scale=a)
                    A(HH[:, b, :], TN[:, b % 2, :], ACT.Identity, bias=sh, scale=a).then_inc(h_hi, 1)

            tables = [""]

            def exp_ln_tables():
                if tables[0] != "exp_ln":
                    nc.scalar.preload_act_table_set("natural_log_exp_and_others")
                tables[0] = "exp_ln"

            def silu_tables():
                nc.scalar.preload_act_table_set("silu_and_others")
                tables[0] = "silu"

            act.wait_ge(small_ready, 1)
            A(COND[:, :], PT[:, PC_C:PC_C + DB], ACT.Silu).then_inc(cond_ready, 1)
            act.wait_ge(lb_ready, 1)
            A(LB[:, :], LBD[:, :], ACT.Sigmoid).then_inc(cond_ready, 1)
            A(OML[:, :], LBD[:, :], ACT.Sigmoid, scale=-1.0).then_inc(cond_ready, 1)
            exp_ln_tables()
            for b in range(DB):
                act.wait_ge(xt_done, b + 1)
                A(X[:, b, :], PS[:, b % 4, :], ACT.Copy).then_inc(xready, 1)
                square(b, b + 1, max(b, 1), X[:, b, :])
            rms(0)
            split_hi(0, 16)
            split_hi(1, 16)
            norm_blocks(0)
            silu_tables()

            def swiglu_in(base_n, which):
                with act.Fori(0, NP) as i:
                    n = base_n
                    act.wait_ge(unit_done, 2 * i + n + 1)
                    act.wait_ge(u_lo, 1 + NP * which + i)
                    A(SG[:, :, :], PS[:, 0:2, :], ACT.Silu).then_inc(silu_done, 1)
                    split_hi(n + 2, 16 * i + raw_value(n + 2), 2 * i + n + 1)
                    split_hi(n + 3, 16 * i + raw_value(n + 3), 2 * i + n + 2)
                    act.wait_ge(umul_done, 1 + NP * which + i + 1)
                    A(UH[:, ds(2 * i, 2), :], SG[:, :, :], ACT.Copy).then_inc(u_hi, 1)

            swiglu_in(N_F1IN, 0)

            def down(base_n, i, x0, sacc0, last=False, final=False):
                for q in range(2):
                    for piece in range(3):
                        n = base_n + 3 * q + piece
                        if piece < 2 and not (last and q == 1 and piece == 1):
                            split_hi(n + 2, 16 * 3 * i + raw_value(n + 2), 6 * i + n + 1,
                                     UNIT if q == 1 and piece == 1 else down_size((piece + 2) % 3))
                    for m in range(2):
                        b = 2 * q + m
                        if isinstance(i, int):
                            blk = X[:, 4 * i + b, :]
                        else:
                            blk = X[:, ds(4 * i + b, 1), :].rearrange("p a t -> p (a t)")
                        square(b, x0 + 4 * i + b + 1, sacc0 + 4 * i + b, blk)
                        if final:
                            g = 4 * i + b
                            if g >= 2:
                                act.wait_ge(fin_t, g - 1)
                            A(YF[g % 2][:, :], blk, ACT.Copy, scale=PT[:, PC_FINAL + g:PC_FINAL + g + 1]).then_inc(fin_y, 1)
                            if g >= 2:
                                final_copy(g - 2)
                    if not (last and q == 1):
                        split_hi(n + 2, 16 * 3 * i + raw_value(n + 2), 6 * i + n + 1)

            def final_copy(b):
                act.wait_ge(fin_t, b + 1)
                A(OUTT[:, :, b * P:(b + 1) * P], PS[:, 4 + b % 2, :].rearrange("p (t f) -> p t f", f=P), ACT.Copy)\
                    .then_inc(fin_ev, 1)

            exp_ln_tables()
            with act.Fori(0, 2) as i:
                down(N_F1DOWN, i, 8, 9)
            rms(1)
            norm_blocks(1)

            def evacuate(j):
                if MIX[j][0] in ("hf", "hq", "gh", "gg"):
                    tables[0] = "sigmoid or silu"
                n = N_MIX + j
                kind, _, half = MIX[j]
                act.wait_ge(unit_done, n + 1)
                ps = PS[:, mix_banks(j)[0]:mix_banks(j)[0] + 2, :]
                two = slice(2 * half, 2 * half + 2)
                toks = ps.rearrange("p b (t c) -> p (b t) c", c=CW)
                if kind == "hf":
                    A(CHG[:, two, :], ps, ACT.Sigmoid)
                    A(KHG[:, two, :], ps, ACT.Sigmoid, scale=-1.0).then_inc(mix_evac, 1)
                elif kind == "hq":
                    A(QHG[:, two, :], ps, ACT.Silu).then_inc(mix_evac, 1)
                elif kind == "vh":
                    A(VHG[:, :, half * CW:(half + 1) * CW], toks, ACT.Copy).then_inc(mix_evac, 1)
                elif kind == "vg":
                    A(VGL[:, :, half * CW:(half + 1) * CW], toks, ACT.Copy).then_inc(mix_evac, 1)
                elif kind == "gh":
                    A(GO[:, two, :], ps, ACT.Silu).then_inc(mix_evac, 1)
                elif kind == "gg":
                    A(GO[:, HEADS + 2 * half:HEADS + 2 * half + 2, :], ps, ACT.Silu).then_inc(mix_evac, 1)
                elif kind == "low":
                    A(S[0:RANK, :], PS[0:RANK, mix_banks(j)[0], :], ACT.Copy).then_inc(mix_evac, 1)
                elif kind == "gk":
                    A(KGL[:, :, :], ps, ACT.Copy).then_inc(mix_evac, 1)
                elif kind == "gq":
                    A(QGL[:, :, :], ps, ACT.Copy, scale=64.0 ** -0.5).then_inc(mix_evac, 1)

            def unit_size(n):
                return DB * RANK if n == N_MIX + mix_at["low", 0] else UNIT

            def decays(p):
                exp_ln_tables()
                cc = PREPS[p]["c"]
                if p < HEADS:
                    act.wait_ge(mix_evac, PREP_NEEDS[p])
                    A(cc, cc, ACT.Ln, bias=LB[:, p:p + 1], scale=OML[:, p:p + 1]).then_inc(logf, 1)
                act.wait_ge(cum, p + 1)
                if p:
                    act.wait_ge(score_done, 6 * before_prep(p) + 6)
                A(QU[:, :], cc, ACT.Exp).then_inc(exps, 1)
                act.wait_ge(kl_diff, p + 1)
                A(KL[:, :], KL[:, :], ACT.Exp).then_inc(exps, 1)
                act.wait_ge(gtab, p + 1)
                A(FT[:, :, :], GT[:, :, :], ACT.Exp).then_inc(exps, 1)

            def near_factors(p):
                exp_ln_tables()
                act.wait_ge(diffs, 12 * p + 6)
                A(QP[:, :, :], QP[:, :, :], ACT.Exp).then_inc(exps, 1)
                for l, B in enumerate(LEVELS):
                    act.wait_ge(diffs, 12 * p + 7 + l)
                    kk = blocks(KP[:, l, :], B)[:, :, 0:B // 2]
                    A(kk, kk, ACT.Exp).then_inc(exps, 1)

            def copy_far(a):
                act.wait_ge(score_done, 6 * a + 5)
                act.wait_ge(evac_v, a + 1)
                diag = SC[:, :].rearrange("p (i x) -> p i x", x=5 * P)
                A(diag[0:64, :, 64:P], PS[0:64, 6, 0:256].rearrange("p (i x) -> p i x", x=64), ACT.Copy)
                A(SC[:, :].rearrange("p (i x) -> p i x", x=2 * T + 2 * P)[:, :, P:2 * P],
                  PS[:, 6, 256:512].rearrange("p (i x) -> p i x", x=P), ACT.Copy).then_inc(evac_a, 1)
                act.wait_ge(score_done, 6 * a + 6)
                A(SC[:, 0:2 * T].rearrange("p (i x) -> p i x", x=T)[:, :, T // 2:T],
                  PS[:, 4, :].rearrange("p (i x) -> p i x", x=T // 2), ACT.Copy).then_inc(evac_a, 1)

            def squares(a):
                act.wait_ge(pv_done, a + 1)
                A(norm_in(a)[0], PS[:, 7, :], ACT.Square).then_inc(sq_o, 1)

            def inverse_rms(a):
                exp_ln_tables()
                act.wait_ge(n_done, a + 1)
                rs = norm_in(a)[1]
                A(rs, PS[:, 7, :], ACT.Ln, bias=EPST[:, 0:1], scale=1.0 / P).then_inc(rs_ln, 1)
                act.wait_ge(rs_ln, a + 1)
                A(rs, rs, ACT.Exp, scale=-0.5).then_inc(rs_ready, 1)

            def output_hi(a):
                act.wait_ge(yf_ready, a + 1)
                A(YH[a // HEADS][:, a % HEADS, :], GO[:, a, :], ACT.Copy).then_inc(y_hi, 1)

            def decay_gla(g):
                exp_ln_tables()
                act.wait_ge(gk_mm, 1)
                if g:
                    act.wait_ge(gk_sub, 2)
                A(S[:, :], PS[:, 6 + g, :], ACT.Abs, bias=PT[:, PC_BGK + g:PC_BGK + g + 1]).then_inc(gk_abs, 1)
                act.wait_ge(gk_abs, g + 1)
                self_wait(A(S[:, :], S[:, :], ACT.Exp, scale=-1.0))
                A(S[:, :], S[:, :], ACT.Ln, bias=ONES[:, 0:1]).then_inc(gk_ln, 1)

            for step in ORDER:
                kind, j = step[0], int(step[1:])
                if kind == "E":
                    n = N_MIX + j
                    split_hi(n + 2, raw_value(n + 2), n + 1, unit_size(n + 2))
                    evacuate(j)
                elif kind == "a":
                    decays(j)
                elif kind == "b":
                    near_factors(j)
                elif kind == "A":
                    copy_far(j)
                elif kind == "Q":
                    squares(j)
                elif kind == "T":
                    inverse_rms(j)
                elif kind == "U":
                    output_hi(j)
                elif kind == "G":
                    decay_gla(j)
                elif kind == "S":
                    split_hi(N_END + 2, raw_value(N_END + 2), N_END + 1)

            for pair in range(DB // 2):
                for b in range(2):
                    n = N_END + 3 * pair + b
                    if n > N_END:
                        split_hi(n + 2, raw_value(n + 2), n + 1)
                    act.wait_ge(m_lo, 1 + pair)
                    A(RG[b][:, :, :], PS[:, 2 * b:2 * b + 2, :], ACT.Sigmoid).then_inc(sig_done, 1)
                n = N_END + 3 * pair + 2
                split_hi(n + 2, raw_value(n + 2), n + 1)
                act.wait_ge(merge, 1 + 3 * pair + 3)
                A(MH[:, 2 * pair:2 * pair + 2, :], RG[0][:, :, :], ACT.Copy).then_inc(m_hi, 1)

            tables[0] = "sigmoid"
            exp_ln_tables()
            with act.Fori(0, 2) as i:
                for q in range(2):
                    n = N_OUT + q
                    for m in range(2):
                        b = 2 * q + m
                        square(b, 16 + 4 * i + b + 1, 18 + 4 * i + b, X[:, ds(4 * i + b, 1), :].rearrange("p a t -> p (a t)"))
                    split_hi(n + 2, 16 * i + raw_value(n + 2), 2 * i + n + 1)
            rms(2)
            norm_blocks(2)
            silu_tables()
            swiglu_in(N_F2IN, 1)
            for i in range(2):
                down(N_F2DOWN, i, 24, 27, last=i == 1, final=True)
            final_copy(6)
            final_copy(7)
            act.wait_ge(r_ready, 1)
            act.wait_ge(fin_ev, DB)
            for t in (2, 3):
                A(OUTT[:, t, :], OUTT[:, t, :], ACT.Copy, scale=R4[:, t:t + 1]).then_inc(fin_a, 1)

        @block.vector
        def _(dve):
            V = nc.vector
            chain = [0]

            def self_wait(ins):
                chain[0] += 1
                ins.then_inc(dve_self, 1)
                dve.wait_ge(dve_self, chain[0])

            def split_lo(n, value, done_val=None, size=UNIT):
                if done_val is not None:
                    dve.wait_ge(unit_done, done_val)
                dve.wait_ge(unit_hi, value)
                s = slot(n)
                V.tensor_tensor(WL[s][:, 0:size], RAW[s][:, 0:size], WH[s][:, 0:size].bitcast(F32), ALU.subtract)\
                    .then_inc(unit_lo, 1)

            def add_square(b, sq_val, acc_val):
                dve.wait_ge(sq_ready, sq_val)
                dve.wait_ge(sacc, acc_val)
                V.tensor_tensor(S[:, :], S[:, :], SG[:, b % 2, :], ALU.add).then_inc(sacc, 1)

            def clear_s():
                V.memset(S[:, :], 0.0).then_inc(sacc, 1)

            def normalise(g, vectors=None, between=None):
                dve.wait_ge(x_rms, g + 1)

                def lo(b):
                    if b == 0:
                        dve.wait_ge(av_ready, g + 1)
                        dve.wait_ge(t_ready, DB * g + 1)
                        self_wait(V.tensor_scalar(HFULL[:, 0, :], TN[:, 0, :], AV[:, g, 0:1],
                                                  MOD[:, 3 * DB * g:3 * DB * g + 1], ALU.mult, ALU.add))
                    dve.wait_ge(h_hi, DB * g + b + 1)
                    V.tensor_tensor(HL[:, b, :], HFULL[:, b % 2, :], HH[:, b, :].bitcast(F32), ALU.subtract).then_inc(h_lo, 1)

                for b in range(DB):
                    if b >= 2:
                        dve.wait_ge(h_hi, DB * g + b - 1)
                    V.tensor_tensor(TN[:, b % 2, :], X[:, b, :], RMS[:, :], ALU.mult).then_inc(t_ready, 1)
                    if b == 1 and vectors is not None:
                        vectors()
                    if b:
                        lo(b - 1)
                    if b == 4 and between is not None:
                        between()
                lo(DB - 1)

            def scale_vector(g):
                V.scalar_tensor_tensor(AV[:, g, :], MOD[:, 3 * DB * g + DB:3 * DB * g + 2 * DB], 1.0,
                                       PT[:, PC_GAIN + DB * g:PC_GAIN + DB * (g + 1)], ALU.add, ALU.mult).then_inc(av_ready, 1)

            dve.wait_ge(small_t, 1)
            V.tensor_copy(PT[:, :], PS[:, 5, 0:124]).then_inc(small_ready, 1)
            dve.wait_ge(small_ready, 1)
            V.tensor_tensor(LBD[:, :], PT[:, PC_LB:PC_LB + HEADS], PT[:, PC_LB + HEADS:PC_LB + 2 * HEADS],
                            ALU.subtract).then_inc(lb_ready, 1)
            dve.wait_ge(cond_ready, 3)
            V.tensor_scalar(LB[:, :], LB[:, :], LN_FLOOR, None, ALU.max).then_inc(lb_ready, 1)

            def ada_term(k, acc_tile, w, acc_val):
                if k == 0:
                    V.tensor_scalar(acc_tile, w, COND[:, 0:1], None, ALU.mult).then_inc(ada_acc, 1)
                else:
                    dve.wait_ge(ada_acc, acc_val)
                    V.scalar_tensor_tensor(acc_tile, w, COND[:, k:k + 1], acc_tile, ALU.mult, ALU.add).then_inc(ada_acc, 1)

            for pair in range(2):
                for k in range(DB):
                    if k % 2 == 0:
                        dve.wait_ge(ada0_in[4 * pair + k // 2], 16)
                    for piece in range(2):
                        ada_term(k, ACC0[:, 2 * pair + piece, :], ADA0[:, pair, k, AW * piece:AW * (piece + 1)],
                                 2 * DB * pair + 2 * k - 1 + piece)

            def vectors0():
                dve.wait_ge(ada_red, 4)
                V.tensor_tensor(MOD[:, 0:2 * DB], PS[:, 6, 0:2 * DB], PT[:, PC_BADA:PC_BADA + 2 * DB], ALU.add)\
                    .then_inc(mod_ready, 4)
                dve.wait_ge(mod_ready, 4)
                scale_vector(0)
                split_lo(0, 1)

            normalise(0, vectors0, between=lambda: split_lo(1, 2))

            def ada_piece(red_val, in_val, acc0):
                dve.wait_ge(ada_red, red_val)
                for k in range(DB):
                    j = k // 2
                    if k % 2 == 0:
                        dve.wait_ge(ada_in[j % 2], in_val + 16 * (j // 2 + 1))
                    ada_term(k, ACC[:, :], ADAW[j % 2][:, k % 2, :], acc0 + k)

            def add_ada_bias(i, piece):
                dve.wait_ge(ada_red, i + piece + 1)
                V.tensor_tensor(MOD[:, ds(4 * i + 4 * piece, 4)], PS[:, 6, 0:4], PT[:, ds(4 * i + PC_BADA + 4 * piece, 4)],
                                ALU.add).then_inc(mod_ready, 1)

            ada_piece(4, 0, 4 * DB)

            def swiglu_in(base_n, which, with_ada):
                with dve.Fori(0, NP) as i:
                    n = base_n
                    split_lo(n + 2, 2 * i + n + 3, 2 * i + n + 1)
                    if with_ada:
                        add_ada_bias(i, 4)
                        ada_piece(i + 5, 32 * i + 32, DB * i + 5 * DB)
                    dve.wait_ge(silu_done, 1 + NP * which + i + 1)
                    dve.wait_ge(unit_done, 2 * i + n + 2)
                    V.tensor_tensor(SG[:, :, :], SG[:, :, :], PS[:, 2:4, :], ALU.mult).then_inc(umul_done, 1)
                    split_lo(n + 3, 2 * i + n + 4, 2 * i + n + 2)
                    dve.wait_ge(u_hi, NP * which + i + 1)
                    V.tensor_tensor(UL[:, ds(2 * i, 2), :], SG[:, :, :], UH[:, ds(2 * i, 2), :].bitcast(F32),
                                    ALU.subtract).then_inc(u_lo, 1)

            swiglu_in(N_F1IN, 0, True)

            def add_to_x(i, b, bank, gate, x_val=None):
                if isinstance(i, int):
                    xb, gg = X[:, 4 * i + b, :], GATE[:, gate, 4 * i + b:4 * i + b + 1]
                else:
                    xb = X[:, ds(4 * i + b, 1), :].rearrange("p a t -> p (a t)")
                    gg = GATE[:, gate, ds(4 * i + b, 1)]
                V.scalar_tensor_tensor(xb, PS[:, bank, :], gg, xb, ALU.mult, ALU.add).then_inc(xready, 1)

            def down(base_n, i, gate, sq0, sacc0, half0, last=False, ada=False):
                for q in range(2):
                    for piece in range(3):
                        n = base_n + 3 * q + piece
                        if piece == 2:
                            for m in range(2):
                                b = 2 * q + m
                                if m == 0 and q == 1:
                                    dve.wait_ge(unit_half, half0 + i + 1)
                                else:
                                    dve.wait_ge(unit_done, 6 * i + n + 1)
                                add_to_x(i, b, b, gate)
                                add_square(b, sq0 + 4 * i + b + 1, sacc0 + 4 * i + b)
                        if not (last and q == 1 and piece >= 1):
                            nxt = (piece + 2) % 3
                            size = (FB - 16) * CW if nxt == 2 and not (q == 1 and piece > 0) else UNIT
                            split_lo(n + 2, 6 * i + n + 3, 6 * i + n + 1, size)
                        if ada and q == 1 and piece == 0:
                            add_ada_bias(i, NP + 4)
                            ada_piece(i + NP + 5, 32 * i + 32 * (NP + 1), DB * i + DB * (NP + 5))
            dve.wait_ge(mod_ready, 6)
            self_wait(V.tensor_scalar(GATE[:, 0, :], MOD[:, 2 * DB:3 * DB], 0.5, None, ALU.mult))
            clear_s()
            with dve.Fori(0, 2) as i:
                down(N_F1DOWN, i, 0, 8, 10, 0, ada=True)

            scale_vector(1)
            normalise(1)
            dve.wait_ge(ada_red, NP + 7)
            V.tensor_tensor(MOD[:, 8 * DB + 4:9 * DB], PS[:, 6, 0:4], PT[:, PC_BADA + 8 * DB + 4:PC_BADA + 9 * DB],
                            ALU.add).then_inc(mod_ready, 1)
            dve.wait_ge(mod_ready, NP + 7)
            V.tensor_copy(GATE[:, 1, :], MOD[:, 5 * DB:6 * DB])
            self_wait(V.tensor_scalar(GATE[:, 2, :], MOD[:, 8 * DB:9 * DB], 0.5, None, ALU.mult))

            def decays(p):
                k, cc = PREPS[p]["k"], PREPS[p]["c"]
                if p < HEADS:
                    dve.wait_ge(mix_evac, PREP_NEEDS[p])
                    V.tensor_scalar(k, k, OML[:, p:p + 1], None, ALU.mult)
                    dve.wait_ge(logf, p + 1)
                V.tensor_tensor_scan(cc, RST[:, :], cc, 0.0, ALU.mult, ALU.add).then_inc(cum, 1)
                dve.wait_ge(cum, p + 1)
                tot = blocks(cc, CHUNK)[:, :, CHUNK - 1:CHUNK]
                if p:
                    dve.wait_ge(score_done, 6 * before_prep(p) + 6)
                V.tensor_tensor(blocks(KL[:, :], CHUNK), tot.to_broadcast([P, NC, CHUNK]), blocks(cc, CHUNK),
                                ALU.subtract).then_inc(kl_diff, 1)
                t1 = cc.rearrange("p (n b) -> p n b", b=CHUNK)[:, :, CHUNK - 1]
                if p:
                    dve.wait_ge(exps, 10 * p - 7)
                V.tensor_copy(GT[:, 0, 0:5:4], t1[:, 1:6:4])
                V.tensor_copy(GT[:, 0, 3:8:4], t1[:, 2:7:4])
                V.tensor_copy(GT[:, 1, 2:6:3], t1[:, 3:5])
                self_wait(V.tensor_tensor(GT[:, 1, 1:7:5], t1[:, 2:6:3], t1[:, 3:5], ALU.add))
                V.tensor_tensor(GT[:, 1, 0:8:7], GT[:, 1, 1:7:5], t1[:, 1:7:5], ALU.add).then_inc(gtab, 1)

            def decayed(p):
                q, k = PREPS[p]["q"], PREPS[p]["k"]
                dve.wait_ge(mix_evac, PREP_NEEDS[p])
                dve.wait_ge(exps, 10 * p + 2)
                V.tensor_tensor(QU[:, :], QU[:, :], q, ALU.mult).then_inc(prep, 1)
                V.tensor_tensor(KL[:, :], KL[:, :], k, ALU.mult).then_inc(prep, 1)
                dve.wait_ge(exps, 10 * p + 3)
                dve.wait_ge(prep, 18 * p + 2)
                for src, c0 in ((KL, 0), (QU, 2)):
                    for j in range(2):
                        cs = slice(4 * j + c0, 4 * j + c0 + 2)
                        ins = V.tensor_tensor(blocks(W256[:, :], CHUNK)[:, cs, :], blocks(src[:, :], CHUNK)[:, cs, :],
                                              FT[:, 0, cs].unsqueeze(2).to_broadcast([P, 2, CHUNK]), ALU.mult)
                    ins.then_inc(prep, 1)
                for src, c0 in ((KL, 0), (QU, 4)):
                    cs = slice(c0, c0 + 4)
                    V.tensor_tensor(blocks(W512[:, :], CHUNK)[:, cs, :], blocks(src[:, :], CHUNK)[:, cs, :],
                                    FT[:, 1, cs].unsqueeze(2).to_broadcast([P, 4, CHUNK]), ALU.mult).then_inc(prep, 1)
                for l, B in enumerate(LEVELS):
                    h = B // 2
                    dve.wait_ge(exps, 10 * p + 4)
                    qp = QP[:, l, :].rearrange("p (n h) -> p n h", h=h)
                    V.tensor_tensor(qp, qp, blocks(q, B)[:, :, h:B], ALU.mult).then_inc(prep, 1)
                    dve.wait_ge(exps, 10 * p + 5 + l)
                    kp = blocks(KP[:, l, :], B)[:, :, 0:h]
                    V.tensor_tensor(kp, kp, blocks(k, B)[:, :, 0:h], ALU.mult).then_inc(prep, 1)

            diag = SC[:, :].rearrange("p (i x) -> p i x", x=5 * P)[:, :, 0:P]

            def copy_near(a):
                for g in range(3):
                    dve.wait_ge(score_done, 6 * a + g + 1)
                    for j in range(2):
                        l = 2 * g + j
                        h = LEVELS[l] // 2
                        near = diag.rearrange("p i (n b) -> p i n b", b=2 * h)[:, :, :, h:2 * h]
                        ps = PS[:, 4 + g % 2, 256 * j:256 * (j + 1)].rearrange("p (i n h) -> p i n h", i=TT, h=h)
                        m = MASK[:, l, :].rearrange("p (n h) -> p n h", h=h).unsqueeze(1).to_broadcast([P, TT, 64 // h, h])
                        if l:
                            dve.wait_ge(near_done, 6 * a + l)
                        ins = V.copy_predicated(near, m, ps).then_inc(near_done, 1)
                dve.wait_ge(score_done, 6 * a + 4)
                dve.wait_ge(near_done, 6 * a + 6)
                V.copy_predicated(diag, MASKD[:, :].unsqueeze(1).to_broadcast([P, TT, P]),
                                  PS[:, 5, :].rearrange("p (i x) -> p i x", x=P)).then_inc(evac_v, 1)

            def gate_out(a):
                dve.wait_ge(sq_o, a + 1)
                dve.wait_ge(mix_evac, G_NEEDS[a])
                V.tensor_tensor(GO[:, a, :], GO[:, a, :], PS[:, 7, :], ALU.mult).then_inc(og_done, 1)

            def finish(a):
                gain = PT[:, PC_HGN:PC_HGN + 1] if a < HEADS else PT[:, PC_GLN:PC_GLN + 1]
                dve.wait_ge(og_done, a + 1)
                dve.wait_ge(rs_ready, a + 1)
                V.scalar_tensor_tensor(GO[:, a, :], GO[:, a, :], gain, norm_in(a)[1], ALU.mult, ALU.mult).then_inc(yf_ready, 1)

            def output_lo(a):
                dve.wait_ge(y_hi, a + 1)
                V.tensor_tensor(YL[a // HEADS][:, a % HEADS, :], GO[:, a, :], YH[a // HEADS][:, a % HEADS, :].bitcast(F32),
                                ALU.subtract).then_inc(y_lo, 1)

            def decay_gla(g):
                cc = CGL[:, g, :]
                dve.wait_ge(gk_abs, g + 1)
                V.tensor_scalar(cc, PS[:, 6 + g, :], PT[:, PC_BGK + g:PC_BGK + g + 1], 0.0, ALU.add, ALU.min).then_inc(gk_sub, 1)
                dve.wait_ge(gk_sub, 2 * g + 1)
                dve.wait_ge(gk_ln, g + 1)
                V.tensor_tensor(cc, cc, S[:, :], ALU.subtract).then_inc(gk_sub, 1)
                dve.wait_ge(gk_sub, 2 * g + 2)
                self_wait(V.tensor_scalar(cc, cc, 1.0 / 16.0, None, ALU.mult))

            for step in ORDER:
                kind, j = step[0], int(step[1:])
                if kind == "E":
                    n = N_MIX + j
                    size = DB * RANK if n + 2 == N_MIX + mix_at["low", 0] else UNIT
                    split_lo(n + 2, n + 3, n + 1, size)
                elif kind == "a":
                    decays(j)
                elif kind == "b":
                    decayed(j)
                elif kind == "V":
                    if j == 0:
                        dve.wait_ge(consts, 9 + 4 * len(LEVELS))
                    copy_near(j)
                elif kind == "Q":
                    gate_out(j)
                elif kind == "T":
                    finish(j)
                elif kind == "U":
                    output_lo(j)
                elif kind == "G":
                    decay_gla(j)
                elif kind == "S":
                    split_lo(N_END + 2, N_END + 3, N_END + 1)

            for pair in range(DB // 2):
                for b in range(3):
                    n = N_END + 3 * pair + b
                    if b == 2:
                        dve.wait_ge(unit_done, n + 1)
                        dve.wait_ge(sig_done, 1 + 2 * pair + 2)
                        for br in range(2):
                            V.tensor_tensor(RG[br][:, :, :], RG[br][:, :, :], PS[:, 4 + 2 * br:6 + 2 * br, :],
                                            ALU.mult).then_inc(merge, 1)
                        dve.wait_ge(merge, 1 + 3 * pair + 2)
                        V.tensor_tensor(RG[0][:, :, :], RG[0][:, :, :], RG[1][:, :, :], ALU.add).then_inc(merge, 1)
                    if n > N_END:
                        split_lo(n + 2, n + 3, n + 1)
                dve.wait_ge(m_hi, pair + 1)
                V.tensor_tensor(ML[:, 2 * pair:2 * pair + 2, :], RG[0][:, :, :],
                                MH[:, 2 * pair:2 * pair + 2, :].bitcast(F32), ALU.subtract).then_inc(m_lo, 1)

            clear_s()
            with dve.Fori(0, 2) as i:
                for q in range(2):
                    n = N_OUT + q
                    for m in range(2):
                        b = 2 * q + m
                        if m == 0 and q == 1:
                            dve.wait_ge(unit_half, i + 3)
                        else:
                            dve.wait_ge(unit_done, 2 * i + n + 1)
                        add_to_x(i, b, b, 1)
                        add_square(b, 16 + 4 * i + b + 1, 19 + 4 * i + b)
                    split_lo(n + 2, 2 * i + n + 3, 2 * i + n + 1)
            scale_vector(2)
            normalise(2)
            swiglu_in(N_F2IN, 1, False)
            clear_s()
            for i in range(2):
                down(N_F2DOWN, i, 2, 24, 28, 4, last=i == 1)
            dve.wait_ge(ssq_done, 4)
            V.tensor_scalar(V4[:, :], PS[:, 7, 0:TT], 1.0 / D, EPS, ALU.mult, ALU.add).then_inc(v_ready, 1)
            dve.wait_ge(r_ready, 1)
            dve.wait_ge(fin_ev, DB)
            for t in (0, 1):
                V.tensor_scalar(OUTT[:, t, :], OUTT[:, t, :], R4[:, t:t + 1], None, ALU.mult).then_inc(fin_v, 1)


def arena_offset(nc, arena):
    size = arena.shape[1] * 4
    return (nc.sbuf_base - size) // 32 * 32


_INS = ["x", "c", "w_ada", "b_ada", "norm_gains", "ffn1_w_in", "ffn1_w_down", "w_in_mix", "w_gk_up", "b_gk_up",
        "lb_logits", "hg_norm", "gla_norm", "w_up_hg", "w_up_gla", "w_out", "ffn2_w_in", "ffn2_w_down", "final_norm"]


def kernel(**inputs):
    import numpy as _np
    import concourse.bacc as _bacc
    from concourse import mybir as _mybir
    from concourse.bass_utils import run_bass_kernel_spmd as _run

    nc = _bacc.Bacc("TRN2", target_bir_lowering=False, num_devices=1)
    arrays, args = {}, []
    for name in _INS:
        a = _np.ascontiguousarray(inputs[name])
        arrays[f"in_{name}_dram"] = a
        args.append(nc.dram_tensor(f"in_{name}_dram", a.shape, _mybir.dt.from_np(a.dtype), kind="ExternalInput").ap())
    args.append(nc.dram_tensor("out_0_dram", inputs["x"].shape, _mybir.dt.float32, kind="ExternalOutput").ap())
    trunk_program(nc, *args)
    r = _run(nc, [arrays], core_ids=[0])
    return r.results[0]["out_0_dram"]
```
